# Optimizing a Trainium2 kernel written in Bass

```python
import math
import jax, jax.numpy as jnp
from jax import lax
import numpy as np

D_MODEL = 1024
BATCH = 1
SEQ = 1024
DEPTH = 2
DEC_BATCH = 8
DEC_SEQ = 8
PAST_LEN = 512
PAGE_SIZE = 128

N_A_LAYERS = DEPTH // 2
N_B_LAYERS = DEPTH - N_A_LAYERS
D_RNN = (D_MODEL * 5) // 4
RG_BLOCKS = 16
RG_BLOCK_W = D_RNN // RG_BLOCKS
RG_CONV_W = 4
RG_C = 8.0
N_HEADS = 16
HEAD_DIM = 64
Q_BLOCK = 128
D_FF = 3 * D_MODEL
FFN_CONV_W = 3
EPS = 1e-6

kernel_name = 'yoco_rglru_fox_convffn_step'

def _rmsnorm(x, g):
    x32 = x.astype(jnp.float32)
    n = x32 * lax.rsqrt(jnp.mean(x32 * x32, axis=-1, keepdims=True) + EPS)
    return n * g.astype(jnp.float32)

def _modnorm(x, g, shift, scale):
    n = _rmsnorm(x, g) * (1.0 + scale.astype(jnp.float32)[:, None, :]) + shift.astype(jnp.float32)[:, None, :]
    return n.astype(x.dtype)

def _causal_dwconv(x, buf, w, b):
    width = w.shape[0]
    t = x.shape[1]
    xp = jnp.concatenate([buf.astype(x.dtype), x], axis=1)
    y = xp[:, 0:t] * w[0]
    for k in range(1, width):
        y = y + xp[:, k:k + t] * w[k]
    return y + b, xp[:, t:]

def _lin_combine(left, right):
    a1, b1 = left
    a2, b2 = right
    return a1 * a2, a2 * b1 + b2

def _rglru_block(h, conv_buf, h0, w_in, conv_w, conv_b, wa, ba, wx, bx, lam, w_out):
    bsz, t, _ = h.shape
    u = h @ w_in
    gate_br, x_br = jnp.split(u, 2, axis=-1)
    xc, conv_new = _causal_dwconv(x_br, conv_buf, conv_w, conv_b)
    xb = xc.reshape(bsz, t, RG_BLOCKS, RG_BLOCK_W)
    r = jax.nn.sigmoid(jnp.einsum('bthi,hij->bthj', xb, wa).reshape(bsz, t, D_RNN).astype(jnp.float32) + ba.astype(jnp.float32))
    i = jax.nn.sigmoid(jnp.einsum('bthi,hij->bthj', xb, wx).reshape(bsz, t, D_RNN).astype(jnp.float32) + bx.astype(jnp.float32))
    log_a = -RG_C * r * jax.nn.softplus(-lam.astype(jnp.float32))
    a = jnp.exp(log_a)
    b = jnp.sqrt(-jnp.expm1(2.0 * log_a)) * (i * xc.astype(jnp.float32))
    b = b.at[:, 0].add(a[:, 0] * h0.astype(jnp.float32))
    _, hs = lax.associative_scan(_lin_combine, (a, b), axis=1)
    y = (jax.nn.gelu(gate_br) * hs.astype(h.dtype)) @ w_out
    return y, conv_new, hs[:, -1]

def _conv_ffn(h, buf, w_up, conv_w, conv_b, w_down):
    u = h @ w_up
    uc, buf_new = _causal_dwconv(u, buf, conv_w, conv_b)
    g, v = jnp.split(uc, 2, axis=-1)
    return (jax.nn.gelu(g) * v) @ w_down, buf_new

def _forgetting_attention(q, k, v, cq, ck, q_pos, k_pos):
    bsz, t, nh, hd = q.shape
    qb = min(Q_BLOCK, t)
    nblk = -(-t // qb)
    pad = nblk * qb - t
    qp = jnp.pad(q, ((0, 0), (0, pad), (0, 0), (0, 0)))
    cqp = jnp.pad(cq, ((0, 0), (0, pad), (0, 0)))
    posp = jnp.pad(q_pos, (0, pad), mode='edge')
    q_blocks = jnp.moveaxis(qp.reshape(bsz, nblk, qb, nh, hd), 1, 0)
    cq_blocks = jnp.moveaxis(cqp.reshape(bsz, nblk, qb, nh), 1, 0)
    pos_blocks = posp.reshape(nblk, qb)
    ck_t = jnp.transpose(ck, (0, 2, 1))[:, :, None, :]
    scale = 1.0 / math.sqrt(hd)

    def one_block(args):
        qblk, cqblk, pblk = args
        s = jnp.einsum('bqhd,bkhd->bhqk', qblk, k, preferred_element_type=jnp.float32) * scale
        s = s + jnp.transpose(cqblk, (0, 2, 1))[..., None] - ck_t
        mask = k_pos[None, :] <= pblk[:, None]
        s = jnp.where(mask, s, -jnp.inf)
        p = jax.nn.softmax(s, axis=-1)
        return jnp.einsum('bhqk,bkhd->bqhd', p.astype(v.dtype), v)

    o = lax.map(one_block, (q_blocks, cq_blocks, pos_blocks))
    return jnp.moveaxis(o, 0, 1).reshape(bsz, nblk * qb, nh, hd)[:, :t]

def _trunk(x, c, k_past, v_past, lf_past, rg_conv_buf, rg_h0, ffn_buf, p):
    bsz, t, _ = x.shape
    past = k_past.shape[1]
    q_pos = past + jnp.arange(t, dtype=jnp.int32)
    k_pos = jnp.arange(past + t, dtype=jnp.int32)
    c_act = jax.nn.silu(c)
    hw = N_HEADS * HEAD_DIM
    rg_conv_new, rg_h_new, ffn_new = [], [], []
    for l in range(DEPTH):
        mod = c_act @ p['mod_w'][l] + p['mod_b'][l]
        sh1, sc1, g1, sh2, sc2, g2 = jnp.split(mod, 6, axis=-1)
        hn = _modnorm(x, p['norm_mix_g'][l], sh1, sc1)
        if l < N_A_LAYERS:
            out, cb, hl = _rglru_block(hn, rg_conv_buf[l], rg_h0[l], p['rg_w_in'][l], p['rg_conv_w'][l],
                                       p['rg_conv_b'][l], p['rg_wa'][l], p['rg_ba'][l], p['rg_wx'][l],
                                       p['rg_bx'][l], p['rg_lambda'][l], p['rg_w_out'][l])
            rg_conv_new.append(cb)
            rg_h_new.append(hl)
        else:
            j = l - N_A_LAYERS
            q = (hn @ p['fa_wq'][j]).reshape(bsz, t, N_HEADS, HEAD_DIM)
            o = _forgetting_attention(q, k_all, v_all, cq, cum, q_pos, k_pos)
            out = o.reshape(bsz, t, hw) @ p['fa_wo'][j]
        x = x + ((1.0 + g1)[:, None, :] * out).astype(x.dtype)
        hn = _modnorm(x, p['norm_ffn_g'][l], sh2, sc2)
        out, fb = _conv_ffn(hn, ffn_buf[l], p['ffn_w_up'][l], p['ffn_conv_w'][l], p['ffn_conv_b'][l], p['ffn_w_down'][l])
        ffn_new.append(fb)
        x = x + ((1.0 + g2)[:, None, :] * out).astype(x.dtype)
        if l == N_A_LAYERS - 1:
            kv_shift, kv_scale = jnp.split(c_act @ p['kv_mod_w'] + p['kv_mod_b'], 2, axis=-1)
            hk = _modnorm(x, p['kv_norm_g'], kv_shift, kv_scale)
            proj = hk @ p['kv_w']
            k_new = proj[..., :hw].reshape(bsz, t, N_HEADS, HEAD_DIM)
            v_new = proj[..., hw:2 * hw].reshape(bsz, t, N_HEADS, HEAD_DIM)
            lf_new = jax.nn.log_sigmoid(proj[..., 2 * hw:].astype(jnp.float32) + p['kv_b_f'].astype(jnp.float32))
            k_all = jnp.concatenate([k_past.astype(k_new.dtype), k_new], axis=1)
            v_all = jnp.concatenate([v_past.astype(v_new.dtype), v_new], axis=1)
            cum = jnp.cumsum(jnp.concatenate([lf_past.astype(jnp.float32), lf_new], axis=1), axis=1)
            cq = cum[:, past:]
    y = _rmsnorm(x, p['final_norm_g']).astype(x.dtype)
    return y, k_new, v_new, lf_new, jnp.stack(rg_conv_new), jnp.stack(rg_h_new), jnp.stack(ffn_new)

def setup_inputs(seed: int = 0) -> dict:
    key = jax.random.key(seed)
    ks = jax.random.split(key, 40)

    def nrm(k, shape, scale):
        return jax.random.normal(k, shape, jnp.float32) * scale

    n_pages = PAST_LEN // PAGE_SIZE
    n_used = DEC_BATCH * n_pages
    n_phys = n_used + max(1, n_used // 4)
    u = jax.random.uniform(ks[22], (N_A_LAYERS, D_RNN), jnp.float32, 0.9, 0.999)
    a_base = u ** (1.0 / RG_C)
    return {
        'x_prompt': nrm(ks[0], (BATCH, SEQ, D_MODEL), 1.0),
        'x_sample': nrm(ks[1], (DEC_BATCH, DEC_SEQ, D_MODEL), 1.0),
        'c_prompt': nrm(ks[2], (BATCH, D_MODEL), 1.0),
        'c_sample': nrm(ks[3], (DEC_BATCH, D_MODEL), 1.0),
        'cache_k': nrm(ks[4], (n_phys, PAGE_SIZE, N_HEADS, HEAD_DIM), 1.0),
        'cache_v': nrm(ks[5], (n_phys, PAGE_SIZE, N_HEADS, HEAD_DIM), 1.0),
        'cache_logf': jax.nn.log_sigmoid(nrm(ks[6], (n_phys, PAGE_SIZE, N_HEADS), 1.0) + 3.0),
        'page_table': jax.random.permutation(ks[7], n_phys)[:n_used].reshape(DEC_BATCH, n_pages).astype(jnp.int32),
        'state_rglru_conv': nrm(ks[8], (N_A_LAYERS, DEC_BATCH, RG_CONV_W - 1, D_RNN), 1.0),
        'state_rglru_h': nrm(ks[9], (N_A_LAYERS, DEC_BATCH, D_RNN), 0.5),
        'state_ffn_conv': nrm(ks[10], (DEPTH, DEC_BATCH, FFN_CONV_W - 1, 2 * D_FF), 1.0),
        'mod_w': nrm(ks[11], (DEPTH, D_MODEL, 6 * D_MODEL), 0.1 * D_MODEL ** -0.5),
        'mod_b': nrm(ks[12], (DEPTH, 6 * D_MODEL), 0.02),
        'norm_mix_g': 1.0 + nrm(ks[13], (DEPTH, D_MODEL), 0.05),
        'norm_ffn_g': 1.0 + nrm(ks[14], (DEPTH, D_MODEL), 0.05),
        'rg_w_in': nrm(ks[15], (N_A_LAYERS, D_MODEL, 2 * D_RNN), D_MODEL ** -0.5),
        'rg_conv_w': nrm(ks[16], (N_A_LAYERS, RG_CONV_W, D_RNN), RG_CONV_W ** -0.5),
        'rg_conv_b': nrm(ks[17], (N_A_LAYERS, D_RNN), 0.02),
        'rg_wa': nrm(ks[18], (N_A_LAYERS, RG_BLOCKS, RG_BLOCK_W, RG_BLOCK_W), RG_BLOCK_W ** -0.5),
        'rg_ba': nrm(ks[19], (N_A_LAYERS, D_RNN), 0.02),
        'rg_wx': nrm(ks[20], (N_A_LAYERS, RG_BLOCKS, RG_BLOCK_W, RG_BLOCK_W), RG_BLOCK_W ** -0.5),
        'rg_bx': nrm(ks[21], (N_A_LAYERS, D_RNN), 0.02),
        'rg_lambda': jnp.log(a_base) - jnp.log1p(-a_base),
        'rg_w_out': nrm(ks[23], (N_A_LAYERS, D_RNN, D_MODEL), D_RNN ** -0.5),
        'kv_norm_g': 1.0 + nrm(ks[24], (D_MODEL,), 0.05),
        'kv_mod_w': nrm(ks[25], (D_MODEL, 2 * D_MODEL), 0.1 * D_MODEL ** -0.5),
        'kv_mod_b': nrm(ks[26], (2 * D_MODEL,), 0.02),
        'kv_w': nrm(ks[27], (D_MODEL, 2 * N_HEADS * HEAD_DIM + N_HEADS), D_MODEL ** -0.5),
        'kv_b_f': jax.random.uniform(ks[28], (N_HEADS,), jnp.float32, 1.0, 5.0),
        'fa_wq': nrm(ks[29], (N_B_LAYERS, D_MODEL, N_HEADS * HEAD_DIM), D_MODEL ** -0.5),
        'fa_wo': nrm(ks[30], (N_B_LAYERS, N_HEADS * HEAD_DIM, D_MODEL), (N_HEADS * HEAD_DIM) ** -0.5),
        'ffn_w_up': nrm(ks[31], (DEPTH, D_MODEL, 2 * D_FF), D_MODEL ** -0.5),
        'ffn_conv_w': nrm(ks[32], (DEPTH, FFN_CONV_W, 2 * D_FF), FFN_CONV_W ** -0.5),
        'ffn_conv_b': nrm(ks[33], (DEPTH, 2 * D_FF), 0.02),
        'ffn_w_down': nrm(ks[34], (DEPTH, D_FF, D_MODEL), D_FF ** -0.5),
        'final_norm_g': 1.0 + nrm(ks[35], (D_MODEL,), 0.05),
    }

def reference(x_prompt, x_sample, c_prompt, c_sample, cache_k, cache_v, cache_logf, page_table,
              state_rglru_conv, state_rglru_h, state_ffn_conv, mod_w, mod_b, norm_mix_g, norm_ffn_g,
              rg_w_in, rg_conv_w, rg_conv_b, rg_wa, rg_ba, rg_wx, rg_bx, rg_lambda, rg_w_out,
              kv_norm_g, kv_mod_w, kv_mod_b, kv_w, kv_b_f, fa_wq, fa_wo,
              ffn_w_up, ffn_conv_w, ffn_conv_b, ffn_w_down, final_norm_g):
    p = dict(mod_w=mod_w, mod_b=mod_b, norm_mix_g=norm_mix_g, norm_ffn_g=norm_ffn_g,
             rg_w_in=rg_w_in, rg_conv_w=rg_conv_w, rg_conv_b=rg_conv_b, rg_wa=rg_wa, rg_ba=rg_ba,
             rg_wx=rg_wx, rg_bx=rg_bx, rg_lambda=rg_lambda, rg_w_out=rg_w_out,
             kv_norm_g=kv_norm_g, kv_mod_w=kv_mod_w, kv_mod_b=kv_mod_b, kv_w=kv_w, kv_b_f=kv_b_f,
             fa_wq=fa_wq, fa_wo=fa_wo, ffn_w_up=ffn_w_up, ffn_conv_w=ffn_conv_w,
             ffn_conv_b=ffn_conv_b, ffn_w_down=ffn_w_down, final_norm_g=final_norm_g)

    bsz = x_prompt.shape[0]
    empty_kv = jnp.zeros((bsz, 0, N_HEADS, HEAD_DIM), x_prompt.dtype)
    empty_lf = jnp.zeros((bsz, 0, N_HEADS), jnp.float32)
    zero_rc = jnp.zeros((N_A_LAYERS, bsz, RG_CONV_W - 1, D_RNN), x_prompt.dtype)
    zero_rh = jnp.zeros((N_A_LAYERS, bsz, D_RNN), jnp.float32)
    zero_fc = jnp.zeros((DEPTH, bsz, FFN_CONV_W - 1, 2 * D_FF), x_prompt.dtype)
    y_prompt, p_k, p_v, p_lf, p_rc, p_rh, p_fc = _trunk(
        x_prompt, c_prompt, empty_kv, empty_kv, empty_lf, zero_rc, zero_rh, zero_fc, p)

    dbsz = x_sample.shape[0]
    past_len = page_table.shape[1] * cache_k.shape[1]
    k_past = cache_k[page_table].reshape(dbsz, past_len, N_HEADS, HEAD_DIM)
    v_past = cache_v[page_table].reshape(dbsz, past_len, N_HEADS, HEAD_DIM)
    lf_past = cache_logf[page_table].reshape(dbsz, past_len, N_HEADS)
    y_sample, s_k, s_v, s_lf, s_rc, s_rh, s_fc = _trunk(
        x_sample, c_sample, k_past, v_past, lf_past, state_rglru_conv, state_rglru_h, state_ffn_conv, p)

    return (y_prompt, y_sample, p_k, p_v, p_lf, p_rc, p_rh, p_fc, s_k, s_v, s_lf, s_rc, s_rh, s_fc)


_drawn_inputs = setup_inputs


def setup_inputs(seed=0):
    import zlib

    import numpy as np

    out = dict(_drawn_inputs(seed))
    spreads = {}
    factors = {'rg_ba': 8.0, 'rg_bx': 7.42, 'ffn_conv_b': 2.689}
    for name, (base, spread) in spreads.items():
        noise = np.random.default_rng([zlib.crc32(name.encode()), seed]).standard_normal(out[name].shape)
        drawn = base * np.exp(spread * noise) if base else spread * noise
        out[name] = __import__('jax').numpy.asarray(drawn.astype(out[name].dtype))
    for name, factor in factors.items():
        out[name] = (out[name] * factor).astype(out[name].dtype)
    return out
```

```python
from contextlib import ExitStack, contextmanager

import concourse.bass as bass
from concourse import mybir

ALU = mybir.AluOpType
ACT = mybir.ActivationFunctionType
F32 = mybir.dt.float32
F32R = mybir.dt.float32r
BF16 = mybir.dt.bfloat16
AX_X = mybir.AxisListType.X

P = 128
D = 1024
KT = D // P
SEQ = 1024
NB, TD = 8, 8
TS = NB * TD
T = SEQ + TS
NV = 1 + NB
D_RNN = 1280
RT = D_RNN // P
RH = RT // 2
D_FF = 3072
FT = D_FF // P
GC = 4
NG = FT // GC
NH, HD = 16, 64
PAGE, NPG = 128, 4
PAST = PAGE * NPG
EPS = 1e-6
NEG = -1e30
KV_ROUNDS = 2 * KT // 4
UNIT = KT * P

SH1, SC1, G1, SH2, SC2, G2 = range(6)
MT = 2 * 6 * KT + 2 * KT


def mod_at(layer, chunk):
    return (layer * 6 + chunk) * KT


KV_SH, KV_SC = 2 * 6 * KT, 2 * 6 * KT + KT
NORMS = [(mod_at(0, SH1), mod_at(0, SC1)), (mod_at(0, SH2), mod_at(0, SC2)), (KV_SH, KV_SC),
         (mod_at(1, SH1), mod_at(1, SC1)), (mod_at(1, SH2), mod_at(1, SC2)), None]

RG_W = D_RNN // 16
GATE_IN = []
for _j in range(RT):
    _b0, _b1 = (P * _j) // RG_W, (P * _j + P - 1) // RG_W
    GATE_IN.append(list(range(RG_W * _b0 // P, (RG_W * (_b1 + 1) - 1) // P + 1)))

U_RG, U_OUT, U_FFN, U_LF, U_D = 2 * RT, 2 * KT, 2 * FT + NG * GC, 2, KT
UNITS_1 = U_RG + U_OUT + U_FFN + U_LF + 3 * U_D
UNITS_2 = U_D + U_FFN
PIECES = ((0, 512), (512, 1024), (1024, T))


class Count:

    def __init__(self, sem, n=0):
        self.sem, self.n, self.loop = sem, n, 0

    def next(self, k=1):
        self.n += k
        return self.n + self.loop

    def now(self):
        return self.n + self.loop


@contextmanager
def rounds(eng, trips, per):
    before = [(c, c.n, c.loop) for c in per]
    with eng.Fori(0, trips) as i:
        for c, k in per.items():
            c.loop = c.loop + i * k
        yield i
    for c, n, loop in before:
        assert c.n - n == per[c], (c.sem, c.n - n, per[c])
        c.n, c.loop = n + per[c] * trips, loop


def trunk(nc, I, O):
    ctx = ExitStack()
    B0 = 16512
    placed = []

    def at(name, off, shape, dt=F32):
        size = 4 if dt != BF16 else 2
        for s in shape[1:]:
            size *= s
        placed.append(off + size)
        assert off + size <= 212832, (name, off + size)
        return nc.alloc_sbuf_tensor_at(name, shape, dt, offset=B0 + off, align_bytes=4)

    class Area:
        def __init__(self, off, end):
            self.off, self.end = off, end

        def __call__(self, name, shape, dt=F32):
            t = at(name, self.off, shape, dt)
            self.off = (placed[-1] + 31) // 32 * 32
            assert placed[-1] <= self.end, (name, placed[-1], self.end)
            return t

    TB = T * 4
    O_X, O_HN, O_R3, O_W, O_C = 0, KT * TB, 3 * KT * TB, 3 * KT * TB + 65280, 3 * KT * TB + 65280 + 6 * UNIT * 4

    X = at("X", O_X, [P, KT, T])
    HH = at("HH", O_HN, [P, KT, T], F32R)
    HL = at("HL", O_HN + KT * TB, [P, KT, T], F32R)
    w = Area(O_W, O_C)
    WRAW = w("WRAW", [P, 2, UNIT])
    WH = w("WH", [P, 2, UNIT], F32R)
    WL = w("WL", [P, 2, UNIT], F32R)
    c = Area(O_C, 212832)
    MOD = c("MOD", [P, MT, NV])
    MODB = c("MODB", [P, MT])
    NGAIN = c("NGAIN", [P, 6, KT])
    RS_OFF = c.off
    RS = c("RS", [P, T])
    ID = c("ID", [P, P])
    ONES = c("ONES", [P, P])
    IDB = c("IDB", [P, P], BF16)
    MSKB = c("MSKB", [P, P], BF16)
    RGP = c("RGP", [P, RT, 8])
    SP4 = c("SP4", [P, RT])
    SPT = c("SPT", [P, 4, RT])
    H0 = c("H0", [P, RT, NB])
    KVB = c("KVB", [NH, 1])
    CT = c("CT", [P, KT, NV])
    SG = c("SG", [P, KT, NV])
    ZERO = c("ZERO", [P, 1])
    TINY = c("TINY", [P, 1])
    NM = c("NM", [P, 4])
    SUM = c("SUM", [P, 4])
    RI = c("RI", [P, 4])
    CQ = c("CQ", [P, KT, NH])
    EA = c("EA", [P, P])
    BM = c("BM", [P, NB])
    MQ = c("MQ", [P, TD])
    CQS = c("CQS", [P, NB])
    LFN = c("LFN", [P, TD])
    CN = c("CN", [P, TD])
    CNM = c("CNM", [P, NB, TD])
    CQT = c("CQT", [P, NB, TD])
    CUM_OFF = c.off
    CUM = c("CUM", [NH, SEQ])
    CUMM = at("CUMM", CUM_OFF, [P, PAST + TS])
    CUMS = at("CUMS", RS_OFF, [P, PAST + TS])
    MKS = at("MKS", RS_OFF + 4 * (PAST + TS), [P, NB, TS])

    MW = at("MW", O_R3, [P, 4, 2, UNIT])

    n_ = Area(O_R3, O_W)
    SQ = n_("SQ", [P, 2, T])
    ACC = n_("ACC", [P, T])
    TN = n_("TN", [P, 2, T])
    NT = n_("NT", [P, T])
    YO = n_("YO", [P, 2, T])

    r = Area(O_X, O_HN)
    WU = 3 + SEQ + NB * (3 + TD)
    RU = r("RU", [P, WU])
    RS1 = r("RS1", [P, T])
    RI1 = r("RI1", [P, T])
    RW1 = r("RW1", [P, T])
    RQ1 = r("RQ1", [P, T])
    RA1 = r("RA1", [P, T])
    GW = r("GW", [P, 2, 2, 3, P])
    RHALO = r("RHALO", [P, RT, NB * 3])
    RST = r("RST", [P, RT, 3 * NV])
    HST = at("HST", placed[-1], [P, RT, NV])
    assert placed[-1] <= O_HN
    XC = at("XC", O_R3, [P, RH, T])
    YG = at("YG", O_R3 + RH * TB, [P, RT, T])
    YH = at("YH", O_HN, [P, RT, T], F32R)
    YL = at("YL", O_HN + RT * TB, [P, RT, T], F32R)

    f = Area(O_R3, O_W)
    AH = f("AH", [P, GC, T], F32R)
    AL = f("AL", [P, GC, T], F32R)
    WF = 2 + SEQ + NB * (2 + TD)
    FU = f("FU", [P, 2, WF])
    FC = f("FC", [P, 2, T])
    FHALO = f("FHALO", [P, 2 * FT, NB * 2])
    FST = f("FST", [P, 2 * FT, 2 * NV])
    FCW = f("FCW", [P, 2 * FT, 4])
    XS = f("XS", [P, 2, TS])

    kv = Area(O_R3, O_W)
    STG = kv("STG", [P, 4, T])
    LZ = kv("LZ", [NH, T])
    LA = kv("LA", [NH, T])
    LE = kv("LE", [NH, T])
    LF = kv("LF", [NH, T])
    Q = at("Q", O_R3, [P, KT, T])
    OT = at("OT", O_HN, [P, KT, T])
    a = Area(O_HN + KT * TB, O_R3)
    KP = a("KP", [P, 2, SEQ])
    VT = a("VT", [P, 2, SEQ])
    V = a("V", [P, KT, P])
    QS = a("QS", [P, SEQ])
    SB01 = a("SB01", [P, 2, SEQ])
    b = Area(O_R3 + KT * TB, O_W)
    PT = b("PT", [P, 2, SEQ])
    NBC = b("NBC", [P, 2, SEQ])
    SB23 = b("SB23", [P, 2, SEQ])
    CUMH = b("CUMH", [NH, SEQ])
    SBUFS = [SB01[:, 0, :], SB01[:, 1, :], SB23[:, 0, :], SB23[:, 1, :]]
    a = Area(O_HN + KT * TB, O_R3)
    KB = a("KB", [P, 2, KT, PAST])
    KS = a("KS", [P, KT, TS])
    b = Area(O_R3 + KT * TB, O_W)
    VB = b("VB", [P, NPG, D])
    QX = b("QX", [P, KT * (P + 16)])
    SS = b("SS", [P, PAST + TS])
    PTS = b("PTS", [P, NPG + 1, P])
    VN = b("VN", [TS, D])
    LFP = at("LFP", O_HN + KT * TB, [P, PAST])
    OH = at("OH", O_HN + KT * TB, [P, KT, T], F32R)
    OL = at("OL", O_R3, [P, KT, T], F32R)

    PS = ctx.enter_context(nc.psum_tensor("PS", [P, 8 * 512], F32))
    SLOT = (0, 1536)

    names = """w_raw0 w_raw1 pool_hi split_done unit_used ready0 ready1 free0 free1
        mw0 mw1 mw2 mw3 mw_used consts filled sigmoid silu mods_psum mods_done lam_exp sp_done x_in
        act_sq dve_acc dve_var act_root act_hi dve_tn dve_lo act_self dve_self
        rg_halo gate_w0 gate_w1 conv_free xc_ready act_tanh act_sqrt pair_free
        y_hi y_ready x_done x_back rst_out ffn_in ffn_out f_conv f_gelu f_prod f_hi act_ready
        kv_out0 kv_out1 kv_out2 kv_out3 lf_e lf_ready lf_out q_ready
        kv_in0 kv_in1 qs_ready cumh s_ready s_free0 s_free1 stt_done exp_done p_ready pt_psum pt_ready
        o_psum o_free pair_done cq_psum cq_done
        lfp_in lfn_in kb_in0 kb_in1 vb_in kb_used vb_used ks_in vst_in vn_psum vn_ready qx_ready cumm_ready
        sc_psum sc_nm sc_exp sc_p sc_ptp sc_pt sc_o sc_done sconst o_hi o_ready y_out0 y_out1""".split()
    S = {n: ctx.enter_context(nc.semaphore(n)) for n in names}

    def bc_t(ap):
        return ap.unsqueeze(2).broadcast_to([ap.shape[0], NB, TD])

    def req(ap):
        return ap.rearrange("p (b t) -> p b t", b=NB)

    block = ctx.enter_context(nc.Block())

    @block.sync
    def _(sp):
        def weights(first, units, peel):
            k = 0
            if peel:
                for u in range(2):
                    sp.dma_start(WRAW[:, u, :], I["wstream"][u]).then_inc(S[f"w_raw{u}"], 16)
                k = 1
            with sp.Fori(k, units // 2) as i:
                for u in range(2):
                    sp.wait_ge(S["split_done"], first + i * 2 + u - 1)
                    sp.dma_start(WRAW[:, u, :], I["wstream"][i * 2 + first + u]).then_inc(S[f"w_raw{u}"], 16)

        for dst, src in ((CT, "cT"), (MODB, "mod_b"), (NGAIN, "gains"), (ID, "ident"), (CQ, "mask"), (RGP, "rg_par"), (H0, "rg_h0"), (KVB, "kv_b"), (EA, "pick_head"),
                         (BM, "req_rows"), (MQ, "pick_q")):
            sp.dma_start(dst[:], I[src]).then_inc(S["consts"], 16)
        for v in range(4):
            sp.dma_start(MW[:, v], I["mod_w"][v]).then_inc(S[f"mw{v}"], 16)
        sp.dma_start(X[:], I["xT"].rearrange("k p t -> p k t")).then_inc(S["x_in"], 16)
        with sp.Fori(1, MT // 8) as i:
            for v in range(4):
                sp.wait_ge(S["mw_used"], i * 4 + (v - 3))
                sp.dma_start(MW[:, v], I["mod_w"][i * 4 + v]).then_inc(S[f"mw{v}"], 16)
        weights(0, UNITS_1, True)

        for n in range(4):
            sp.wait_ge(S[f"kv_out{n}"], KV_ROUNDS * 16 + 16)
        sp.wait_ge(S["q_ready"], 2)
        with sp.Fori(0, KT // 2) as i:
            for e in range(2):
                sp.wait_ge(S["pair_done"], i * 2 + (e + 1))
                sp.dma_start(KP[:, e, :], O["kv"][i * 2 + e, :, 0:SEQ]).then_inc(S[f"kv_in{e}"], 16)
                sp.dma_start(VT[:, e, :], O["kv"][i * 2 + (KT + e), :, 0:SEQ]).then_inc(S[f"kv_in{e}"], 16)

        sp.wait_ge(S["pair_done"], KT + 2)
        sp.wait_ge(S["lf_out"], 16)
        for k in range(NB):
            sp.dma_start(LFN[16 * k:16 * k + 16, :], O["lf"][:, SEQ + TD * k:SEQ + TD * k + TD])\
              .then_inc(S["lfn_in"], 16)
        sp.dma_start(KS[:], O["kv"][0:KT, :, SEQ:T].rearrange("k p t -> p k t")).then_inc(S["ks_in"], 16)
        sp.dma_start(PTS[:, 0:4, :].rearrange("p a c -> p (a c)"),
                         O["kv"][KT:2 * KT, :, SEQ:T].rearrange("k p t -> p k t")).then_inc(S["vst_in"], 16)
        sp.dma_start(MKS[:], I["mask_new"]).then_inc(S["sconst"], 16)
        for k in range(NB):
            for g in range(NPG):
                page = sp.value_load(I["page_table"][0:1, k * NPG + g:k * NPG + g + 1], min_val=0,
                                     max_val=I["cache_k"].shape[0] - 1)
                sp.dma_start(LFP[16 * k:16 * k + 16, g * PAGE:(g + 1) * PAGE],
                             I["cache_lf"][page]).then_inc(S["lfp_in"], 16)
        with sp.Fori(0, NB // 2) as i:
            for e in range(2):
                for g in range(NPG):
                    page = sp.value_load(I["page_table"][0:1, bass.ds(i * 2 * NPG + (e * NPG + g), 1)], min_val=0,
                                         max_val=I["cache_k"].shape[0] - 1)
                    if g == 0:
                        sp.wait_ge(S["kb_used"], i * 2 + (e + 1))
                        sp.wait_ge(S["vb_used"], i * 2 + (e + 1))
                    sp.dma_start(KB[:, e, :, g * PAGE:(g + 1) * PAGE], I["cache_k"][page])\
                      .then_inc(S[f"kb_in{e}"], 16)
                    sp.dma_start(VB[:, g, :], I["cache_v"][page]).then_inc(S["vb_in"], 16)
        weights(UNITS_1, UNITS_2, False)

    @block.gpsimd
    def _(pool):
        pool.memset(ZERO[:], 0.0).then_inc(S["filled"], 1)
        pool.memset(ONES[:], 1.0).then_inc(S["filled"], 1)
        pool.memset(TINY[:], 1e-30).then_inc(S["filled"], 1)
        pool.wait_ge(S["filled"], 3)
        with pool.Fori(0, (UNITS_1 + UNITS_2) // 2) as i:
            for u in range(2):
                pool.wait_ge(S[f"w_raw{u}"], i * 16 + 16)
                pool.wait_ge(S["unit_used"], i * 2 + (u + 1))
                pool.tensor_tensor(WH[:, u, :], WRAW[:, u, :], ZERO[:].broadcast_to([P, UNIT]),
                                   ALU.add).then_inc(S["pool_hi"], 1)
                pool.wait_ge(S["pool_hi"], i * 2 + (u + 1))
                pool.tensor_tensor(WL[:, u, :], WRAW[:, u, :], WH[:, u, :].bitcast(F32),
                                   ALU.subtract).then_inc(S["split_done"], 1)

    @block.tensor
    def _(pe):
        split = Count(S["split_done"])
        free = [Count(S["free0"]), Count(S["free1"])]
        ready = [S["ready0"], S["ready1"]]
        acc, hn = Count(S["dve_acc"], 2), Count(S["dve_lo"], 1)
        act_chunk = Count(S["act_ready"], 1)
        pe.sem_inc(S["unit_used"], 2)
        pe.sem_inc(S["vb_used"], 1)

        def tiles(t, u):
            return lambda n: t[:, u, n * P:(n + 1) * P]

        def job(slot, wh, wl, xh, xl, kts, first=True, last=True):
            for n, k in enumerate(kts):
                for m, (lhs, rhs) in enumerate(((wh, xh), (wh, xl), (wl, xh))):
                    for lo, hi in PIECES:
                        mm = pe.matmul(PS[:, SLOT[slot] + lo:SLOT[slot] + hi], lhs(n), rhs[:, k, lo:hi],
                                       start=first and n == 0 and m == 0,
                                       stop=last and n == len(kts) - 1 and m == 2)
            return mm

        def release(n=1):
            pe.drain().then_inc(S["unit_used"], n)

        def unit_job(u, xh, xl):
            pe.wait_ge(split.sem, split.next())
            pe.wait_ge(free[u].sem, free[u].next())
            job(u, tiles(WH, u), tiles(WL, u), xh, xl, range(KT)).then_inc(ready[u], 1)
            release()

        def proj(xh, xl, pairs):
            with rounds(pe, pairs, {split: 2, free[0]: 1, free[1]: 1}):
                for u in range(2):
                    unit_job(u, xh, xl)

        def norm(sums=True, tiles_follow=True):
            if sums:
                pe.wait_ge(acc.sem, acc.next(KT))
                pe.wait_ge(free[0].sem, free[0].next())
                for lo, hi in PIECES:
                    mm = pe.matmul(PS[:, lo:hi], ONES[:], ACC[:, lo:hi], start=True, stop=True)
                mm.then_inc(ready[0], 1)
            if tiles_follow:
                pe.wait_ge(hn.sem, hn.next(KT))

        pe.wait_ge(S["silu"], 1)
        for bank, (v0, n) in enumerate(((0, 6), (6, 6), (12, 2))):
            with pe.Fori(0, n) as i:
                for v in range(4):
                    pe.wait_ge(S[f"mw{v}"], i * 16 + (v0 + 1) * 16)
                    for o in range(2):
                        for k in range(KT):
                            mm = pe.matmul(PS[:, bass.ds(i * (8 * NV) + (512 * bank + (v * 2 + o) * NV), NV)],
                                           MW[:, v, o, k * P:(k + 1) * P], CT[:, k, :],
                                           start=(k == 0), stop=(k == KT - 1))
                    mm.then_inc(S["mw_used"], 1)
        norm()
        gate_w, xc = [Count(S["gate_w0"]), Count(S["gate_w1"])], Count(S["xc_ready"])
        for half in range(2):
            with rounds(pe, RH, {split: 2, free[0]: 1, free[1]: 1}):
                for u in range(2):
                    unit_job(u, HH, HL)
            for j in range(RH):
                kk = [k - RH * half for k in GATE_IN[RH * half + j]]
                pe.wait_ge(xc.sem, RH * half + max(kk) + 1)
                gw = gate_w[(RH * half + j) % 2]
                pe.wait_ge(gw.sem, gw.next(16))
                for u in range(2):
                    pe.wait_ge(free[u].sem, free[u].next())
                    for n, k in enumerate(kk):
                        for lo, hi in PIECES:
                            mm = pe.matmul(PS[:, SLOT[u] + lo:SLOT[u] + hi], GW[:, (RH * half + j) % 2, u, n, :],
                                           XC[:, k, lo:hi], start=(n == 0), stop=(n == len(kk) - 1))
                    mm.then_inc(ready[u], 1)
        pe.wait_ge(S["y_ready"], RT)
        with rounds(pe, KT // 2, {split: 4, free[0]: 1, free[1]: 1}):
            for s in range(2):
                pe.wait_ge(free[s].sem, free[s].next())
                for u in range(2):
                    pe.wait_ge(split.sem, split.next())
                    mm = job(s, tiles(WH, u), tiles(WL, u), YH, YL, range(5 * u, 5 * u + 5), u == 0, u == 1)
                    if u == 1:
                        mm.then_inc(ready[s], 1)
                    release()

        def ffn():
            def up(pairs):
                with rounds(pe, pairs, {split: 2, free[0]: 1, free[1]: 1}):
                    for u in range(2):
                        unit_job(u, HH, HL)

            def down():
                chunks = act_chunk.next(GC)
                with rounds(pe, 2, {split: 2, free[0]: 2, free[1]: 2}):
                    pe.wait_ge(act_chunk.sem, chunks)
                    for u in range(2):
                        pe.wait_ge(split.sem, split.next())
                        for s in range(2):
                            pe.wait_ge(free[s].sem, free[s].next())
                            job(s, lambda n: WH[:, u, (s * GC + n) * P:(s * GC + n + 1) * P],
                                lambda n: WL[:, u, (s * GC + n) * P:(s * GC + n + 1) * P],
                                AH, AL, range(GC)).then_inc(ready[s], 1)
                        release()
            up(GC)
            with rounds(pe, NG - 1, {split: 12, free[0]: 8, free[1]: 8, act_chunk: GC}):
                up(1)
                down()
                up(GC - 1)
            down()

        norm()
        ffn()
        norm()
        pe.wait_ge(split.sem, split.next())
        pe.wait_ge(free[0].sem, free[0].next())
        job(0, tiles(WH, 0), tiles(WL, 0), HH, HL, range(KT)).then_inc(ready[0], 1)
        split.next()
        release(2)
        proj(HH, HL, KT)
        norm(sums=False)
        proj(HH, HL, KT // 2)

        s_free, o_free = [Count(S["s_free0"]), Count(S["s_free1"])], Count(S["o_free"])
        qs, nbr, p_rdy, pt_rdy = (Count(S[n]) for n in ("qs_ready", "cumh", "p_ready", "pt_ready"))
        kvi = [Count(S["kv_in0"]), Count(S["kv_in1"])]
        pe.wait_ge(S["q_ready"], 2)
        pe.wait_ge(S["lf_ready"], 2)
        for q in range(KT):
            mm = pe.transpose(PS[:, q * NH:(q + 1) * NH], CUM[:, q * P:(q + 1) * P], ID[0:NH, 0:NH])
        mm.then_inc(S["cq_psum"], 1)
        pe.wait_ge(S["cq_done"], 1)
        STEPS = 2 * KT
        per = {s_free[0]: 2 + STEPS // 2, s_free[1]: 2 + STEPS // 2, o_free: STEPS, qs: 1, kvi[0]: 16, kvi[1]: 16,
               nbr: 2, p_rdy: STEPS, pt_rdy: STEPS}
        with rounds(pe, KT // 2, {s_: 2 * k for s_, k in per.items()}):
            for par in range(2):
                sjob = 0

                def s_buffer():
                    nonlocal sjob
                    fr = s_free[sjob % 2]
                    pe.wait_ge(fr.sem, fr.next())
                    sjob += 1
                    return 1024 * ((sjob - 1) % 2)

                pe.wait_ge(kvi[par].sem, kvi[par].next(32))
                for hv in range(2):
                    o = s_buffer()
                    for k in range(4):
                        mm = pe.transpose(PS[:, o + k * P:o + (k + 1) * P], VT[:, par, (hv * 4 + k) * P:(hv * 4 + k + 1) * P], ID[:])
                    mm.then_inc(S["s_ready"], 1)
                pe.wait_ge(qs.sem, qs.next())
                for t in range(STEPS + 3):
                    if t < STEPS:
                        e, qi = divmod(t, KT)
                        rows = slice(HD * e, HD * e + HD)
                        if qi == 0:
                            pe.wait_ge(nbr.sem, nbr.next())
                            o = s_buffer()
                            for lo in (0, 512):
                                mm = pe.matmul(PS[:, o + lo:o + lo + 512], ONES[0:NH, :], CUMH[:, lo:lo + 512],
                                               start=True, stop=True)
                            mm.then_inc(S["s_ready"], 1)
                        o = s_buffer()
                        L = (qi + 1) * P
                        for lo in range(0, L, 512):
                            hi = min(L, lo + 512)
                            pe.matmul(PS[:, o + lo:o + hi], QS[rows, qi * P:(qi + 1) * P], KP[rows, par, lo:hi],
                                      start=True, stop=True)
                        mm = pe.matmul(PS[:, o + L - P:o + L], IDB[:], MSKB[:], start=False, stop=True,
                                       skip_group_check=True)
                        mm.then_inc(S["s_ready"], 1)
                    if t >= 3:
                        u = t - 3
                        e, qi = divmod(u, KT)
                        pe.wait_ge(pt_rdy.sem, pt_rdy.next())
                        pe.wait_ge(o_free.sem, o_free.next())
                        for k in range(qi + 1):
                            mm = pe.matmul(PS[HD * e:HD * e + HD, 3072 + 512 * (u % 2):3072 + 512 * (u % 2) + P],
                                           V[:, k, HD * e:HD * e + HD], PT[:, u % 2, k * P:(k + 1) * P],
                                           start=(k == 0), stop=(k == qi))
                        mm.then_inc(S["o_psum"], 1)
                    if 2 <= t < STEPS + 2:
                        u = t - 2
                        qi = u % KT
                        pe.wait_ge(p_rdy.sem, p_rdy.next())
                        for k in range(qi + 1):
                            mm = pe.transpose(PS[:, 2048 + k * P:2048 + (k + 1) * P], SBUFS[u % 4][:, k * P:(k + 1) * P], ID[:])
                        mm.then_inc(S["pt_psum"], 1)

        pe.wait_ge(S["vst_in"], 16)
        for k in range(KT):
            mm = pe.transpose(PS[0:TS, 2048 + k * P:2048 + (k + 1) * P],
                              PTS[:, 0:4, :].rearrange("p a c -> p (a c)")[:, k * TS:(k + 1) * TS], ID[:])
        mm.then_inc(S["vn_psum"], 1)
        pe.wait_ge(S["cumm_ready"], 1)
        pe.matmul(PS[:, 0:TS], EA[:], CNM[:].rearrange("p b t -> p (b t)"), start=True, stop=True)\
          .then_inc(S["cq_psum"], 1)
        pe.wait_ge(S["cq_done"], 2)
        pe.wait_ge(S["vn_ready"], 1)
        pe.wait_ge(S["ks_in"], 16)
        vbi, qx, scp, scpt = (Count(S[n]) for n in ("vb_in", "qx_ready", "sc_p", "sc_pt"))
        kbi = [Count(S["kb_in0"]), Count(S["kb_in1"])]
        with rounds(pe, NB // 2, {kbi[0]: 64, kbi[1]: 64, vbi: 128, qx: 2, scp: 2, scpt: 2}):
            for e in range(2):
                o = 1024 * e
                pe.wait_ge(kbi[e].sem, kbi[e].next(64))
                pe.wait_ge(qx.sem, qx.next())
                for k in range(KT):
                    pe.matmul(PS[:, o:o + 512], QX[:, k * P:(k + 1) * P], KB[:, e, k, :], start=(k == 0), stop=False)
                    pe.matmul(PS[:, o + 512:o + 512 + TS], QX[:, k * P:(k + 1) * P], KS[:, k, :], start=(k == 0), stop=False)
                pe.matmul(PS[:, o:o + 512], EA[:], CUMM[:, 0:512], start=False, stop=True)
                pe.matmul(PS[:, o + 512:o + 512 + TS], EA[:], CUMM[:, 512:512 + TS], start=False, stop=True)\
                  .then_inc(S["sc_psum"], 1)
                pe.drain().then_inc(S["kb_used"], 1)
                pe.wait_ge(scp.sem, scp.next())
                for k in range(NPG):
                    pe.transpose(PS[:, 2048 + k * P:2048 + (k + 1) * P], SS[:, k * P:(k + 1) * P], ID[:])
                pe.transpose(PS[0:TS, 2560:2560 + P], SS[:, PAST:PAST + TS], ID[:]).then_inc(S["sc_ptp"], 1)
                pe.wait_ge(vbi.sem, vbi.next(64))
                pe.wait_ge(scpt.sem, scpt.next())
                oo = 3072 + 512 * e
                for k in range(KT):
                    for g in range(NPG):
                        pe.matmul(PS[:, oo + 16 * k:oo + 16 * k + 16], VB[:, g, k * P:(k + 1) * P],
                                  PTS[:, g, 16 * k:16 * k + 16], start=(g == 0), stop=False)
                    mm = pe.matmul(PS[:, oo + 16 * k:oo + 16 * k + 16], VN[:, k * P:(k + 1) * P],
                                   PTS[0:TS, NPG, 16 * k:16 * k + 16], start=False, stop=True)
                mm.then_inc(S["sc_o"], 1)
                pe.drain().then_inc(S["vb_used"], 1)
        pe.wait_ge(S["sc_done"], NB)
        pe.wait_ge(S["o_ready"], KT)
        proj(OH, OL, KT // 2)
        norm()
        ffn()
        norm(tiles_follow=False)

    @block.scalar
    def _(act):
        ready, free = [Count(S["ready0"]), Count(S["ready1"])], [S["free0"], S["free1"]]
        sq_free, x_done, var, tn = Count(S["dve_acc"]), Count(S["x_done"]), Count(S["dve_var"]), Count(S["dve_tn"])
        me = Count(S["act_self"])
        for n in range(4):
            act.sem_inc(S[f"kv_out{n}"], 16)

        def chain(ins):
            ins.then_inc(me.sem, 1)
            act.wait_ge(me.sem, me.next())

        def got(s):
            act.wait_ge(ready[s].sem, ready[s].next())

        def norm(n, sums=True):
            if sums:
                with rounds(act, KT // 2, {sq_free: 2}) as i:
                    for u in range(2):
                        act.wait_ge(sq_free.sem, sq_free.next())
                        act.activation(SQ[:, u, :], X[:, i * 2 + u, :], ACT.Square).then_inc(S["act_sq"], 1)
                ready[0].next()
                act.wait_ge(var.sem, var.next())
                act.activation(RS[:], ACC[:], ACT.Sqrt).then_inc(S["act_root"], 1)
            if NORMS[n]:
                sh, sc = NORMS[n]
                with rounds(act, KT // 2, {tn: 2}) as i:
                    for u in range(2):
                        act.wait_ge(tn.sem, tn.next())
                        par = dict(scale=MOD[:, sc + u + i * 2, 0:1], bias=MOD[:, sh + u + i * 2, 0:1])
                        act.activation(HH[:, i * 2 + u, 0:SEQ], TN[:, u, 0:SEQ], ACT.Identity, **par)
                        act.activation(HH[:, i * 2 + u, SEQ:T], TN[:, u, SEQ:T], ACT.Copy)
                        act.activation(TN[:, u, 0:SEQ], TN[:, u, 0:SEQ], ACT.Identity, **par)\
                           .then_inc(S["act_hi"], 1)

        act.wait_ge(S["consts"], 16 * N_CONSTS)
        act.wait_ge(S["filled"], 3)
        act.activation(SG[:], CT[:], ACT.Sigmoid).then_inc(S["sigmoid"], 1)
        chain(act.activation(SPT[:, 0, :], RGP[:, :, 7], ACT.Abs))
        act.activation(SPT[:, 1, :], SPT[:, 0, :], ACT.Exp, scale=-1.0).then_inc(S["lam_exp"], 1)
        act.wait_ge(S["x_in"], 16)
        act.wait_ge(S["mods_done"], 1)
        norm(0)
        act.dma_start(RHALO[:], I["rg_halo"]).then_inc(S["rg_halo"], 16)
        act.wait_ge(S["rg_halo"], 16)
        conv_free, pair_free, tanh_ = Count(S["conv_free"]), Count(S["pair_free"]), Count(S["act_tanh"])
        for jt in range(2):
            act.dma_start(GW[:, jt], I["rg_gate_w"][jt]).then_inc(S[f"gate_w{jt}"], 16)
        for half in range(2):
            with rounds(act, RH, {ready[0]: 1, ready[1]: 1, conv_free: 1}) as j:
                got(0)
                act.wait_ge(conv_free.sem, conv_free.next())
                act.activation(RU[:, 3:3 + SEQ], PS[:, 0:SEQ], ACT.Copy)
                ru = RU[:, 3 + SEQ:WU].rearrange("p (b t) -> p b t", b=NB)
                act.activation(ru[:, :, 0:3], RHALO[:, j + RH * half, :].rearrange("p (b t) -> p b t", b=NB), ACT.Copy)
                act.activation(ru[:, :, 3:3 + TD], req(PS[:, SEQ:T]), ACT.Copy).then_inc(free[0], 1)
                got(1)
                act.activation(YG[:, j + RH * half, :], PS[:, 1536:1536 + T], ACT.Gelu_apprx_tanh).then_inc(free[1], 1)
            for j in range(RH):
                jt = RH * half + j
                act.wait_ge(pair_free.sem, pair_free.next())
                got(0)
                act.activation(RS1[:], PS[:, 0:T], ACT.Sigmoid, bias=RGP[:, jt, 5:6]).then_inc(free[0], 1)
                got(1)
                act.activation(RI1[:], PS[:, 1536:1536 + T], ACT.Sigmoid, bias=RGP[:, jt, 6:7]).then_inc(free[1], 1)
                if jt + 2 < RT:
                    act.dma_start(GW[:, jt % 2], I["rg_gate_w"][jt + 2]).then_inc(S[f"gate_w{jt % 2}"], 16)
                act.wait_ge(free[0], ready[0].now() + 1)
                act.wait_ge(free[1], ready[1].now() + 1)
                act.wait_ge(S["sp_done"], 1)
                act.activation(RS1[:], RS1[:], ACT.Tanh, scale=SP4[:, jt:jt + 1]).then_inc(tanh_.sem, 1)
                act.wait_ge(tanh_.sem, tanh_.next())
                act.activation(RQ1[:], RS1[:], ACT.Sqrt, bias=TINY[:]).then_inc(S["act_sqrt"], 1)
        act.wait_ge(pair_free.sem, pair_free.next())
        act.dma_start(O["rst"], RST[:]).then_inc(S["rst_out"], 16)
        act.dma_start(O["hst"], HST[:]).then_inc(S["rst_out"], 16)
        with act.Fori(0, RT) as k:
            act.activation(YH[:, k, :], YG[:, k, :], ACT.Copy).then_inc(S["y_hi"], 1)
        act.wait_ge(S["rst_out"], 32)
        act.dma_start(X[:], I["xT"].rearrange("k p t -> p k t")).then_inc(S["x_back"], 16)
        for s in range(2):
            ready[s].next(KT // 2)

        act_rdy = Count(S["act_ready"])
        conv, prod, gelu = Count(S["f_conv"]), Count(S["f_prod"]), Count(S["f_gelu"])
        loads, stores = Count(S["ffn_in"]), Count(S["ffn_out"])

        def ffn(layer):
            def chunk(n, c):
                act.wait_ge(act_rdy.sem, act_rdy.next())
                for s in range(2):
                    got(s)
                    o = SLOT[s]
                    fu = FU[:, s, 2 + SEQ:WF].rearrange("p (b t) -> p b t", b=NB)
                    act.activation(FU[:, s, 2:2 + SEQ], PS[:, o:o + SEQ], ACT.Copy)
                    act.activation(fu[:, :, 2:2 + TD], req(PS[:, o + SEQ:o + T]), ACT.Copy)
                    act.activation(fu[:, :, 0:2], FHALO[:, n + FT * s, :].rearrange("p (b t) -> p b t", b=NB), ACT.Copy)
                    act.activation(FC[:, s, :], PS[:, o:o + T], ACT.Identity, scale=FCW[:, n + FT * s, 2:3],
                                   bias=FCW[:, n + FT * s, 3:4]).then_inc(free[s], 1)
                act.wait_ge(conv.sem, conv.next())
                act.activation(FC[:, 0, :], FC[:, 0, :], ACT.Gelu_apprx_tanh).then_inc(S["f_gelu"], 1)
                act.wait_ge(prod.sem, prod.next())
                act.activation(AH[:, c, :], FC[:, 0, :], ACT.Copy).then_inc(S["f_hi"], 1)

            def down():
                for s in range(2):
                    ready[s].next(KT // 2)
            act.dma_start(FHALO[:], I["ffn_halo"][layer]).then_inc(S["ffn_in"], 16)
            act.dma_start(FCW[:], I["ffn_par"][layer]).then_inc(S["ffn_in"], 16)
            norm(1 if layer == 0 else 4)
            act.wait_ge(loads.sem, loads.next(32))
            ones = {ready[0]: 1, ready[1]: 1, act_rdy: 1, conv: 1, prod: 1}
            with rounds(act, GC, ones) as c:
                chunk(c, c)
            with rounds(act, NG - 1, {ready[0]: 8, ready[1]: 8, act_rdy: GC, conv: GC, prod: GC}) as g:
                chunk(g * GC + GC, 0)
                down()
                with rounds(act, GC - 1, ones) as c:
                    chunk(g * GC + c + (GC + 1), c + 1)
            down()
            act.wait_ge(x_done.sem, x_done.next(NG * KT))
            act.dma_start(O["fst"][layer], FST[:]).then_inc(S["ffn_out"], 16)
            act.wait_ge(stores.sem, stores.next(16))

        act.wait_ge(x_done.sem, x_done.next(KT))
        ffn(0)
        norm(2)
        ready[0].next()
        act.wait_ge(free[0], ready[0].now() + 1)
        chain(act.activation(LA[:], LZ[:], ACT.Abs))
        chain(act.activation(LE[:], LA[:], ACT.Exp, scale=-1.0))
        act.activation(LE[:], LE[:], ACT.Ln, bias=ONES[0:NH, 0:1]).then_inc(S["lf_e"], 1)
        act.wait_ge(S["lf_ready"], 1)
        act.dma_start(O["lf"], LF[:]).then_inc(S["lf_out"], 16)
        out = [Count(S[f"kv_out{n}"]) for n in range(4)]
        per = {ready[0]: 2, ready[1]: 2, me: 4} | {o: 16 for o in out}
        with rounds(act, KV_ROUNDS, per) as i:
            for n in range(4):
                s = n % 2
                got(s)
                act.wait_ge(out[n].sem, out[n].next(16))
                act.activation(STG[:, n, :], PS[:, SLOT[s]:SLOT[s] + T], ACT.Copy).then_inc(me.sem, 1)
                act.wait_ge(me.sem, me.next())
                act.sem_inc(free[s], 1)
                act.dma_start(O["kv"][i * 4 + n], STG[:, n, :]).then_inc(out[n].sem, 16)
        for n in range(4):
            act.wait_ge(out[n].sem, out[n].next(16))
        act.wait_ge(S["lf_out"], 16)
        norm(3, sums=False)
        act.wait_ge(S["dve_lo"], 4 * KT + 1)
        with rounds(act, KT // 2, {ready[0]: 1, ready[1]: 1}) as i:
            for s in range(2):
                got(s)
                act.activation(Q[:, i * 2 + s, :], PS[:, SLOT[s]:SLOT[s] + T], ACT.Copy,
                               scale=float(HD) ** -0.5).then_inc(free[s], 1)
        act.drain().then_inc(S["q_ready"], 2)

        STEPS = 2 * KT
        stt, ptp, ops = Count(S["stt_done"]), Count(S["pt_psum"]), Count(S["o_psum"])
        freeq = Count(S["pair_done"], 1)
        with rounds(act, KT, {stt: STEPS, ptp: STEPS, ops: STEPS, freeq: 1}) as pair:
            act.wait_ge(freeq.sem, freeq.next())
            act.activation(QS[:], Q[:, pair, 0:SEQ], ACT.Copy).then_inc(S["qs_ready"], 1)
            for t in range(STEPS + 2):
                if t < STEPS:
                    L = (t % KT + 1) * P
                    act.wait_ge(stt.sem, stt.next())
                    act.activation(SBUFS[t % 4][:, 0:L], SBUFS[t % 4][:, 0:L], ACT.Exp, bias=NM[:, t % 4:t % 4 + 1],
                                   accum_out=SUM[:, t % 4:t % 4 + 1]).then_inc(S["exp_done"], 1)
                if t >= 2:
                    u = t - 2
                    L = (u % KT + 1) * P
                    act.wait_ge(ptp.sem, ptp.next())
                    if u >= 2:
                        act.wait_ge(ops.sem, ops.next())
                    act.activation(PT[:, u % 2, 0:L], PS[:, 2048:2048 + L], ACT.Copy).then_inc(S["pt_ready"], 1)
            ops.next(2)

        act.wait_ge(S["vn_psum"], 1)
        act.activation(VN[:], PS[0:TS, 2048:2048 + D], ACT.Copy).then_inc(S["vn_ready"], 1)
        nm, scp = Count(S["sc_nm"]), Count(S["sc_ptp"])
        with rounds(act, NB, {nm: 1, scp: 1}):
            act.wait_ge(nm.sem, nm.next())
            act.activation(SS[:], SS[:], ACT.Exp, bias=NM[:, 0:1], accum_out=SUM[:, 0:1]).then_inc(S["sc_exp"], 1)
            act.wait_ge(scp.sem, scp.next())
            act.activation(PTS[:, 0:NPG, :].rearrange("p g q -> p (g q)"), PS[:, 2048:2048 + PAST], ACT.Copy)
            act.activation(PTS[0:TS, NPG, :], PS[0:TS, 2560:2560 + P], ACT.Copy).then_inc(S["sc_pt"], 1)
        act.wait_ge(S["sc_done"], NB)
        with act.Fori(0, KT) as k:
            act.activation(OH[:, k, :], OT[:, k, :], ACT.Copy).then_inc(S["o_hi"], 1)
        for s in range(2):
            ready[s].next(KT // 2)
        act.wait_ge(S["o_ready"], KT)
        act.wait_ge(x_done.sem, x_done.next(KT))
        ffn(1)
        norm(5)
        hi, yo = Count(S["act_hi"], 5 * KT), [Count(S["y_out0"]), Count(S["y_out1"])]
        for u in range(2):
            act.sem_inc(yo[u].sem, 16)
        with rounds(act, KT // 2, {tn: 2, hi: 2, yo[0]: 16, yo[1]: 16}) as i:
            for u in range(2):
                act.wait_ge(tn.sem, tn.next())
                act.wait_ge(yo[u].sem, yo[u].next(16))
                act.activation(YO[:, u, :], TN[:, u, :], ACT.Copy, scale=NGAIN[:, 5, bass.ds(i * 2 + u, 1)])\
                   .then_inc(hi.sem, 1)
                act.wait_ge(hi.sem, hi.next())
                act.dma_start(O["yT"][i * 2 + u], YO[:, u, :]).then_inc(yo[u].sem, 16)
        for u in range(2):
            act.wait_ge(yo[u].sem, yo[u].next(16))

    @block.vector
    def _(dve):
        ready, free = [Count(S["ready0"]), Count(S["ready1"])], [S["free0"], S["free1"]]
        sq, root, hi = Count(S["act_sq"]), Count(S["act_root"]), Count(S["act_hi"])
        accs, los = Count(S["dve_acc"], 2), Count(S["dve_lo"], 1)
        me = Count(S["dve_self"])
        TT, TSC, STT = dve.tensor_tensor, dve.tensor_scalar, dve.scalar_tensor_tensor

        def chain(ins):
            ins.then_inc(me.sem, 1)
            dve.wait_ge(me.sem, me.next())

        def got(s):
            dve.wait_ge(ready[s].sem, ready[s].next())

        def norm(n, sums=True):
            if sums:
                chain(dve.memset(ACC[:], 0.0))
                with rounds(dve, KT // 2, {sq: 2, accs: 2}):
                    for u in range(2):
                        dve.wait_ge(sq.sem, sq.next())
                        TT(ACC[:], ACC[:], SQ[:, u, :], ALU.add).then_inc(accs.sem, 1)
                        dve.wait_ge(accs.sem, accs.next())
                got(0)
                TSC(ACC[:], PS[:, 0:T], 1.0 / D, EPS, ALU.mult, ALU.add).then_inc(S["dve_var"], 1)
                var.next()
                dve.wait_ge(var.sem, var.now())
                dve.sem_inc(free[0], 1)
                dve.wait_ge(root.sem, root.next())
                chain(dve.reciprocal(RS[:], RS[:]))
                chain(TT(NT[:], ACC[:], RS[:], ALU.mult))
                chain(TT(NT[:], NT[:], RS[:], ALU.mult))
                chain(TSC(NT[:], NT[:], -0.5, 1.5, ALU.mult, ALU.add))
                chain(TT(RS[:], RS[:], NT[:], ALU.mult))

            def tile(k, u, reused=True):
                if reused and NORMS[n]:
                    dve.wait_ge(los.sem, los.now())
                if not NORMS[n]:
                    TT(TN[:, u, :], X[:, k, :], RS[:], ALU.mult).then_inc(S["dve_tn"], 1)
                    return
                sh, sc = NORMS[n]
                chain(TT(TN[:, u, :], X[:, k, :], RS[:], ALU.mult))
                s = req(TN[:, u, SEQ:T])
                chain(TT(s, s, bc_t(MOD[:, sc + k, 1:NV]), ALU.mult))
                TT(s, s, bc_t(MOD[:, sh + k, 1:NV]), ALU.add).then_inc(S["dve_tn"], 1)

            def low(k, u):
                dve.wait_ge(hi.sem, hi.next())
                if NORMS[n]:
                    TT(HL[:, k, :], TN[:, u, :], HH[:, k, :].bitcast(F32), ALU.subtract).then_inc(los.sem, 1)
                    los.next()

            m = 2 if NORMS[n] else 0
            tile(0, 0, False)
            with rounds(dve, KT // 2 - 1, {me: 2 * m, hi: 2, los: m}) as i:
                tile(i * 2 + 1, 1)
                low(i * 2, 0)
                tile(i * 2 + 2, 0)
                low(i * 2 + 1, 1)
            tile(KT - 1, 1)
            low(KT - 2, 0)
            low(KT - 1, 1)

        def residual(s, k, gate):
            got(s)
            TT(req(XS[:, s, :]), req(PS[:, SLOT[s] + SEQ:SLOT[s] + T]), bc_t(MOD[:, gate + k, 1:NV]), ALU.mult)\
              .then_inc(me.sem, 1)
            STT(X[:, k, 0:SEQ], PS[:, SLOT[s]:SLOT[s] + SEQ], MOD[:, gate + k, 0:1], X[:, k, 0:SEQ],
                ALU.mult, ALU.add).then_inc(free[s], 1)
            dve.wait_ge(me.sem, me.next())
            TT(X[:, k, SEQ:T], X[:, k, SEQ:T], XS[:, s, :], ALU.add).then_inc(S["x_done"], 1)

        var = Count(S["dve_var"])
        dve.sem_inc(S["dve_acc"], 2)
        dve.sem_inc(S["dve_lo"], 1)
        dve.sem_inc(S["conv_free"], 1)
        dve.sem_inc(S["pair_free"], 1)
        dve.sem_inc(S["act_ready"], 1)
        dve.wait_ge(S["consts"], 16 * N_CONSTS)
        chain(dve.tensor_copy(IDB[:], ID[:]))
        chain(dve.tensor_copy(MSKB[:], CQ[:].rearrange("p q h -> p (q h)")))
        dve.wait_ge(S["sigmoid"], 1)
        TT(CT[:], CT[:], SG[:], ALU.mult).then_inc(S["silu"], 1)
        lam = RGP[:, :, 7]
        dve.wait_ge(S["lam_exp"], 1)
        e, z, z2, acc_ = SPT[:, 1, :], SPT[:, 2, :], SPT[:, 3, :], SPT[:, 0, :]
        chain(TSC(z, e, 2.0, None, ALU.add))
        chain(dve.reciprocal(z, z))
        chain(TT(z, z, e, ALU.mult))
        chain(TT(z2, z, z, ALU.mult))
        chain(dve.memset(acc_, 1.0 / 17))
        for n in (15, 13, 11, 9, 7, 5, 3, 1):
            chain(TT(acc_, acc_, z2, ALU.mult))
            chain(TSC(acc_, acc_, 1.0 / n, None, ALU.add))
        chain(TT(acc_, acc_, z, ALU.mult))
        chain(TSC(z, lam, -1.0, 0.0, ALU.mult, ALU.max))
        chain(TSC(acc_, acc_, 8.0, None, ALU.mult))
        STT(SP4[:], z, 4.0, acc_, ALU.mult, ALU.add).then_inc(S["sp_done"], 1)
        dve.wait_ge(S["mw_used"], MT // 2)
        for bank, (m0, m1) in enumerate(((0, 48), (48, 96), (96, MT))):
            ins = TT(MOD[:, m0:m1, :], PS[:, 512 * bank:512 * bank + (m1 - m0) * NV].rearrange("p (m v) -> p m v", v=NV),
                     MODB[:, m0:m1].unsqueeze(2).broadcast_to([P, m1 - m0, NV]), ALU.add)
        chain(ins)
        dve.sem_inc(free[0], 1)
        dve.sem_inc(free[1], 1)
        for n, pair in enumerate(NORMS[:5]):
            blk = MOD[:, pair[1]:pair[1] + KT, :]
            STT(blk, blk, 1.0, NGAIN[:, n, :].unsqueeze(2).broadcast_to([P, KT, NV]), ALU.add, ALU.mult)
        for layer in range(2):
            for chunk in (G1, G2):
                m = mod_at(layer, chunk)
                ins = TSC(MOD[:, m:m + KT, :], MOD[:, m:m + KT, :], 1.0, None, ALU.add)
        ins.then_inc(S["mods_done"], 1)
        dve.wait_ge(S["mods_done"], 1)
        dve.wait_ge(S["x_in"], 16)
        norm(0)

        dve.wait_ge(S["dve_lo"], KT + 1)
        chain(dve.memset(RU[:, 0:3], 0.0))
        dve.wait_ge(S["rg_halo"], 16)
        sqr = Count(S["act_sqrt"])
        for half in range(2):
            if half:
                dve.wait_ge(ready[1].sem, ready[1].now())
            with rounds(dve, RH, {ready[0]: 1, ready[1]: 1, me: 7}) as j:
                jt = j + RH * half
                ready[0].next(), ready[1].next()
                dve.wait_ge(free[0], ready[0].now() + 1)
                ru = RU[:, 3 + SEQ:WU].rearrange("p (b t) -> p b t", b=NB)
                xp, xs = XC[:, j, 0:SEQ], req(XC[:, j, SEQ:T])
                TSC(xp, RU[:, 0:SEQ], RGP[:, jt, 0:1], RGP[:, jt, 4:5], ALU.mult, ALU.add).then_inc(me.sem, 1)
                TSC(xs, ru[:, :, 0:TD], RGP[:, jt, 0:1], RGP[:, jt, 4:5], ALU.mult, ALU.add).then_inc(me.sem, 1)
                me.next(2)
                for k in (1, 2, 3):
                    dve.wait_ge(me.sem, me.now())
                    STT(xp, RU[:, k:k + SEQ], RGP[:, jt, k:k + 1], xp, ALU.mult, ALU.add).then_inc(me.sem, 1)
                    STT(xs, ru[:, :, k:k + TD], RGP[:, jt, k:k + 1], xs, ALU.mult, ALU.add)\
                        .then_inc(me.sem if k < 3 else S["xc_ready"], 1)
                    me.next(2 if k < 3 else 1)
                dve.tensor_copy(RST[:, jt, 0:3], RU[:, SEQ:SEQ + 3])
                dve.tensor_copy(RST[:, jt, 3:3 * NV].rearrange("p (b t) -> p b t", b=NB), ru[:, :, TD:TD + 3])\
                   .then_inc(S["conv_free"], 1)
            for j in range(RH):
                jt = RH * half + j
                ready[0].next(), ready[1].next()
                dve.wait_ge(sqr.sem, sqr.next())
                chain(TSC(RW1[:], RS1[:], 1.0, None, ALU.add))
                chain(dve.reciprocal(RW1[:], RW1[:]))
                TSC(RA1[:], RW1[:], 2.0, -1.0, ALU.mult, ALU.add).then_inc(me.sem, 1)
                TT(RI1[:], RI1[:], XC[:, j, :], ALU.mult).then_inc(me.sem, 1)
                STT(RQ1[:], RQ1[:], 2.0, RW1[:], ALU.mult, ALU.mult).then_inc(me.sem, 1)
                dve.wait_ge(me.sem, me.next(3))
                chain(TT(RI1[:], RI1[:], RQ1[:], ALU.mult))
                a0, b0 = req(RA1[:, SEQ:T])[:, :, 0], req(RI1[:, SEQ:T])[:, :, 0]
                chain(TT(RW1[:, 0:NB], a0, H0[:, jt, :], ALU.mult))
                TT(b0, b0, RW1[:, 0:NB], ALU.add).then_inc(me.sem, 1)
                dve.memset(a0, 0.0).then_inc(me.sem, 1)
                dve.wait_ge(me.sem, me.next(2))
                chain(dve.tensor_tensor_scan(RQ1[:], RA1[:], RI1[:], 0.0, ALU.mult, ALU.add))
                dve.tensor_copy(HST[:, jt, 0:1], RQ1[:, SEQ - 1:SEQ])
                dve.tensor_copy(HST[:, jt, 1:NV], req(RQ1[:, SEQ:T])[:, :, TD - 1])
                TT(YG[:, jt, :], YG[:, jt, :], RQ1[:], ALU.mult).then_inc(S["pair_free"], 1)
        yhi = Count(S["y_hi"])
        with rounds(dve, RT, {yhi: 1}) as k:
            dve.wait_ge(yhi.sem, yhi.next())
            TT(YL[:, k, :], YG[:, k, :], YH[:, k, :].bitcast(F32), ALU.subtract).then_inc(S["y_ready"], 1)
        dve.wait_ge(S["x_back"], 16)

        def residuals(gate):
            with rounds(dve, KT // 2, {ready[0]: 1, ready[1]: 1, me: 2}) as i:
                for s in range(2):
                    residual(s, i * 2 + s, gate)

        residuals(mod_at(0, G1))
        xdone = Count(S["x_done"])
        dve.wait_ge(xdone.sem, xdone.next(KT))

        gel, fhi, loads = Count(S["f_gelu"]), Count(S["f_hi"]), Count(S["ffn_in"])

        def ffn(layer):
            gate = mod_at(layer, G2)
            norm(1 if layer == 0 else 4)
            dve.wait_ge(S["dve_lo"], KT * (2 if layer == 0 else 5) + 1)
            chain(dve.memset(FU[:, :, 0:2], 0.0))
            dve.wait_ge(loads.sem, loads.next(32))

            def taps(n):
                for s in range(2):
                    got(s)
                    dve.wait_ge(free[s], ready[s].now() + 1)
                    idx = n + FT * s
                    fu = FU[:, s, 2 + SEQ:WF].rearrange("p (b t) -> p b t", b=NB)
                    STT(FC[:, s, 0:SEQ], FU[:, s, 1:1 + SEQ], FCW[:, idx, 1:2], FC[:, s, 0:SEQ], ALU.mult, ALU.add)\
                        .then_inc(me.sem, 1)
                    STT(req(FC[:, s, SEQ:T]), fu[:, :, 1:1 + TD], FCW[:, idx, 1:2], req(FC[:, s, SEQ:T]),
                        ALU.mult, ALU.add).then_inc(me.sem, 1)
                    me.next(2)
                    dve.tensor_copy(FST[:, idx, 0:2], FU[:, s, SEQ:SEQ + 2])
                    dve.tensor_copy(FST[:, idx, 2:2 * NV].rearrange("p (b t) -> p b t", b=NB), fu[:, :, TD:TD + 2])
                    dve.wait_ge(me.sem, me.now())
                    STT(FC[:, s, 0:SEQ], FU[:, s, 0:SEQ], FCW[:, idx, 0:1], FC[:, s, 0:SEQ], ALU.mult, ALU.add)
                    STT(req(FC[:, s, SEQ:T]), fu[:, :, 0:TD], FCW[:, idx, 0:1], req(FC[:, s, SEQ:T]),
                        ALU.mult, ALU.add).then_inc(S["f_conv"] if s == 0 else me.sem, 1)
                me.next()

            def finish(c):
                dve.wait_ge(gel.sem, gel.next())
                dve.wait_ge(me.sem, me.now())
                TT(FC[:, 0, :], FC[:, 0, :], FC[:, 1, :], ALU.mult).then_inc(S["f_prod"], 1)
                dve.wait_ge(fhi.sem, fhi.next())
                TT(AL[:, c, :], FC[:, 0, :], AH[:, c, :].bitcast(F32), ALU.subtract).then_inc(S["act_ready"], 1)

            def down():
                residuals(gate)

            ones = {ready[0]: 1, ready[1]: 1, me: 5, gel: 1, fhi: 1}
            with rounds(dve, GC, ones) as c:
                taps(c)
                finish(c)
            with rounds(dve, NG - 1, {ready[0]: 8, ready[1]: 8, me: GC * 5 + KT,
                                      gel: GC, fhi: GC}) as g:
                taps(g * GC + GC)
                kept = me.now()
                down()
                finish(0)
                with rounds(dve, GC - 1, ones) as c:
                    taps(g * GC + c + (GC + 1))
                    finish(c + 1)
            down()
            dve.wait_ge(xdone.sem, xdone.next(NG * KT))

        ffn(0)
        norm(2)
        got(0)
        dve.wait_ge(S["dve_lo"], 3 * KT + 1)
        TSC(LZ[:], PS[0:NH, 0:T], KVB[:], None, ALU.add).then_inc(free[0], 1)
        dve.wait_ge(free[0], ready[0].now() + 1)
        dve.wait_ge(S["lf_e"], 1)
        STT(LF[:], LZ[:], 0.0, LE[:], ALU.min, ALU.subtract).then_inc(S["lf_ready"], 1)
        dve.wait_ge(S["lf_ready"], 1)
        dve.tensor_tensor_scan(CUM[:], ONES[0:NH, 0:1].broadcast_to([NH, SEQ]), LF[:, 0:SEQ], 0.0,
                               ALU.mult, ALU.add).then_inc(S["lf_ready"], 1)
        for s in range(2):
            ready[s].next(KT)
        for n in range(4):
            dve.wait_ge(S[f"kv_out{n}"], KV_ROUNDS * 16 + 16)
        dve.wait_ge(S["lf_out"], 16)
        norm(3, sums=False)
        for s in range(2):
            ready[s].next(KT // 2)

        dve.wait_ge(S["q_ready"], 2)
        dve.wait_ge(S["cq_psum"], 1)
        dve.tensor_copy(CQ[:], PS[:, 0:KT * NH].rearrange("p (q h) -> p q h", h=NH)).then_inc(S["cq_done"], 1)
        dve.wait_ge(S["cq_done"], 1)
        for n in (0, 1):
            dve.sem_inc(S[f"s_free{n}"], 1)
        dve.sem_inc(S["o_free"], 2)
        dve.sem_inc(S["pair_done"], 2)
        STEPS = 2 * KT
        srd, ex, ops = Count(S["s_ready"]), Count(S["exp_done"]), Count(S["o_psum"])
        with rounds(dve, KT, {srd: STEPS + 4, ex: STEPS, ops: STEPS, me: 2 * STEPS + 2}) as pair:
            sj = 0

            def s_job():
                nonlocal sj
                dve.wait_ge(srd.sem, srd.next())
                sj += 1
                return 1024 * ((sj - 1) % 2), S[f"s_free{(sj - 1) % 2}"]

            def head_logs(e):
                TSC(CUMH[:], CUM[:], ID[0:NH, bass.ds(pair * 2 + e, 1)], -1.0, ALU.mult, ALU.mult)\
                   .then_inc(S["cumh"], 1)

            head_logs(0)
            for hv in range(2):
                o, fr = s_job()
                dve.tensor_copy(V[:, hv * 4:hv * 4 + 4, :].rearrange("p k c -> p (k c)"), PS[:, o:o + 512]).then_inc(fr, 1)
            for t in range(STEPS + 3):
                if t < STEPS:
                    e, qi = divmod(t, KT)
                    L = (qi + 1) * P
                    if qi == 0:
                        o, fr = s_job()
                        chain(dve.tensor_copy(NBC[:, e, :], PS[:, o:o + SEQ]))
                        dve.sem_inc(fr, 1)
                    if t == 1:
                        head_logs(1)
                    o, fr = s_job()
                    sb_ = SBUFS[t % 4][:, 0:L]
                    STT(sb_, NBC[:, e, 0:L], CQ[:, qi, bass.ds(pair * 2 + e, 1)], PS[:, o:o + L], ALU.add, ALU.add)\
                        .then_inc(me.sem, 1)
                    dve.wait_ge(me.sem, me.next())
                    dve.sem_inc(fr, 1)
                    dve.tensor_reduce(NM[:, t % 4:t % 4 + 1], sb_, AX_X, ALU.max, negate=True).then_inc(S["stt_done"], 1)
                if 1 <= t < STEPS + 1:
                    u = t - 1
                    L = (u % KT + 1) * P
                    dve.wait_ge(ex.sem, ex.next())
                    chain(dve.reciprocal(RI[:, u % 4:u % 4 + 1], SUM[:, u % 4:u % 4 + 1]))
                    sb_ = SBUFS[u % 4][:, 0:L]
                    TSC(sb_, sb_, RI[:, u % 4:u % 4 + 1], None, ALU.mult).then_inc(S["p_ready"], 1)
                if t >= 3:
                    u = t - 3
                    e, qi = divmod(u, KT)
                    rows = slice(HD * e, HD * e + HD)
                    dve.wait_ge(ops.sem, ops.next())
                    dve.tensor_copy(OT[rows, pair, qi * P:(qi + 1) * P],
                                    PS[rows, 3072 + 512 * (u % 2):3072 + 512 * (u % 2) + P]).then_inc(S["o_free"], 1)
            dve.sem_inc(S["pair_done"], 1)

        chain(dve.memset(QX[:], 0.0))
        dve.wait_ge(S["lfp_in"], NB * NPG * 16)
        dve.wait_ge(S["lfn_in"], NB * 16)
        chain(dve.tensor_tensor_scan(CUMS[:, 0:PAST], ONES[:, 0:1].broadcast_to([P, PAST]), LFP[:], 0.0, ALU.mult, ALU.add))
        dve.sem_inc(S["kb_used"], 2)
        chain(dve.tensor_tensor_scan(CN[:], ONES[:, 0:TD], LFN[:], CUMS[:, PAST - 1:PAST], ALU.mult, ALU.add))
        chain(dve.tensor_copy(req(CUMS[:, PAST:PAST + TS]), CN[:].unsqueeze(1).broadcast_to([P, NB, TD])))
        TT(CNM[:], CN[:].unsqueeze(1).broadcast_to([P, NB, TD]), bc_t(BM[:]), ALU.mult).then_inc(S["cumm_ready"], 1)
        dve.wait_ge(S["cq_psum"], 2)
        chain(TT(CQT[:], req(PS[:, 0:TS]), MQ[:].unsqueeze(1).broadcast_to([P, NB, TD]), ALU.mult))
        dve.tensor_reduce(CQS[:], CQT[:], AX_X, ALU.add).then_inc(S["cq_done"], 1)
        dve.wait_ge(S["cq_done"], 2)
        dve.wait_ge(S["sconst"], 16)
        scps, scex, sco = Count(S["sc_psum"]), Count(S["sc_exp"]), Count(S["sc_o"])
        with rounds(dve, NB // 2, {scps: 2, scex: 2, sco: 2, me: 6}) as i:
            for e in range(2):
                k = i * 2 + e
                for hv in range(2):
                    rows = slice(HD * hv, HD * hv + HD)
                    dve.tensor_copy(QX[rows, :].rearrange("p (k x) -> p k x", x=P + 16)[:, :, 8 * hv:8 * hv + 8],
                                    Q[rows, :, bass.ds(k * TD + SEQ, TD)])
                TSC(CUMM[:], CUMS[:], BM[:, bass.ds(k, 1)], None, ALU.mult).then_inc(S["qx_ready"], 1)
                dve.wait_ge(scps.sem, scps.next())
                chain(TSC(SS[:], PS[:, 1024 * e:1024 * e + PAST + TS], CQS[:, bass.ds(k, 1)], None, ALU.add))
                chain(TT(SS[:, PAST:PAST + TS], SS[:, PAST:PAST + TS], MKS[:, k, :], ALU.add))
                dve.tensor_reduce(NM[:, 0:1], SS[:], AX_X, ALU.max, negate=True).then_inc(S["sc_nm"], 1)
                dve.wait_ge(scex.sem, scex.next())
                chain(dve.reciprocal(RI[:, 0:1], SUM[:, 0:1]))
                TSC(SS[:], SS[:], RI[:, 0:1], None, ALU.mult).then_inc(S["sc_p"], 1)
                dve.wait_ge(sco.sem, sco.next())
                for hv in range(2):
                    rows = slice(HD * hv, HD * hv + HD)
                    ins = dve.tensor_copy(OT[rows, :, bass.ds(k * TD + SEQ, TD)],
                                          PS[rows, 3072 + 512 * e:3072 + 512 * e + P]
                                          .rearrange("p (k x) -> p k x", x=16)[:, :, 8 * hv:8 * hv + 8])
                ins.then_inc(S["sc_done"], 1)
        ohi = Count(S["o_hi"])
        with rounds(dve, KT, {ohi: 1}) as k:
            dve.wait_ge(ohi.sem, ohi.next())
            TT(OL[:, k, :], OT[:, k, :], OH[:, k, :].bitcast(F32), ALU.subtract).then_inc(S["o_ready"], 1)
        residuals(mod_at(1, G1))
        dve.wait_ge(xdone.sem, xdone.next(KT))
        ffn(1)
        norm(5)


N_CONSTS = 11
_OUTS = {"yT": (KT, P, T), "kv": (2 * KT, P, T), "lf": (NH, T), "rst": (P, RT, 3 * NV), "hst": (P, RT, NV),
         "fst": (2, P, 2 * FT, 2 * NV)}


def _layouts(d):
    import numpy as np
    f = np.float32
    a = {k: np.asarray(v) for k, v in d.items()}

    def cols(w, c0, c1, r0=0, r1=None):
        w = w[r0:r1, c0:c1]
        return w.reshape(-1, P, c1 - c0).transpose(1, 0, 2)

    def unit(*parts):
        u = np.concatenate([p.reshape(P, -1) for p in parts], 1)
        out = np.zeros((P, UNIT), f)
        out[:, :u.shape[1]] = u
        return out

    units = []
    w_in, w_out = a["rg_w_in"][0], a["rg_w_out"][0]
    for j in range(RT):
        units += [unit(cols(w_in, D_RNN + P * j, D_RNN + P * j + P)), unit(cols(w_in, P * j, P * j + P))]
    for o in range(KT):
        units += [unit(cols(w_out, P * o, P * o + P, 5 * P * h, 5 * P * h + 5 * P)) for h in range(2)]

    def ffn(l):
        up, dn = a["ffn_w_up"][l], a["ffn_w_down"][l]

        def pair(n):
            return [unit(cols(up, P * n, P * n + P)), unit(cols(up, D_FF + P * n, D_FF + P * n + P))]

        def down(g):
            r0 = g * GC * P
            return [unit(*(cols(dn, P * o, P * o + P, r0, r0 + GC * P) for o in (2 * v, 2 * v + 1))) for v in range(4)]
        out = []
        for g in range(NG):
            out += pair(GC * g)
            if g:
                out += down(g - 1)
            for c in range(1, GC):
                out += pair(GC * g + c)
        return out + down(NG - 1)

    units += ffn(0)
    kvw = a["kv_w"]
    units += [unit(np.pad(cols(kvw, 2 * D, 2 * D + NH), ((0, 0), (0, 0), (0, P - NH)))), np.zeros((P, UNIT), f)]
    units += [unit(cols(kvw, P * j, P * j + P)) for j in range(2 * KT)]
    units += [unit(cols(a["fa_wq"][0], P * j, P * j + P)) for j in range(KT)]
    units += [unit(cols(a["fa_wo"][0], P * j, P * j + P)) for j in range(KT)]
    units += ffn(1)
    assert len(units) == UNITS_1 + UNITS_2

    mw = np.concatenate([a["mod_w"][0], a["mod_w"][1], a["kv_mod_w"]], 1)
    mb = np.concatenate([a["mod_b"][0], a["mod_b"][1], a["kv_mod_b"]])
    chan = lambda v: v.reshape(-1, P).T
    x = np.concatenate([a["x_prompt"][0], a["x_sample"].reshape(TS, D)])
    c = np.concatenate([a["c_prompt"], a["c_sample"]])
    gates = np.zeros((RT, P, 2, 3, P), f)
    for u, w in enumerate((a["rg_wa"][0], a["rg_wx"][0])):
        full = np.zeros((D_RNN, D_RNN), f)
        for h in range(16):
            full[RG_W * h:RG_W * h + RG_W, RG_W * h:RG_W * h + RG_W] = w[h]
        for j in range(RT):
            for n, k in enumerate(GATE_IN[j]):
                gates[j, :, u, n] = full[P * k:P * k + P, P * j:P * j + P]
    par = np.stack([chan(v) for v in (*a["rg_conv_w"][0], a["rg_conv_b"][0], a["rg_ba"][0], a["rg_bx"][0],
                                      a["rg_lambda"][0])], 2)
    hs = np.arange(P)
    q = np.arange(P)
    pick = -((hs[:, None] % NH) == (hs[None, :] // TD)).astype(f)
    mask_new = np.full((P, NB, NB, TD), NEG, f)
    for b in range(NB):
        mask_new[:, b, b, :] = np.where(np.arange(TD)[None, :] <= (hs % TD)[:, None], 0.0, NEG)
    return {
        "wstream": np.stack(units),
        "mod_w": mw.reshape(KT, P, MT // 2, 2, P).transpose(2, 1, 3, 0, 4).reshape(MT // 2, P, 2, UNIT),
        "mod_b": chan(mb),
        "cT": c.reshape(NV, KT, P).transpose(2, 1, 0),
        "gains": np.stack([chan(v) for v in (a["norm_mix_g"][0], a["norm_ffn_g"][0], a["kv_norm_g"],
                                             a["norm_mix_g"][1], a["norm_ffn_g"][1], a["final_norm_g"])], 1),
        "xT": x.T.reshape(KT, P, T),
        "rg_par": par,
        "rg_h0": a["state_rglru_h"][0].reshape(NB, RT, P).transpose(2, 1, 0),
        "rg_halo": a["state_rglru_conv"][0].reshape(NB, 3, RT, P).transpose(3, 2, 0, 1).reshape(P, RT, NB * 3),
        "rg_gate_w": gates,
        "ffn_halo": a["state_ffn_conv"].reshape(2, NB, 2, 2 * FT, P).transpose(0, 4, 3, 1, 2).reshape(2, P, 2 * FT, NB * 2),
        "ffn_par": np.concatenate([a["ffn_conv_w"].reshape(2, 3, 2 * FT, P).transpose(0, 3, 2, 1),
                                   a["ffn_conv_b"].reshape(2, 1, 2 * FT, P).transpose(0, 3, 2, 1)], 3),
        "kv_b": a["kv_b_f"].reshape(NH, 1),
        "cache_k": a["cache_k"].reshape(-1, PAGE, KT, P).transpose(0, 3, 2, 1),
        "cache_v": a["cache_v"].reshape(-1, PAGE, D),
        "cache_lf": a["cache_logf"].transpose(0, 2, 1),
        "page_table": a["page_table"].reshape(1, NB * NPG),
        "ident": np.eye(P, dtype=f),
        "mask": np.where(q[None, :] <= q[:, None], 0.0, NEG).astype(f).reshape(P, KT, NH),
        "pick_head": pick,
        "req_rows": ((hs[:, None] // NH) == np.arange(NB)[None, :]).astype(f),
        "pick_q": -((hs[:, None] % TD) == np.arange(TD)[None, :]).astype(f),
        "mask_new": mask_new.reshape(P, NB, TS),
    }


def kernel(**inputs):
    import numpy as np
    import concourse.bacc as bacc
    from concourse.bass_utils import run_bass_kernel_spmd

    nc = bacc.Bacc("TRN2", target_bir_lowering=False, num_devices=1)
    arrays, ins, outs = {}, {}, {}
    for name, v in _layouts(inputs).items():
        arrays[f"in_{name}"] = np.ascontiguousarray(v)
        ins[name] = nc.dram_tensor(f"in_{name}", v.shape, mybir.dt.from_np(v.dtype), kind="ExternalInput").ap()
    for name, shape in _OUTS.items():
        outs[name] = nc.dram_tensor(f"out_{name}", shape, F32, kind="ExternalOutput").ap()
    trunk(nc, ins, outs)
    res = run_bass_kernel_spmd(nc, [arrays], core_ids=[0]).results[0]
    g = {n: res[f"out_{n}"] for n in _OUTS}

    y = g["yT"].reshape(D, T).T
    kv = g["kv"].reshape(2, D, T).transpose(0, 2, 1).reshape(2, T, NH, HD)
    lf = g["lf"].T
    rst = g["rst"].transpose(2, 1, 0).reshape(NV, 3, D_RNN)
    hst = g["hst"].transpose(2, 1, 0).reshape(NV, D_RNN)
    fst = g["fst"].transpose(0, 3, 2, 1).reshape(2, NV, 2, 2 * D_FF)
    return (y[None, :SEQ], y[SEQ:].reshape(NB, TD, D),
            kv[0][None, :SEQ], kv[1][None, :SEQ], lf[None, :SEQ],
            rst[None, :1], hst[None, :1], fst[:, :1],
            kv[0][SEQ:].reshape(NB, TD, NH, HD), kv[1][SEQ:].reshape(NB, TD, NH, HD), lf[SEQ:].reshape(NB, TD, NH),
            rst[None, 1:], hst[None, 1:], fst[:, 1:])
```

```python
from contextlib import ExitStack, contextmanager

import concourse.bass as bass
from concourse import mybir

ALU = mybir.AluOpType
ACT = mybir.ActivationFunctionType
F32 = mybir.dt.float32
F32R = mybir.dt.float32r
BF16 = mybir.dt.bfloat16
AX_X = mybir.AxisListType.X

P = 128
D = 1024
KT = D // P
SEQ = 1024
NB, TD = 8, 8
TS = NB * TD
PAD = 2
S0 = SEQ + PAD
T = S0 + TS
PC = S0 // 3
NV = 1 + NB
D_RNN = 1280
RT = D_RNN // P
RH = RT // 2
D_FF = 3072
FT = D_FF // P
GC = 4
NG = FT // GC
NH, HD = 16, 64
PAGE, NPG = 128, 4
PAST = PAGE * NPG
EPS = 1e-6
NEG = -1e30
KV_ROUNDS = 2 * KT // 4
UNIT = KT * P
MB = 4

SH1, SC1, G1, SH2, SC2, G2 = range(6)
MT = 2 * 6 * KT + 2 * KT


def mod_at(layer, chunk):
    return (layer * 6 + chunk) * KT


KV_SH, KV_SC = 2 * 6 * KT, 2 * 6 * KT + KT
NORMS = [(mod_at(0, SH1), mod_at(0, SC1)), (mod_at(0, SH2), mod_at(0, SC2)), (KV_SH, KV_SC),
         (mod_at(1, SH1), mod_at(1, SC1)), (mod_at(1, SH2), mod_at(1, SC2)), None]

RG_W = D_RNN // 16
GATE_IN = []
for _j in range(RT):
    _b0, _b1 = (P * _j) // RG_W, (P * _j + P - 1) // RG_W
    GATE_IN.append(list(range(RG_W * _b0 // P, (RG_W * (_b1 + 1) - 1) // P + 1)))

U_RG, U_OUT, U_FFN, U_LF, U_D = 2 * RT, 2 * KT, 2 * FT + NG * GC, 2, KT
UNITS_1 = U_RG + U_OUT + U_FFN + U_LF + 3 * U_D
UNITS_2 = U_D + U_FFN
PIECES = ((0, PC), (PC, 2 * PC), (2 * PC, T))


class Count:

    def __init__(self, sem, n=0):
        self.sem, self.n, self.loop = sem, n, 0

    def next(self, k=1):
        self.n += k
        return self.n + self.loop

    def now(self):
        return self.n + self.loop


@contextmanager
def rounds(eng, trips, per):
    before = [(c, c.n, c.loop) for c in per]
    with eng.Fori(0, trips) as i:
        for c, k in per.items():
            c.loop = c.loop + i * k
        yield i
    for c, n, loop in before:
        assert c.n - n == per[c], (c.sem, c.n - n, per[c])
        c.n, c.loop = n + per[c] * trips, loop


def trunk(nc, I, O):
    ctx = ExitStack()
    B0 = 16512
    placed = []

    def at(name, off, shape, dt=F32):
        size = 4 if dt != BF16 else 2
        for s in shape[1:]:
            size *= s
        placed.append(off + size)
        assert off + size <= 212832, (name, off + size)
        return nc.alloc_sbuf_tensor_at(name, shape, dt, offset=B0 + off, align_bytes=4)

    class Area:
        def __init__(self, off, end):
            self.off, self.end = off, end

        def __call__(self, name, shape, dt=F32):
            t = at(name, self.off, shape, dt)
            self.off = (placed[-1] + 31) // 32 * 32
            assert placed[-1] <= self.end, (name, placed[-1], self.end)
            return t

    TB = T * 4
    O_X, O_HN, O_R3, O_W, O_C = 0, KT * TB, 3 * KT * TB, 3 * KT * TB + 65408, 3 * KT * TB + 65408 + 6 * UNIT * 4

    X = at("X", O_X, [P, KT, T])
    HH = at("HH", O_HN, [P, KT, T], F32R)
    HL = at("HL", O_HN + KT * TB, [P, KT, T], F32R)
    w = Area(O_W, O_C)
    WRAW = w("WRAW", [P, 2, UNIT])
    WH = w("WH", [P, 2, UNIT], F32R)
    WL = w("WL", [P, 2, UNIT], F32R)
    c = Area(O_C, 212832)
    MOD = c("MOD", [P, MT, NV])
    MODB = c("MODB", [P, MT])
    NGAIN = c("NGAIN", [P, 6, KT])
    RS_OFF = c.off
    RS = c("RS", [P, T])
    ID = c("ID", [P, P])
    ONES = c("ONES", [P, P])
    IDB = c("IDB", [P, P], BF16)
    MSKB = c("MSKB", [P, P], BF16)
    RGP = c("RGP", [P, RT, 8])
    SP4 = c("SP4", [P, RT])
    SPT = c("SPT", [P, 4, RT])
    H0 = c("H0", [P, RT, NB])
    KVB = c("KVB", [NH, 1])
    CT = c("CT", [P, KT, NV])
    SG = c("SG", [P, KT, NV])
    ZERO = c("ZERO", [P, 1])
    TINY = c("TINY", [P, 1])
    NM = c("NM", [P, 4])
    SUM = c("SUM", [P, 4])
    RI = c("RI", [P, 4])
    CQ_OFF = c.off
    CQ = c("CQ", [P, KT, NH])
    HST = at("HST", CQ_OFF, [P, RT, NV])
    EA = c("EA", [P, P])
    BM = c("BM", [P, NB])
    MQ = c("MQ", [P, TD])
    CQS = c("CQS", [P, NB])
    LFN = c("LFN", [P, TD])
    CN = c("CN", [P, TD])
    CNM = c("CNM", [P, NB, TD])
    CQT = c("CQT", [P, NB, TD])
    CUM_OFF = c.off
    CUM = c("CUM", [NH, SEQ])
    CUMM = at("CUMM", CUM_OFF, [P, PAST + TS])
    CUMS = at("CUMS", RS_OFF, [P, PAST + TS])
    MKS = at("MKS", RS_OFF + 4 * (PAST + TS), [P, NB, TS])

    n_ = Area(O_R3, O_W)
    TN = n_("TN", [P, 2, T])
    NT = n_("NT", [P, T])
    YO_OFF = n_.off
    YO = n_("YO", [P, 2, T])
    n_.off = O_R3 + 2 * GC * TB
    SQ = n_("SQ", [P, 2, T])
    ACC = n_("ACC", [P, T])
    MWB = n_("MWB", [P, 2, KT // 2, MB * P])
    n_.off = YO_OFF
    MROW = n_("MROW", [NV, 2, MB * P])
    MWA = n_("MWA", [P, 2, KT // 2, MB * P])
    assert placed[-1] <= O_R3 + 2 * GC * TB
    MW = [MWA[:, 0], MWA[:, 1], MWB[:, 0], MWB[:, 1]]

    r = Area(O_X, O_HN)
    WU = 3 + S0 + NB * (3 + TD)
    RU = r("RU", [P, WU])
    RS1 = r("RS1", [P, T])
    RI1 = r("RI1", [P, T])
    RW1 = r("RW1", [P, T])
    RQ1 = r("RQ1", [P, T])
    RA1 = r("RA1", [P, T])
    GW = r("GW", [P, 2, 2, 3, P])
    RHALO = r("RHALO", [P, RT, NB * 3])
    RST = r("RST", [P, RT, 3 * NV])
    XC = at("XC", O_R3, [P, RH, T])
    YG = at("YG", O_R3 + RH * TB, [P, RT, T])
    YH = at("YH", O_HN, [P, RT, T], F32R)
    YL = at("YL", O_HN + RT * TB, [P, RT, T], F32R)

    f = Area(O_R3, O_W)
    AH = f("AH", [P, GC, T], F32R)
    AL = f("AL", [P, GC, T], F32R)
    WF = 2 + S0 + NB * (2 + TD)
    FU = f("FU", [P, 2, WF])
    FC = f("FC", [P, 2, T])
    FHALO = f("FHALO", [P, 2 * FT, NB * 2])
    FST = f("FST", [P, 2 * FT, 2 * NV])
    FCW = f("FCW", [P, 2 * FT, 4])
    XS = f("XS", [P, 2, TS])

    kv = Area(O_R3, O_W)
    STG = kv("STG", [P, 4, T])
    LZ = kv("LZ", [NH, T])
    LA = kv("LA", [NH, T])
    LE = kv("LE", [NH, T])
    LF = kv("LF", [NH, T])
    Q = at("Q", O_R3, [P, KT, T])
    OT = at("OT", O_HN, [P, KT, T])
    a = Area(O_HN + KT * TB, O_R3)
    KP = a("KP", [P, 2, SEQ])
    VT = a("VT", [P, 2, SEQ])
    V = a("V", [P, KT, P])
    QS = a("QS", [P, SEQ])
    SB01 = a("SB01", [P, 2, SEQ])
    b = Area(O_R3 + KT * TB, O_W)
    PT = b("PT", [P, 2, SEQ])
    NBC = b("NBC", [P, 2, SEQ])
    SB23 = b("SB23", [P, 2, SEQ])
    CUMH = b("CUMH", [NH, SEQ])
    SBUFS = [SB01[:, 0, :], SB01[:, 1, :], SB23[:, 0, :], SB23[:, 1, :]]
    a = Area(O_HN + KT * TB, O_R3)
    KB = a("KB", [P, 2, NPG, KT, PAGE])
    KS = a("KS", [P, KT, TS])
    b = Area(O_R3 + KT * TB, O_W)
    VB = b("VB", [P, NPG, D])
    QX = b("QX", [P, 2, KT * (P + 16)])
    PTS = b("PTS", [P, NPG + 1, P])
    SS = [Q[:, e, 0:PAST + TS] for e in range(2)]
    VN = Q[0:TS, 2, 0:D]
    CUMX = [CUMM[:], Q[:, 3, 0:PAST + TS]]
    LFP = at("LFP", O_HN + KT * TB, [P, PAST])
    OH = at("OH", O_HN + KT * TB, [P, KT, T], F32R)
    OL = at("OL", O_R3, [P, KT, T], F32R)

    PS = ctx.enter_context(nc.psum_tensor("PS", [P, 8 * 512], F32))
    SLOT = (0, 1536)

    names = """w_raw0 w_raw1 pool_hi split_done unit_used ready0 ready1 free0 free1
        mw0 mw1 mw2 mw3 mw_used consts filled sigmoid silu mods_psum mods_row mods_turned mods_tile mods_done lam_exp sp_done x_in
        act_sq dve_acc dve_var act_root act_hi dve_tn dve_lo act_self dve_self
        rg_halo gate_w0 gate_w1 conv_free xc_ready act_tanh act_sqrt pair_free
        y_hi y_ready x_done x_back rst_out ffn_in ffn_out f_conv f_gelu f_prod f_hi act_ready
        kv_out0 kv_out1 kv_out2 kv_out3 lf_e lf_ready lf_out q_ready
        kv_in0 kv_in1 qs_ready cumh s_ready s_free0 s_free1 stt_done exp_done p_ready pt_psum pt_ready
        o_psum o_free pair_done cq_psum cq_done
        lfp_in lfn_in kb_in0 kb_in1 vb_in kb_used vb_used ks_in vst_in vn_psum vn_ready qx_ready cumm_ready
        sc_psum sc_nm sc_exp sc_p sc_ptp sc_pt sc_o sc_done sconst o_hi o_ready y_out0 y_out1""".split()
    S = {n: ctx.enter_context(nc.semaphore(n)) for n in names}

    def bc_t(ap):
        return ap.unsqueeze(2).broadcast_to([ap.shape[0], NB, TD])

    def req(ap):
        return ap.rearrange("p (b t) -> p b t", b=NB)

    def three(ap):
        return ap.rearrange("p (b x) -> p b x", b=3)

    def prompt(slot, rows=P):
        return three(PS[0:rows, SLOT[slot]:SLOT[slot] + 1536])[:, :, 0:PC]

    def sample(slot, rows=P):
        o = SLOT[slot] + 1024 + PC
        return PS[0:rows, o:o + TS]

    block = ctx.enter_context(nc.Block())

    @block.sync
    def _(sp):
        def weights(first, units, peel):
            k = 0
            if peel:
                for u in range(2):
                    sp.dma_start(WRAW[:, u, :], I["wstream"][u]).then_inc(S[f"w_raw{u}"], 16)
                k = 1
            with sp.Fori(k, units // 2) as i:
                for u in range(2):
                    sp.wait_ge(S["split_done"], first + i * 2 + u - 1)
                    sp.dma_start(WRAW[:, u, :], I["wstream"][i * 2 + first + u]).then_inc(S[f"w_raw{u}"], 16)

        for dst, src in ((CT, "cT"), (MODB, "mod_b"), (NGAIN, "gains"), (ID, "ident"), (CQ, "mask"), (RGP, "rg_par"), (H0, "rg_h0"), (KVB, "kv_b"), (EA, "pick_head"),
                         (BM, "req_rows"), (MQ, "pick_q")):
            sp.dma_start(dst[:], I[src]).then_inc(S["consts"], 16)
        sp.dma_start(X[:], I["xT"].rearrange("k p t -> p k t")).then_inc(S["x_in"], 16)
        for v in range(4):
            sp.dma_start(MW[v], I["mod_w"][v]).then_inc(S[f"mw{v}"], 16)
        with sp.Fori(1, MT // (2 * MB)) as i:
            for v in range(4):
                sp.wait_ge(S["mods_psum" if v % 2 else "mw_used"], i * 2 + (v // 2 - 1))
                sp.dma_start(MW[v], I["mod_w"][i * 4 + v]).then_inc(S[f"mw{v}"], 16)
        weights(0, UNITS_1, True)

        for n in range(4):
            sp.wait_ge(S[f"kv_out{n}"], KV_ROUNDS * 16 + 16)
        sp.wait_ge(S["q_ready"], 2)
        with sp.Fori(0, KT // 2) as i:
            for e in range(2):
                sp.wait_ge(S["pair_done"], i * 2 + (e + 1))
                sp.dma_start(KP[:, e, :], O["kv"][i * 2 + e, :, 0:SEQ]).then_inc(S[f"kv_in{e}"], 16)
                sp.dma_start(VT[:, e, :], O["kv"][i * 2 + (KT + e), :, 0:SEQ]).then_inc(S[f"kv_in{e}"], 16)

        sp.wait_ge(S["pair_done"], KT + 2)
        sp.wait_ge(S["lf_out"], 16)
        for k in range(NB):
            sp.dma_start(LFN[16 * k:16 * k + 16, :], O["lf"][:, S0 + TD * k:S0 + TD * k + TD])\
              .then_inc(S["lfn_in"], 16)
        sp.dma_start(KS[:], O["kv"][0:KT, :, S0:T].rearrange("k p t -> p k t")).then_inc(S["ks_in"], 16)
        sp.dma_start(PTS[:, 0:4, :].rearrange("p a c -> p (a c)"),
                         O["kv"][KT:2 * KT, :, S0:T].rearrange("k p t -> p k t")).then_inc(S["vst_in"], 16)
        sp.dma_start(MKS[:], I["mask_new"]).then_inc(S["sconst"], 16)
        for k in range(NB):
            for g in range(NPG):
                page = sp.value_load(I["page_table"][0:1, k * NPG + g:k * NPG + g + 1], min_val=0,
                                     max_val=I["cache_k"].shape[0] - 1)
                sp.dma_start(LFP[16 * k:16 * k + 16, g * PAGE:(g + 1) * PAGE],
                             I["cache_lf"][page]).then_inc(S["lfp_in"], 16)
        def pages(k):
            return [sp.value_load(I["page_table"][0:1, bass.ds(k * NPG + g, 1)], min_val=0,
                                  max_val=I["cache_k"].shape[0] - 1) for g in range(NPG)]

        def keys(k, e):
            for g, page in enumerate(pages(k)):
                if g == 0:
                    sp.wait_ge(S["kb_used"], k + 1)
                sp.dma_start(KB[:, e, g], I["cache_k"][page]).then_inc(S[f"kb_in{e}"], 16)

        def values(k, first=False):
            for g, page in enumerate(pages(k)):
                if g == 0 and not first:
                    sp.wait_ge(S["vb_used"], k)
                sp.dma_start(VB[:, g, :], I["cache_v"][page]).then_inc(S["vb_in"], 16)

        keys(0, 0)
        keys(1, 1)
        values(0, first=True)
        with sp.Fori(0, NB // 2 - 1) as i:
            for e in range(2):
                keys(i * 2 + (e + 2), e)
                values(i * 2 + (e + 1))
        values(NB - 1)
        weights(UNITS_1, UNITS_2, False)

    @block.gpsimd
    def _(pool):
        pool.memset(ZERO[:], 0.0).then_inc(S["filled"], 1)
        pool.memset(ONES[:], 1.0).then_inc(S["filled"], 1)
        pool.memset(TINY[:], 1e-30).then_inc(S["filled"], 1)
        pool.wait_ge(S["filled"], 3)
        with pool.Fori(0, (UNITS_1 + UNITS_2) // 2) as i:
            for u in range(2):
                pool.wait_ge(S[f"w_raw{u}"], i * 16 + 16)
                pool.wait_ge(S["unit_used"], i * 2 + (u + 1))
                pool.tensor_tensor(WH[:, u, :], WRAW[:, u, :], ZERO[:].broadcast_to([P, UNIT]),
                                   ALU.add).then_inc(S["pool_hi"], 1)
                pool.wait_ge(S["pool_hi"], i * 2 + (u + 1))
                pool.tensor_tensor(WL[:, u, :], WRAW[:, u, :], WH[:, u, :].bitcast(F32),
                                   ALU.subtract).then_inc(S["split_done"], 1)

    @block.tensor
    def _(pe):
        split = Count(S["split_done"])
        free = [Count(S["free0"]), Count(S["free1"])]
        ready = [S["ready0"], S["ready1"]]
        acc, hn = Count(S["dve_acc"], 2), Count(S["dve_lo"], 1)
        act_chunk = Count(S["act_ready"], 1)
        pe.sem_inc(S["unit_used"], 2)

        def tiles(t, u):
            return lambda n: t[:, u, n * P:(n + 1) * P]

        def job(slot, wh, wl, xh, xl, kts, first=True, last=True, fresh=None):
            for n, k in enumerate(kts):
                if fresh:
                    pe.wait_ge(fresh.sem, fresh.next())
                for m, (lhs, rhs) in enumerate(((wh, xh), (wh, xl), (wl, xh))):
                    for c, (lo, hi) in enumerate(PIECES):
                        o = SLOT[slot] + 512 * c
                        mm = pe.matmul(PS[:, o:o + hi - lo], lhs(n), rhs[:, k, lo:hi],
                                       start=first and n == 0 and m == 0,
                                       stop=last and n == len(kts) - 1 and m == 2)
            return mm

        def release(n=1):
            pe.drain().then_inc(S["unit_used"], n)

        def unit_job(u, xh, xl, fresh=None):
            pe.wait_ge(split.sem, split.next())
            pe.wait_ge(free[u].sem, free[u].next())
            job(u, tiles(WH, u), tiles(WL, u), xh, xl, range(KT), fresh=fresh).then_inc(ready[u], 1)
            release()

        def proj(xh, xl, pairs, fresh=None):
            if fresh:
                unit_job(0, xh, xl, fresh)
                unit_job(1, xh, xl)
                pairs -= 1
            with rounds(pe, pairs, {split: 2, free[0]: 1, free[1]: 1}):
                for u in range(2):
                    unit_job(u, xh, xl)

        def norm():
            pe.wait_ge(acc.sem, acc.next(KT))
            pe.wait_ge(free[0].sem, free[0].next())
            for c, (lo, hi) in enumerate(PIECES):
                mm = pe.matmul(PS[:, 512 * c:512 * c + hi - lo], ONES[:], ACC[:, lo:hi], start=True, stop=True)
            mm.then_inc(ready[0], 1)

        norm()
        mod_rows = Count(S["mods_row"])
        mwi = [Count(S[f"mw{v}"]) for v in range(4)]

        def mod_block(e):
            for h in range(2):
                v = 2 * e + h
                pe.wait_ge(mwi[v].sem, mwi[v].next(16))
                for k in range(KT // 2):
                    mm = pe.matmul(PS[0:NV, 3072 + 512 * e:3584 + 512 * e], CT[:, h * KT // 2 + k, :], MW[v][:, k, :],
                                   start=(h + k == 0), stop=(h == 1 and k == KT // 2 - 1))
                mm.then_inc(S["mods_psum"] if h else S["mw_used"], 1)

        def mod_turn(e):
            pe.wait_ge(mod_rows.sem, mod_rows.next())
            for m in range(MB):
                mm = pe.matmul(PS[:, 2048 + 512 * e + m * NV:2048 + 512 * e + (m + 1) * NV],
                               MROW[:, e, m * P:(m + 1) * P], ID[0:NV, 0:NV], start=True, stop=True)
            mm.then_inc(S["mods_turned"], 1)

        pe.wait_ge(S["silu"], 1)
        mod_block(0)
        with rounds(pe, MT // (2 * MB) - 1, {mod_rows: 2} | {w_: 16 for w_ in mwi}):
            mod_block(1)
            mod_turn(0)
            mod_block(0)
            mod_turn(1)
        mod_block(1)
        mod_turn(0)
        mod_turn(1)
        gate_w, xc = [Count(S["gate_w0"]), Count(S["gate_w1"])], Count(S["xc_ready"])
        for half in range(2):
            proj(HH, HL, RH, None if half else hn)
            for j in range(RH):
                kk = [k - RH * half for k in GATE_IN[RH * half + j]]
                pe.wait_ge(xc.sem, RH * half + max(kk) + 1)
                gw = gate_w[(RH * half + j) % 2]
                pe.wait_ge(gw.sem, gw.next(16))
                for u in range(2):
                    pe.wait_ge(free[u].sem, free[u].next())
                    for n, k in enumerate(kk):
                        for c, (lo, hi) in enumerate(PIECES):
                            mm = pe.matmul(PS[:, SLOT[u] + 512 * c:SLOT[u] + 512 * c + hi - lo], GW[:, (RH * half + j) % 2, u, n, :],
                                           XC[:, k, lo:hi], start=(n == 0), stop=(n == len(kk) - 1))
                    mm.then_inc(ready[u], 1)
        pe.wait_ge(S["y_ready"], RT)
        with rounds(pe, KT // 2, {split: 4, free[0]: 1, free[1]: 1}):
            for s in range(2):
                pe.wait_ge(free[s].sem, free[s].next())
                for u in range(2):
                    pe.wait_ge(split.sem, split.next())
                    mm = job(s, tiles(WH, u), tiles(WL, u), YH, YL, range(5 * u, 5 * u + 5), u == 0, u == 1)
                    if u == 1:
                        mm.then_inc(ready[s], 1)
                    release()

        def ffn():
            def up(pairs, fresh=None):
                proj(HH, HL, pairs, fresh)

            def down():
                chunks = act_chunk.next(GC)
                with rounds(pe, 2, {split: 2, free[0]: 2, free[1]: 2}):
                    pe.wait_ge(act_chunk.sem, chunks)
                    for u in range(2):
                        pe.wait_ge(split.sem, split.next())
                        for s in range(2):
                            pe.wait_ge(free[s].sem, free[s].next())
                            job(s, lambda n: WH[:, u, (s * GC + n) * P:(s * GC + n + 1) * P],
                                lambda n: WL[:, u, (s * GC + n) * P:(s * GC + n + 1) * P],
                                AH, AL, range(GC)).then_inc(ready[s], 1)
                        release()
            up(GC, hn)
            with rounds(pe, NG - 1, {split: 12, free[0]: 8, free[1]: 8, act_chunk: GC}):
                for u in range(2):
                    unit_job(u, HH, HL)
                down()
                up(GC - 1)
            down()

        norm()
        ffn()
        norm()
        pe.wait_ge(split.sem, split.next())
        pe.wait_ge(free[0].sem, free[0].next())
        job(0, tiles(WH, 0), tiles(WL, 0), HH, HL, range(KT), fresh=hn).then_inc(ready[0], 1)
        split.next()
        release(2)
        proj(HH, HL, KT)
        proj(HH, HL, KT // 2, hn)

        s_free, o_free = [Count(S["s_free0"]), Count(S["s_free1"])], Count(S["o_free"])
        qs, nbr, p_rdy, pt_rdy = (Count(S[n]) for n in ("qs_ready", "cumh", "p_ready", "pt_ready"))
        kvi = [Count(S["kv_in0"]), Count(S["kv_in1"])]
        pe.wait_ge(S["q_ready"], 2)
        pe.wait_ge(S["lf_ready"], 2)
        for q in range(KT):
            mm = pe.transpose(PS[:, q * NH:(q + 1) * NH], CUM[:, q * P:(q + 1) * P], ID[0:NH, 0:NH])
        mm.then_inc(S["cq_psum"], 1)
        pe.wait_ge(S["cq_done"], 1)
        STEPS = 2 * KT
        per = {s_free[0]: 2 + STEPS // 2, s_free[1]: 2 + STEPS // 2, o_free: STEPS, qs: 1, kvi[0]: 16, kvi[1]: 16,
               nbr: 2, p_rdy: STEPS, pt_rdy: STEPS}
        with rounds(pe, KT // 2, {s_: 2 * k for s_, k in per.items()}):
            for par in range(2):
                sjob = 0

                def s_buffer():
                    nonlocal sjob
                    fr = s_free[sjob % 2]
                    pe.wait_ge(fr.sem, fr.next())
                    sjob += 1
                    return 1024 * ((sjob - 1) % 2)

                pe.wait_ge(kvi[par].sem, kvi[par].next(32))
                for hv in range(2):
                    o = s_buffer()
                    for k in range(4):
                        mm = pe.transpose(PS[:, o + k * P:o + (k + 1) * P], VT[:, par, (hv * 4 + k) * P:(hv * 4 + k + 1) * P], ID[:])
                    mm.then_inc(S["s_ready"], 1)
                pe.wait_ge(qs.sem, qs.next())
                for t in range(STEPS + 3):
                    if t < STEPS:
                        e, qi = divmod(t, KT)
                        rows = slice(HD * e, HD * e + HD)
                        if qi == 0:
                            pe.wait_ge(nbr.sem, nbr.next())
                            o = s_buffer()
                            for lo in (0, 512):
                                mm = pe.matmul(PS[:, o + lo:o + lo + 512], ONES[0:NH, :], CUMH[:, lo:lo + 512],
                                               start=True, stop=True)
                            mm.then_inc(S["s_ready"], 1)
                        o = s_buffer()
                        L = (qi + 1) * P
                        for lo in range(0, L, 512):
                            hi = min(L, lo + 512)
                            pe.matmul(PS[:, o + lo:o + hi], QS[rows, qi * P:(qi + 1) * P], KP[rows, par, lo:hi],
                                      start=True, stop=True)
                        mm = pe.matmul(PS[:, o + L - P:o + L], IDB[:], MSKB[:], start=False, stop=True,
                                       skip_group_check=True)
                        mm.then_inc(S["s_ready"], 1)
                    if t >= 3:
                        u = t - 3
                        e, qi = divmod(u, KT)
                        pe.wait_ge(pt_rdy.sem, pt_rdy.next())
                        pe.wait_ge(o_free.sem, o_free.next())
                        for k in range(qi + 1):
                            mm = pe.matmul(PS[HD * e:HD * e + HD, 3072 + 512 * (u % 2):3072 + 512 * (u % 2) + P],
                                           V[:, k, HD * e:HD * e + HD], PT[:, u % 2, k * P:(k + 1) * P],
                                           start=(k == 0), stop=(k == qi))
                        mm.then_inc(S["o_psum"], 1)
                    if 2 <= t < STEPS + 2:
                        u = t - 2
                        qi = u % KT
                        pe.wait_ge(p_rdy.sem, p_rdy.next())
                        for k in range(qi + 1):
                            mm = pe.transpose(PS[:, 2048 + k * P:2048 + (k + 1) * P], SBUFS[u % 4][:, k * P:(k + 1) * P], ID[:])
                        mm.then_inc(S["pt_psum"], 1)

        pe.wait_ge(S["vst_in"], 16)
        for k in range(KT):
            mm = pe.transpose(PS[0:TS, 2048 + k * P:2048 + (k + 1) * P],
                              PTS[:, 0:4, :].rearrange("p a c -> p (a c)")[:, k * TS:(k + 1) * TS], ID[:])
        mm.then_inc(S["vn_psum"], 1)
        pe.wait_ge(S["cumm_ready"], 1)
        pe.matmul(PS[:, 0:TS], EA[:], CNM[:].rearrange("p b t -> p (b t)"), start=True, stop=True)\
          .then_inc(S["cq_psum"], 1)
        pe.wait_ge(S["cq_done"], 2)
        pe.wait_ge(S["vn_ready"], 1)
        pe.wait_ge(S["ks_in"], 16)
        vbi, qx, scp, scpt = (Count(S[n]) for n in ("vb_in", "qx_ready", "sc_p", "sc_pt"))
        kbi = [Count(S["kb_in0"]), Count(S["kb_in1"])]

        def scores(e):
            o = 1024 * e
            pe.wait_ge(kbi[e].sem, kbi[e].next(64))
            pe.wait_ge(qx.sem, qx.next())
            for k in range(KT):
                qk = QX[:, e, k * P:(k + 1) * P]
                pe.matmul(PS[:, o:o + PAST].rearrange("p (g c) -> p g c", g=NPG), qk, KB[:, e, :, k, :],
                          start=(k == 0), stop=False)
                pe.matmul(PS[:, o + PAST:o + PAST + TS], qk, KS[:, k, :], start=(k == 0), stop=False)
            pe.matmul(PS[:, o:o + PAST], EA[:], CUMX[e][:, 0:PAST], start=False, stop=True)
            pe.matmul(PS[:, o + PAST:o + PAST + TS], EA[:], CUMX[e][:, PAST:PAST + TS], start=False, stop=True)\
              .then_inc(S["sc_psum"], 1)
            pe.drain().then_inc(S["kb_used"], 1)

        def weighted(e):
            pe.wait_ge(scp.sem, scp.next())
            for k in range(NPG):
                pe.transpose(PS[:, 2048 + k * P:2048 + (k + 1) * P], SS[e][:, k * P:(k + 1) * P], ID[:])
            pe.transpose(PS[0:TS, 2560:2560 + P], SS[e][:, PAST:PAST + TS], ID[:]).then_inc(S["sc_ptp"], 1)
            pe.wait_ge(vbi.sem, vbi.next(64))
            pe.wait_ge(scpt.sem, scpt.next())
            oo = 3072 + 512 * e
            for k in range(KT):
                for g in range(NPG):
                    pe.matmul(PS[:, oo + 16 * k:oo + 16 * k + 16], VB[:, g, k * P:(k + 1) * P],
                              PTS[:, g, 16 * k:16 * k + 16], start=(g == 0), stop=False)
                mm = pe.matmul(PS[:, oo + 16 * k:oo + 16 * k + 16], VN[:, k * P:(k + 1) * P],
                               PTS[0:TS, NPG, 16 * k:16 * k + 16], start=False, stop=True)
            mm.then_inc(S["sc_o"], 1)
            pe.drain().then_inc(S["vb_used"], 1)

        scores(0)
        with rounds(pe, NB // 2 - 1, {kbi[0]: 64, kbi[1]: 64, vbi: 128, qx: 2, scp: 2, scpt: 2}):
            for e in range(2):
                scores(1 - e)
                weighted(e)
        scores(1)
        weighted(0)
        weighted(1)
        pe.wait_ge(S["sc_done"], NB)
        pe.wait_ge(S["o_ready"], KT)
        proj(OH, OL, KT // 2)
        norm()
        ffn()
        norm()

    @block.scalar
    def _(act):
        ready, free = [Count(S["ready0"]), Count(S["ready1"])], [S["free0"], S["free1"]]
        sq_free, x_done, var, tn = Count(S["dve_acc"]), Count(S["x_done"]), Count(S["dve_var"]), Count(S["dve_tn"])
        me = Count(S["act_self"])
        for n in range(4):
            act.sem_inc(S[f"kv_out{n}"], 16)

        def chain(ins):
            ins.then_inc(me.sem, 1)
            act.wait_ge(me.sem, me.next())

        def got(s):
            act.wait_ge(ready[s].sem, ready[s].next())

        def squares(made=None):
            with rounds(act, KT // 2, {sq_free: 2} | ({made: 2} if made else {})) as i:
                for u in range(2):
                    if made:
                        act.wait_ge(made.sem, made.next())
                    act.wait_ge(sq_free.sem, sq_free.next())
                    act.activation(SQ[:, u, :], X[:, i * 2 + u, :], ACT.Square).then_inc(S["act_sq"], 1)

        def norm(n, sums=True):
            if sums:
                ready[0].next()
                act.wait_ge(var.sem, var.next())
                chain(act.activation(RS[:], ACC[:], ACT.Ln))
                act.activation(RS[:], RS[:], ACT.Exp, scale=-0.5).then_inc(S["act_root"], 1)
            if NORMS[n]:
                sh, sc = NORMS[n]
                with rounds(act, KT // 2, {tn: 2}) as i:
                    for u in range(2):
                        act.wait_ge(tn.sem, tn.next())
                        par = dict(scale=MOD[:, sc + u + i * 2, 0:1], bias=MOD[:, sh + u + i * 2, 0:1])
                        act.activation(HH[:, i * 2 + u, 0:S0], TN[:, u, 0:S0], ACT.Identity, **par)
                        act.activation(HH[:, i * 2 + u, S0:T], TN[:, u, S0:T], ACT.Copy)
                        act.activation(TN[:, u, 0:S0], TN[:, u, 0:S0], ACT.Identity, **par)\
                           .then_inc(S["act_hi"], 1)

        act.wait_ge(S["consts"], 16 * N_CONSTS)
        act.wait_ge(S["filled"], 3)
        act.activation(SG[:], CT[:], ACT.Sigmoid).then_inc(S["sigmoid"], 1)
        chain(act.activation(SPT[:, 0, :], RGP[:, :, 7], ACT.Abs))
        act.activation(SPT[:, 1, :], SPT[:, 0, :], ACT.Exp, scale=-1.0).then_inc(S["lam_exp"], 1)
        act.wait_ge(S["x_in"], 16)
        squares()
        norm(0)
        act.dma_start(RHALO[:], I["rg_halo"]).then_inc(S["rg_halo"], 16)
        act.wait_ge(S["rg_halo"], 16)
        conv_free, pair_free, tanh_ = Count(S["conv_free"]), Count(S["pair_free"]), Count(S["act_tanh"])
        for jt in range(2):
            act.dma_start(GW[:, jt], I["rg_gate_w"][jt]).then_inc(S[f"gate_w{jt}"], 16)
        for half in range(2):
            with rounds(act, RH, {ready[0]: 1, ready[1]: 1, conv_free: 1}) as j:
                got(0)
                act.wait_ge(conv_free.sem, conv_free.next())
                act.activation(three(RU[:, 3:3 + S0]), prompt(0), ACT.Copy)
                ru = RU[:, 3 + S0:WU].rearrange("p (b t) -> p b t", b=NB)
                act.activation(ru[:, :, 0:3], RHALO[:, j + RH * half, :].rearrange("p (b t) -> p b t", b=NB), ACT.Copy)
                act.activation(ru[:, :, 3:3 + TD], req(sample(0)), ACT.Copy).then_inc(free[0], 1)
                got(1)
                act.activation(three(YG[:, j + RH * half, 0:S0]), prompt(1), ACT.Gelu_apprx_tanh)
                act.activation(YG[:, j + RH * half, S0:T], sample(1), ACT.Gelu_apprx_tanh).then_inc(free[1], 1)
            for j in range(RH):
                jt = RH * half + j
                act.wait_ge(pair_free.sem, pair_free.next())
                got(0)
                act.activation(three(RS1[:, 0:S0]), prompt(0), ACT.Sigmoid, bias=RGP[:, jt, 5:6])
                act.activation(RS1[:, S0:T], sample(0), ACT.Sigmoid, bias=RGP[:, jt, 5:6]).then_inc(free[0], 1)
                got(1)
                act.activation(three(RI1[:, 0:S0]), prompt(1), ACT.Sigmoid, bias=RGP[:, jt, 6:7])
                act.activation(RI1[:, S0:T], sample(1), ACT.Sigmoid, bias=RGP[:, jt, 6:7]).then_inc(free[1], 1)
                if jt + 2 < RT:
                    act.dma_start(GW[:, jt % 2], I["rg_gate_w"][jt + 2]).then_inc(S[f"gate_w{jt % 2}"], 16)
                act.wait_ge(free[0], ready[0].now() + 1)
                act.wait_ge(free[1], ready[1].now() + 1)
                act.wait_ge(S["sp_done"], 1)
                act.activation(RS1[:], RS1[:], ACT.Tanh, scale=SP4[:, jt:jt + 1]).then_inc(tanh_.sem, 1)
                act.wait_ge(tanh_.sem, tanh_.next())
                act.activation(RQ1[:], RS1[:], ACT.Sqrt, bias=TINY[:]).then_inc(S["act_sqrt"], 1)
        act.wait_ge(pair_free.sem, pair_free.next())
        act.dma_start(O["rst"], RST[:]).then_inc(S["rst_out"], 16)
        act.dma_start(O["hst"], HST[:]).then_inc(S["rst_out"], 16)
        with act.Fori(0, RT) as k:
            act.activation(YH[:, k, :], YG[:, k, :], ACT.Copy).then_inc(S["y_hi"], 1)
        act.wait_ge(S["rst_out"], 32)
        act.dma_start(X[:], I["xT"].rearrange("k p t -> p k t")).then_inc(S["x_back"], 16)
        for s in range(2):
            ready[s].next(KT // 2)

        act_rdy = Count(S["act_ready"])
        conv, prod, gelu = Count(S["f_conv"]), Count(S["f_prod"]), Count(S["f_gelu"])
        loads, stores = Count(S["ffn_in"]), Count(S["ffn_out"])

        def ffn(layer):
            def chunk(n, c):
                act.wait_ge(act_rdy.sem, act_rdy.next())
                for s in range(2):
                    got(s)
                    fu = FU[:, s, 2 + S0:WF].rearrange("p (b t) -> p b t", b=NB)
                    act.activation(three(FU[:, s, 2:2 + S0]), prompt(s), ACT.Copy)
                    act.activation(fu[:, :, 2:2 + TD], req(sample(s)), ACT.Copy)
                    act.activation(fu[:, :, 0:2], FHALO[:, n + FT * s, :].rearrange("p (b t) -> p b t", b=NB), ACT.Copy)
                    par = dict(scale=FCW[:, n + FT * s, 2:3], bias=FCW[:, n + FT * s, 3:4])
                    act.activation(three(FC[:, s, 0:S0]), prompt(s), ACT.Identity, **par)
                    act.activation(FC[:, s, S0:T], sample(s), ACT.Identity, **par).then_inc(free[s], 1)
                act.wait_ge(conv.sem, conv.next())
                act.activation(FC[:, 0, :], FC[:, 0, :], ACT.Gelu_apprx_tanh).then_inc(S["f_gelu"], 1)
                act.wait_ge(prod.sem, prod.next())
                act.activation(AH[:, c, :], FC[:, 0, :], ACT.Copy).then_inc(S["f_hi"], 1)

            def down():
                for s in range(2):
                    ready[s].next(KT // 2)
            act.dma_start(FHALO[:], I["ffn_halo"][layer]).then_inc(S["ffn_in"], 16)
            act.dma_start(FCW[:], I["ffn_par"][layer]).then_inc(S["ffn_in"], 16)
            norm(1 if layer == 0 else 4)
            act.wait_ge(loads.sem, loads.next(32))
            ones = {ready[0]: 1, ready[1]: 1, act_rdy: 1, conv: 1, prod: 1}
            with rounds(act, GC, ones) as c:
                chunk(c, c)
            with rounds(act, NG - 1, {ready[0]: 8, ready[1]: 8, act_rdy: GC, conv: GC, prod: GC}) as g:
                chunk(g * GC + GC, 0)
                down()
                with rounds(act, GC - 1, ones) as c:
                    chunk(g * GC + c + (GC + 1), c + 1)
            down()
            x_done.next((NG - 1) * KT)
            squares(x_done)
            act.dma_start(O["fst"][layer], FST[:]).then_inc(S["ffn_out"], 16)
            act.wait_ge(stores.sem, stores.next(16))

        squares(x_done)
        ffn(0)
        norm(2)
        ready[0].next()
        act.wait_ge(free[0], ready[0].now() + 1)
        chain(act.activation(LA[:], LZ[:], ACT.Abs))
        chain(act.activation(LE[:], LA[:], ACT.Exp, scale=-1.0))
        act.activation(LE[:], LE[:], ACT.Ln, bias=ONES[0:NH, 0:1]).then_inc(S["lf_e"], 1)
        act.wait_ge(S["lf_ready"], 1)
        act.dma_start(O["lf"], LF[:]).then_inc(S["lf_out"], 16)
        out = [Count(S[f"kv_out{n}"]) for n in range(4)]
        per = {ready[0]: 2, ready[1]: 2, me: 4} | {o: 16 for o in out}
        with rounds(act, KV_ROUNDS, per) as i:
            for n in range(4):
                s = n % 2
                got(s)
                act.wait_ge(out[n].sem, out[n].next(16))
                act.activation(three(STG[:, n, 0:S0]), prompt(s), ACT.Copy)
                act.activation(STG[:, n, S0:T], sample(s), ACT.Copy).then_inc(me.sem, 1)
                act.wait_ge(me.sem, me.next())
                act.sem_inc(free[s], 1)
                act.dma_start(O["kv"][i * 4 + n], STG[:, n, :]).then_inc(out[n].sem, 16)
        for n in range(4):
            act.wait_ge(out[n].sem, out[n].next(16))
        act.wait_ge(S["lf_out"], 16)
        norm(3, sums=False)
        act.wait_ge(S["dve_lo"], 4 * KT + 1)
        with rounds(act, KT // 2, {ready[0]: 1, ready[1]: 1}) as i:
            for s in range(2):
                got(s)
                act.activation(three(Q[:, i * 2 + s, 0:S0]), prompt(s), ACT.Copy, scale=float(HD) ** -0.5)
                act.activation(Q[:, i * 2 + s, S0:T], sample(s), ACT.Copy, scale=float(HD) ** -0.5).then_inc(free[s], 1)
        act.drain().then_inc(S["q_ready"], 2)

        STEPS = 2 * KT
        stt, ptp, ops = Count(S["stt_done"]), Count(S["pt_psum"]), Count(S["o_psum"])
        freeq = Count(S["pair_done"], 1)
        with rounds(act, KT, {stt: STEPS, ptp: STEPS, ops: STEPS, freeq: 1}) as pair:
            act.wait_ge(freeq.sem, freeq.next())
            act.activation(QS[:], Q[:, pair, 0:SEQ], ACT.Copy).then_inc(S["qs_ready"], 1)
            for t in range(STEPS + 2):
                if t < STEPS:
                    L = (t % KT + 1) * P
                    act.wait_ge(stt.sem, stt.next())
                    act.activation(SBUFS[t % 4][:, 0:L], SBUFS[t % 4][:, 0:L], ACT.Exp, bias=NM[:, t % 4:t % 4 + 1],
                                   accum_out=SUM[:, t % 4:t % 4 + 1]).then_inc(S["exp_done"], 1)
                if t >= 2:
                    u = t - 2
                    L = (u % KT + 1) * P
                    act.wait_ge(ptp.sem, ptp.next())
                    if u >= 2:
                        act.wait_ge(ops.sem, ops.next())
                    act.activation(PT[:, u % 2, 0:L], PS[:, 2048:2048 + L], ACT.Copy).then_inc(S["pt_ready"], 1)
            ops.next(2)

        act.wait_ge(S["vn_psum"], 1)
        act.activation(VN, PS[0:TS, 2048:2048 + D], ACT.Copy).then_inc(S["vn_ready"], 1)
        nm, scp = Count(S["sc_nm"]), Count(S["sc_ptp"])
        with rounds(act, NB // 2, {nm: 2, scp: 2}):
            for e in range(2):
                act.wait_ge(nm.sem, nm.next())
                act.activation(SS[e], SS[e], ACT.Exp, bias=NM[:, e:e + 1], accum_out=SUM[:, e:e + 1])\
                   .then_inc(S["sc_exp"], 1)
                act.wait_ge(scp.sem, scp.next())
                act.activation(PTS[:, 0:NPG, :].rearrange("p g q -> p (g q)"), PS[:, 2048:2048 + PAST], ACT.Copy)
                act.activation(PTS[0:TS, NPG, :], PS[0:TS, 2560:2560 + P], ACT.Copy).then_inc(S["sc_pt"], 1)
        act.wait_ge(S["sc_done"], NB)
        with act.Fori(0, KT) as k:
            act.activation(OH[:, k, :], OT[:, k, :], ACT.Copy).then_inc(S["o_hi"], 1)
        for s in range(2):
            ready[s].next(KT // 2)
        act.wait_ge(S["o_ready"], KT)
        squares(x_done)
        ffn(1)
        norm(5)
        hi, yo = Count(S["act_hi"], 5 * KT), [Count(S["y_out0"]), Count(S["y_out1"])]
        for u in range(2):
            act.sem_inc(yo[u].sem, 16)
        with rounds(act, KT // 2, {tn: 2, hi: 2, yo[0]: 16, yo[1]: 16}) as i:
            for u in range(2):
                act.wait_ge(tn.sem, tn.next())
                act.wait_ge(yo[u].sem, yo[u].next(16))
                act.activation(YO[:, u, :], TN[:, u, :], ACT.Copy, scale=NGAIN[:, 5, bass.ds(i * 2 + u, 1)])\
                   .then_inc(hi.sem, 1)
                act.wait_ge(hi.sem, hi.next())
                act.dma_start(O["yT"][i * 2 + u], YO[:, u, :]).then_inc(yo[u].sem, 16)
        for u in range(2):
            act.wait_ge(yo[u].sem, yo[u].next(16))

    @block.vector
    def _(dve):
        ready, free = [Count(S["ready0"]), Count(S["ready1"])], [S["free0"], S["free1"]]
        sq, root, hi = Count(S["act_sq"]), Count(S["act_root"]), Count(S["act_hi"])
        accs, los = Count(S["dve_acc"], 2), Count(S["dve_lo"], 1)
        me = Count(S["dve_self"])
        TT, TSC, STT = dve.tensor_tensor, dve.tensor_scalar, dve.scalar_tensor_tensor

        def chain(ins):
            ins.then_inc(me.sem, 1)
            dve.wait_ge(me.sem, me.next())

        def got(s):
            dve.wait_ge(ready[s].sem, ready[s].next())

        def add_square(u):
            dve.wait_ge(sq.sem, sq.next())
            TT(ACC[:], ACC[:], SQ[:, u, :], ALU.add).then_inc(accs.sem, 1)
            dve.wait_ge(accs.sem, accs.next())

        def rms():
            got(0)
            TSC(three(ACC[:, 0:S0]), prompt(0), 1.0 / D, EPS, ALU.mult, ALU.add)
            TSC(ACC[:, S0:T], sample(0), 1.0 / D, EPS, ALU.mult, ALU.add).then_inc(S["dve_var"], 1)
            dve.wait_ge(var.sem, var.next())
            dve.sem_inc(free[0], 1)
            dve.wait_ge(root.sem, root.next())
            chain(STT(NT[:], RS[:], -0.5, RS[:], ALU.mult, ALU.mult))
            chain(TT(NT[:], NT[:], ACC[:], ALU.mult))
            chain(STT(RS[:], NT[:], 1.5, RS[:], ALU.add, ALU.mult))

        def normed(n, k, u):
            if not NORMS[n]:
                TT(TN[:, u, :], X[:, k, :], RS[:], ALU.mult).then_inc(S["dve_tn"], 1)
                return
            dve.wait_ge(los.sem, los.now())
            sh, sc = NORMS[n]
            chain(TT(TN[:, u, :], X[:, k, :], RS[:], ALU.mult))
            s = req(TN[:, u, S0:T])
            chain(TT(s, s, bc_t(MOD[:, sc + k, 1:NV]), ALU.mult))
            TT(s, s, bc_t(MOD[:, sh + k, 1:NV]), ALU.add).then_inc(S["dve_tn"], 1)

        def low(n, k, u):
            dve.wait_ge(hi.sem, hi.next())
            if NORMS[n]:
                TT(HL[:, k, :], TN[:, u, :], HH[:, k, :].bitcast(F32), ALU.subtract).then_inc(los.sem, 1)
                los.next()

        def norm(n, sums=True):
            if sums:
                rms()
            m = 2 if NORMS[n] else 0
            normed(n, 0, 0)
            with rounds(dve, KT // 2 - 1, {me: 2 * m, hi: 2, los: m}) as i:
                normed(n, i * 2 + 1, 1)
                low(n, i * 2, 0)
                normed(n, i * 2 + 2, 0)
                low(n, i * 2 + 1, 1)
            normed(n, KT - 1, 1)
            low(n, KT - 2, 0)
            low(n, KT - 1, 1)

        def residual(s, k, gate):
            got(s)
            TT(req(XS[:, s, :]), req(sample(s)), bc_t(MOD[:, gate + k, 1:NV]), ALU.mult)\
              .then_inc(me.sem, 1)
            STT(three(X[:, k, 0:S0]), prompt(s), MOD[:, gate + k, 0:1], three(X[:, k, 0:S0]),
                ALU.mult, ALU.add).then_inc(free[s], 1)
            dve.wait_ge(me.sem, me.next())
            TT(X[:, k, S0:T], X[:, k, S0:T], XS[:, s, :], ALU.add).then_inc(S["x_done"], 1)

        var = Count(S["dve_var"])
        dve.sem_inc(S["dve_acc"], 2)
        dve.sem_inc(S["dve_lo"], 1)
        dve.sem_inc(S["conv_free"], 1)
        dve.sem_inc(S["pair_free"], 1)
        dve.sem_inc(S["act_ready"], 1)
        dve.wait_ge(S["consts"], 16 * N_CONSTS)
        chain(dve.tensor_copy(IDB[:], ID[:]))
        chain(dve.tensor_copy(MSKB[:], CQ[:].rearrange("p q h -> p (q h)")))
        dve.wait_ge(S["sigmoid"], 1)
        TT(CT[:], CT[:], SG[:], ALU.mult).then_inc(S["silu"], 1)
        lam = RGP[:, :, 7]
        dve.wait_ge(S["lam_exp"], 1)
        e, z, z2, acc_ = SPT[:, 1, :], SPT[:, 2, :], SPT[:, 3, :], SPT[:, 0, :]
        chain(TSC(z, e, 2.0, None, ALU.add))
        chain(dve.reciprocal(z, z))
        chain(TT(z, z, e, ALU.mult))
        chain(TT(z2, z, z, ALU.mult))
        chain(dve.memset(acc_, 1.0 / 17))
        for n in (15, 13, 11, 9, 7, 5, 3, 1):
            chain(TT(acc_, acc_, z2, ALU.mult))
            chain(TSC(acc_, acc_, 1.0 / n, None, ALU.add))
        chain(TT(acc_, acc_, z, ALU.mult))
        chain(TSC(z, lam, -1.0, 0.0, ALU.mult, ALU.max))
        chain(TSC(acc_, acc_, 8.0, None, ALU.mult))
        STT(SP4[:], z, 4.0, acc_, ALU.mult, ALU.add).then_inc(S["sp_done"], 1)
        dve.sem_inc(free[0], 1)
        dve.wait_ge(S["x_in"], 16)

        def gained(n):
            blk = MOD[:, NORMS[n][1]:NORMS[n][1] + KT, :]
            return STT(blk, blk, 1.0, NGAIN[:, n, :].unsqueeze(2).broadcast_to([P, KT, NV]), ALU.add, ALU.mult)

        chain(dve.memset(ACC[:], 0.0))
        with rounds(dve, KT // 2, {sq: 2, accs: 2}):
            for u in range(2):
                add_square(u)
        rms()
        rows_in, turned = Count(S["mods_psum"]), Count(S["mods_turned"])

        def rows(e):
            dve.wait_ge(rows_in.sem, rows_in.next())
            dve.tensor_copy(MROW[:, e, :], PS[0:NV, 3072 + 512 * e:3584 + 512 * e]).then_inc(S["mods_row"], 1)

        def turned_tiles(b, e):
            dve.wait_ge(turned.sem, turned.next())
            TT(MOD[:, bass.ds(b * MB, MB), :],
               PS[:, 2048 + 512 * e:2048 + 512 * e + MB * NV].rearrange("p (m v) -> p m v", v=NV),
               MODB[:, bass.ds(b * MB, MB)].unsqueeze(2).broadcast_to([P, MB, NV]), ALU.add)\
              .then_inc(S["mods_tile"], 1)

        def two_blocks(b):
            rows(1)
            turned_tiles(b, 0)
            rows(0)
            turned_tiles(b + 1, 1)

        first = 2 * KT // MB
        rows(0)
        with rounds(dve, first // 2, {rows_in: 2, turned: 2}) as i:
            two_blocks(i * 2)
        dve.wait_ge(S["mods_tile"], first)
        chain(gained(0))
        with rounds(dve, KT // 2, {rows_in: 4, turned: 4, me: 4, hi: 2, los: 2}) as i:
            for u in range(2):
                two_blocks(i * 4 + (2 * u + first))
                normed(0, i * 2 + u, u)
                low(0, i * 2 + u, u)
        done = first + 2 * KT
        with rounds(dve, (MT // MB - 2 - done) // 2, {rows_in: 2, turned: 2}) as i:
            two_blocks(i * 2 + done)
        rows(1)
        turned_tiles(MT // MB - 2, 0)
        turned_tiles(MT // MB - 1, 1)
        dve.wait_ge(S["mods_tile"], MT // MB)
        dve.sem_inc(free[1], 1)
        for n in range(1, 5):
            gained(n)
        for layer in range(2):
            for chunk in (G1, G2):
                m = mod_at(layer, chunk)
                ins = TSC(MOD[:, m:m + KT, :], MOD[:, m:m + KT, :], 1.0, None, ALU.add)
        ins.then_inc(S["mods_done"], 1)
        dve.wait_ge(S["mods_done"], 1)

        dve.wait_ge(S["dve_lo"], KT + 1)
        chain(dve.memset(RU[:, 0:3], 0.0))
        dve.wait_ge(S["rg_halo"], 16)
        sqr = Count(S["act_sqrt"])
        for half in range(2):
            if half:
                dve.wait_ge(ready[1].sem, ready[1].now())
            with rounds(dve, RH, {ready[0]: 1, ready[1]: 1, me: 7}) as j:
                jt = j + RH * half
                ready[0].next(), ready[1].next()
                dve.wait_ge(free[0], ready[0].now() + 1)
                ru = RU[:, 3 + S0:WU].rearrange("p (b t) -> p b t", b=NB)
                xp, xs = XC[:, j, 0:S0], req(XC[:, j, S0:T])
                TSC(xp, RU[:, 0:S0], RGP[:, jt, 0:1], RGP[:, jt, 4:5], ALU.mult, ALU.add).then_inc(me.sem, 1)
                TSC(xs, ru[:, :, 0:TD], RGP[:, jt, 0:1], RGP[:, jt, 4:5], ALU.mult, ALU.add).then_inc(me.sem, 1)
                me.next(2)
                for k in (1, 2, 3):
                    dve.wait_ge(me.sem, me.now())
                    STT(xp, RU[:, k:k + S0], RGP[:, jt, k:k + 1], xp, ALU.mult, ALU.add).then_inc(me.sem, 1)
                    STT(xs, ru[:, :, k:k + TD], RGP[:, jt, k:k + 1], xs, ALU.mult, ALU.add)\
                        .then_inc(me.sem if k < 3 else S["xc_ready"], 1)
                    me.next(2 if k < 3 else 1)
                dve.tensor_copy(RST[:, jt, 0:3], RU[:, SEQ:SEQ + 3])
                dve.tensor_copy(RST[:, jt, 3:3 * NV].rearrange("p (b t) -> p b t", b=NB), ru[:, :, TD:TD + 3])\
                   .then_inc(S["conv_free"], 1)
            for j in range(RH):
                jt = RH * half + j
                ready[0].next(), ready[1].next()
                dve.wait_ge(sqr.sem, sqr.next())
                chain(TSC(RW1[:], RS1[:], 1.0, None, ALU.add))
                chain(dve.reciprocal(RW1[:], RW1[:]))
                TSC(RA1[:], RW1[:], 2.0, -1.0, ALU.mult, ALU.add).then_inc(me.sem, 1)
                TT(RI1[:], RI1[:], XC[:, j, :], ALU.mult).then_inc(me.sem, 1)
                STT(RQ1[:], RQ1[:], 2.0, RW1[:], ALU.mult, ALU.mult).then_inc(me.sem, 1)
                dve.wait_ge(me.sem, me.next(3))
                chain(TT(RI1[:], RI1[:], RQ1[:], ALU.mult))
                a0, b0 = req(RA1[:, S0:T])[:, :, 0], req(RI1[:, S0:T])[:, :, 0]
                chain(TT(RW1[:, 0:NB], a0, H0[:, jt, :], ALU.mult))
                TT(b0, b0, RW1[:, 0:NB], ALU.add).then_inc(me.sem, 1)
                dve.memset(a0, 0.0).then_inc(me.sem, 1)
                dve.wait_ge(me.sem, me.next(2))
                chain(dve.tensor_tensor_scan(RQ1[:], RA1[:], RI1[:], 0.0, ALU.mult, ALU.add))
                dve.tensor_copy(HST[:, jt, 0:1], RQ1[:, SEQ - 1:SEQ])
                dve.tensor_copy(HST[:, jt, 1:NV], req(RQ1[:, S0:T])[:, :, TD - 1])
                TT(YG[:, jt, :], YG[:, jt, :], RQ1[:], ALU.mult).then_inc(S["pair_free"], 1)
        yhi = Count(S["y_hi"])
        with rounds(dve, RT, {yhi: 1}) as k:
            dve.wait_ge(yhi.sem, yhi.next())
            TT(YL[:, k, :], YG[:, k, :], YH[:, k, :].bitcast(F32), ALU.subtract).then_inc(S["y_ready"], 1)
        dve.wait_ge(S["x_back"], 16)

        def residuals(gate):
            with rounds(dve, KT // 2, {ready[0]: 1, ready[1]: 1, me: 2}) as i:
                for s in range(2):
                    residual(s, i * 2 + s, gate)

        def last_residuals(gate):
            chain(dve.memset(ACC[:], 0.0))
            residual(0, 0, gate)
            residual(1, 1, gate)
            add_square(0)
            with rounds(dve, KT // 2 - 1, {ready[0]: 1, ready[1]: 1, me: 2, sq: 2, accs: 2}) as i:
                residual(0, i * 2 + 2, gate)
                add_square(1)
                residual(1, i * 2 + 3, gate)
                add_square(0)
            add_square(1)

        dve.wait_ge(S["y_ready"], RT)
        last_residuals(mod_at(0, G1))
        xdone = Count(S["x_done"])
        dve.wait_ge(xdone.sem, xdone.next(KT))

        gel, fhi, loads = Count(S["f_gelu"]), Count(S["f_hi"]), Count(S["ffn_in"])

        def ffn(layer):
            gate = mod_at(layer, G2)
            norm(1 if layer == 0 else 4)
            dve.wait_ge(S["dve_lo"], KT * (2 if layer == 0 else 5) + 1)
            chain(dve.memset(FU[:, :, 0:2], 0.0))
            dve.wait_ge(loads.sem, loads.next(32))

            def taps(n):
                for s in range(2):
                    got(s)
                    dve.wait_ge(free[s], ready[s].now() + 1)
                    idx = n + FT * s
                    fu = FU[:, s, 2 + S0:WF].rearrange("p (b t) -> p b t", b=NB)
                    STT(FC[:, s, 0:S0], FU[:, s, 1:1 + S0], FCW[:, idx, 1:2], FC[:, s, 0:S0], ALU.mult, ALU.add)\
                        .then_inc(me.sem, 1)
                    STT(req(FC[:, s, S0:T]), fu[:, :, 1:1 + TD], FCW[:, idx, 1:2], req(FC[:, s, S0:T]),
                        ALU.mult, ALU.add).then_inc(me.sem, 1)
                    me.next(2)
                    dve.tensor_copy(FST[:, idx, 0:2], FU[:, s, SEQ:SEQ + 2])
                    dve.tensor_copy(FST[:, idx, 2:2 * NV].rearrange("p (b t) -> p b t", b=NB), fu[:, :, TD:TD + 2])
                    dve.wait_ge(me.sem, me.now())
                    STT(FC[:, s, 0:S0], FU[:, s, 0:S0], FCW[:, idx, 0:1], FC[:, s, 0:S0], ALU.mult, ALU.add)
                    STT(req(FC[:, s, S0:T]), fu[:, :, 0:TD], FCW[:, idx, 0:1], req(FC[:, s, S0:T]),
                        ALU.mult, ALU.add).then_inc(S["f_conv"] if s == 0 else me.sem, 1)
                me.next()

            def finish(c):
                dve.wait_ge(gel.sem, gel.next())
                dve.wait_ge(me.sem, me.now())
                TT(FC[:, 0, :], FC[:, 0, :], FC[:, 1, :], ALU.mult).then_inc(S["f_prod"], 1)
                dve.wait_ge(fhi.sem, fhi.next())
                TT(AL[:, c, :], FC[:, 0, :], AH[:, c, :].bitcast(F32), ALU.subtract).then_inc(S["act_ready"], 1)

            def down():
                residuals(gate)

            ones = {ready[0]: 1, ready[1]: 1, me: 5, gel: 1, fhi: 1}
            with rounds(dve, GC, ones) as c:
                taps(c)
                finish(c)
            with rounds(dve, NG - 1, {ready[0]: 8, ready[1]: 8, me: GC * 5 + KT,
                                      gel: GC, fhi: GC}) as g:
                taps(g * GC + GC)
                down()
                finish(0)
                with rounds(dve, GC - 1, ones) as c:
                    taps(g * GC + c + (GC + 1))
                    finish(c + 1)
            dve.wait_ge(S["act_ready"], FT * (layer + 1) + 1)
            last_residuals(gate)
            dve.wait_ge(xdone.sem, xdone.next(NG * KT))

        ffn(0)
        norm(2)
        got(0)
        dve.wait_ge(S["dve_lo"], 3 * KT + 1)
        TSC(three(LZ[:, 0:S0]), prompt(0, NH), KVB[:], None, ALU.add)
        TSC(LZ[:, S0:T], sample(0, NH), KVB[:], None, ALU.add).then_inc(free[0], 1)
        dve.wait_ge(free[0], ready[0].now() + 1)
        dve.wait_ge(S["lf_e"], 1)
        STT(LF[:], LZ[:], 0.0, LE[:], ALU.min, ALU.subtract).then_inc(S["lf_ready"], 1)
        dve.wait_ge(S["lf_ready"], 1)
        dve.tensor_tensor_scan(CUM[:], ONES[0:NH, 0:1].broadcast_to([NH, SEQ]), LF[:, 0:SEQ], 0.0,
                               ALU.mult, ALU.add).then_inc(S["lf_ready"], 1)
        for s in range(2):
            ready[s].next(KT)
        for n in range(4):
            dve.wait_ge(S[f"kv_out{n}"], KV_ROUNDS * 16 + 16)
        dve.wait_ge(S["lf_out"], 16)
        norm(3, sums=False)
        for s in range(2):
            ready[s].next(KT // 2)

        dve.wait_ge(S["q_ready"], 2)
        dve.wait_ge(S["cq_psum"], 1)
        dve.tensor_copy(CQ[:], PS[:, 0:KT * NH].rearrange("p (q h) -> p q h", h=NH)).then_inc(S["cq_done"], 1)
        dve.wait_ge(S["cq_done"], 1)
        chain(dve.memset(OT[:, :, SEQ:S0], 0.0))
        for n in (0, 1):
            dve.sem_inc(S[f"s_free{n}"], 1)
        dve.sem_inc(S["o_free"], 2)
        dve.sem_inc(S["pair_done"], 2)
        STEPS = 2 * KT
        srd, ex, ops = Count(S["s_ready"]), Count(S["exp_done"]), Count(S["o_psum"])
        with rounds(dve, KT, {srd: STEPS + 4, ex: STEPS, ops: STEPS, me: 2 * STEPS + 2}) as pair:
            sj = 0

            def s_job():
                nonlocal sj
                dve.wait_ge(srd.sem, srd.next())
                sj += 1
                return 1024 * ((sj - 1) % 2), S[f"s_free{(sj - 1) % 2}"]

            def head_logs(e):
                TSC(CUMH[:], CUM[:], ID[0:NH, bass.ds(pair * 2 + e, 1)], -1.0, ALU.mult, ALU.mult)\
                   .then_inc(S["cumh"], 1)

            head_logs(0)
            for hv in range(2):
                o, fr = s_job()
                dve.tensor_copy(V[:, hv * 4:hv * 4 + 4, :].rearrange("p k c -> p (k c)"), PS[:, o:o + 512]).then_inc(fr, 1)
            for t in range(STEPS + 3):
                if t < STEPS:
                    e, qi = divmod(t, KT)
                    L = (qi + 1) * P
                    if qi == 0:
                        o, fr = s_job()
                        chain(dve.tensor_copy(NBC[:, e, :], PS[:, o:o + SEQ]))
                        dve.sem_inc(fr, 1)
                    if t == 1:
                        head_logs(1)
                    o, fr = s_job()
                    sb_ = SBUFS[t % 4][:, 0:L]
                    STT(sb_, NBC[:, e, 0:L], CQ[:, qi, bass.ds(pair * 2 + e, 1)], PS[:, o:o + L], ALU.add, ALU.add)\
                        .then_inc(me.sem, 1)
                    dve.wait_ge(me.sem, me.next())
                    dve.sem_inc(fr, 1)
                    dve.tensor_reduce(NM[:, t % 4:t % 4 + 1], sb_, AX_X, ALU.max, negate=True).then_inc(S["stt_done"], 1)
                if 1 <= t < STEPS + 1:
                    u = t - 1
                    L = (u % KT + 1) * P
                    dve.wait_ge(ex.sem, ex.next())
                    chain(dve.reciprocal(RI[:, u % 4:u % 4 + 1], SUM[:, u % 4:u % 4 + 1]))
                    sb_ = SBUFS[u % 4][:, 0:L]
                    TSC(sb_, sb_, RI[:, u % 4:u % 4 + 1], None, ALU.mult).then_inc(S["p_ready"], 1)
                if t >= 3:
                    u = t - 3
                    e, qi = divmod(u, KT)
                    rows = slice(HD * e, HD * e + HD)
                    dve.wait_ge(ops.sem, ops.next())
                    dve.tensor_copy(OT[rows, pair, qi * P:(qi + 1) * P],
                                    PS[rows, 3072 + 512 * (u % 2):3072 + 512 * (u % 2) + P]).then_inc(S["o_free"], 1)
            dve.sem_inc(S["pair_done"], 1)

        chain(dve.memset(QX[:], 0.0))
        dve.wait_ge(S["lfp_in"], NB * NPG * 16)
        dve.wait_ge(S["lfn_in"], NB * 16)
        chain(dve.tensor_tensor_scan(CUMS[:, 0:PAST], ONES[:, 0:1].broadcast_to([P, PAST]), LFP[:], 0.0, ALU.mult, ALU.add))
        dve.sem_inc(S["kb_used"], 2)
        chain(dve.tensor_tensor_scan(CN[:], ONES[:, 0:TD], LFN[:], CUMS[:, PAST - 1:PAST], ALU.mult, ALU.add))
        chain(dve.tensor_copy(req(CUMS[:, PAST:PAST + TS]), CN[:].unsqueeze(1).broadcast_to([P, NB, TD])))
        TT(CNM[:], CN[:].unsqueeze(1).broadcast_to([P, NB, TD]), bc_t(BM[:]), ALU.mult).then_inc(S["cumm_ready"], 1)
        dve.wait_ge(S["cq_psum"], 2)
        chain(TT(CQT[:], req(PS[:, 0:TS]), MQ[:].unsqueeze(1).broadcast_to([P, NB, TD]), ALU.mult))
        dve.tensor_reduce(CQS[:], CQT[:], AX_X, ALU.add).then_inc(S["cq_done"], 1)
        dve.wait_ge(S["cq_done"], 2)
        dve.wait_ge(S["sconst"], 16)
        scps, scex, sco = Count(S["sc_psum"]), Count(S["sc_exp"]), Count(S["sc_o"])

        def queries(k, e):
            for hv in range(2):
                rows = slice(HD * hv, HD * hv + HD)
                dve.tensor_copy(QX[rows, e, :].rearrange("p (k x) -> p k x", x=P + 16)[:, :, 8 * hv:8 * hv + 8],
                                Q[rows, :, bass.ds(k * TD + S0, TD)])
            TSC(CUMX[e], CUMS[:], BM[:, bass.ds(k, 1)], None, ALU.mult).then_inc(S["qx_ready"], 1)

        def output(k, e):
            dve.wait_ge(sco.sem, sco.next())
            for hv in range(2):
                rows = slice(HD * hv, HD * hv + HD)
                ins = dve.tensor_copy(OT[rows, :, bass.ds(k * TD + S0, TD)],
                                      PS[rows, 3072 + 512 * e:3072 + 512 * e + P]
                                      .rearrange("p (k x) -> p k x", x=16)[:, :, 8 * hv:8 * hv + 8])
            ins.then_inc(S["sc_done"], 1)

        def softmax(k, e, ahead=True, before=True):
            nm, ri = NM[:, e:e + 1], RI[:, e:e + 1]
            dve.wait_ge(scps.sem, scps.next())
            chain(TSC(SS[e], PS[:, 1024 * e:1024 * e + PAST + TS], CQS[:, bass.ds(k, 1)], None, ALU.add))
            chain(TT(SS[e][:, PAST:PAST + TS], SS[e][:, PAST:PAST + TS], MKS[:, k, :], ALU.add))
            dve.tensor_reduce(nm, SS[e], AX_X, ALU.max, negate=True).then_inc(S["sc_nm"], 1)
            if ahead:
                queries(k + 2, e)
            dve.wait_ge(scex.sem, scex.next())
            chain(dve.reciprocal(ri, SUM[:, e:e + 1]))
            TSC(SS[e], SS[e], ri, None, ALU.mult).then_inc(S["sc_p"], 1)
            if before:
                output(k - 1, 1 - e)

        queries(0, 0)
        queries(1, 1)
        softmax(0, 0, before=False)
        softmax(1, 1)
        with rounds(dve, NB // 2 - 2, {scps: 2, scex: 2, sco: 2, me: 6}) as i:
            for e in range(2):
                softmax(i * 2 + (e + 2), e)
        softmax(NB - 2, 0, ahead=False)
        softmax(NB - 1, 1, ahead=False)
        output(NB - 1, 1)
        ohi = Count(S["o_hi"])
        with rounds(dve, KT, {ohi: 1}) as k:
            dve.wait_ge(ohi.sem, ohi.next())
            TT(OL[:, k, :], OT[:, k, :], OH[:, k, :].bitcast(F32), ALU.subtract).then_inc(S["o_ready"], 1)
        last_residuals(mod_at(1, G1))
        dve.wait_ge(xdone.sem, xdone.next(KT))
        ffn(1)
        norm(5)


N_CONSTS = 11
_OUTS = {"yT": (KT, P, T), "kv": (2 * KT, P, T), "lf": (NH, T), "rst": (P, RT, 3 * NV), "hst": (P, RT, NV),
         "fst": (2, P, 2 * FT, 2 * NV)}


def _layouts(d):
    import numpy as np
    f = np.float32
    a = {k: np.asarray(v) for k, v in d.items()}

    def cols(w, c0, c1, r0=0, r1=None):
        w = w[r0:r1, c0:c1]
        return w.reshape(-1, P, c1 - c0).transpose(1, 0, 2)

    def unit(*parts):
        u = np.concatenate([p.reshape(P, -1) for p in parts], 1)
        out = np.zeros((P, UNIT), f)
        out[:, :u.shape[1]] = u
        return out

    units = []
    w_in, w_out = a["rg_w_in"][0], a["rg_w_out"][0]
    for j in range(RT):
        units += [unit(cols(w_in, D_RNN + P * j, D_RNN + P * j + P)), unit(cols(w_in, P * j, P * j + P))]
    for o in range(KT):
        units += [unit(cols(w_out, P * o, P * o + P, 5 * P * h, 5 * P * h + 5 * P)) for h in range(2)]

    def ffn(l):
        up, dn = a["ffn_w_up"][l], a["ffn_w_down"][l]

        def pair(n):
            return [unit(cols(up, P * n, P * n + P)), unit(cols(up, D_FF + P * n, D_FF + P * n + P))]

        def down(g):
            r0 = g * GC * P
            return [unit(*(cols(dn, P * o, P * o + P, r0, r0 + GC * P) for o in (2 * v, 2 * v + 1))) for v in range(4)]
        out = []
        for g in range(NG):
            out += pair(GC * g)
            if g:
                out += down(g - 1)
            for c in range(1, GC):
                out += pair(GC * g + c)
        return out + down(NG - 1)

    units += ffn(0)
    kvw = a["kv_w"]
    units += [unit(np.pad(cols(kvw, 2 * D, 2 * D + NH), ((0, 0), (0, 0), (0, P - NH)))), np.zeros((P, UNIT), f)]
    units += [unit(cols(kvw, P * j, P * j + P)) for j in range(2 * KT)]
    units += [unit(cols(a["fa_wq"][0], P * j, P * j + P)) for j in range(KT)]
    units += [unit(cols(a["fa_wo"][0], P * j, P * j + P)) for j in range(KT)]
    units += ffn(1)
    assert len(units) == UNITS_1 + UNITS_2

    mw = np.concatenate([a["mod_w"][0], a["mod_w"][1], a["kv_mod_w"]], 1)
    mb = np.concatenate([a["mod_b"][0], a["mod_b"][1], a["kv_mod_b"]])
    chan = lambda v: v.reshape(-1, P).T
    x = np.concatenate([a["x_prompt"][0], np.zeros((PAD, D), f), a["x_sample"].reshape(TS, D)])
    c = np.concatenate([a["c_prompt"], a["c_sample"]])
    gates = np.zeros((RT, P, 2, 3, P), f)
    for u, w in enumerate((a["rg_wa"][0], a["rg_wx"][0])):
        full = np.zeros((D_RNN, D_RNN), f)
        for h in range(16):
            full[RG_W * h:RG_W * h + RG_W, RG_W * h:RG_W * h + RG_W] = w[h]
        for j in range(RT):
            for n, k in enumerate(GATE_IN[j]):
                gates[j, :, u, n] = full[P * k:P * k + P, P * j:P * j + P]
    par = np.stack([chan(v) for v in (*a["rg_conv_w"][0], a["rg_conv_b"][0], a["rg_ba"][0], a["rg_bx"][0],
                                      a["rg_lambda"][0])], 2)
    hs = np.arange(P)
    q = np.arange(P)
    pick = -((hs[:, None] % NH) == (hs[None, :] // TD)).astype(f)
    mask_new = np.full((P, NB, NB, TD), NEG, f)
    for b in range(NB):
        mask_new[:, b, b, :] = np.where(np.arange(TD)[None, :] <= (hs % TD)[:, None], 0.0, NEG)
    return {
        "wstream": np.stack(units),
        "mod_w": mw.reshape(2, KT // 2, P, MT // MB, MB * P).transpose(3, 0, 2, 1, 4)
                   .reshape(2 * MT // MB, P, KT // 2, MB * P),
        "mod_b": chan(mb),
        "cT": c.reshape(NV, KT, P).transpose(2, 1, 0),
        "gains": np.stack([chan(v) for v in (a["norm_mix_g"][0], a["norm_ffn_g"][0], a["kv_norm_g"],
                                             a["norm_mix_g"][1], a["norm_ffn_g"][1], a["final_norm_g"])], 1),
        "xT": x.T.reshape(KT, P, T),
        "rg_par": par,
        "rg_h0": a["state_rglru_h"][0].reshape(NB, RT, P).transpose(2, 1, 0),
        "rg_halo": a["state_rglru_conv"][0].reshape(NB, 3, RT, P).transpose(3, 2, 0, 1).reshape(P, RT, NB * 3),
        "rg_gate_w": gates,
        "ffn_halo": a["state_ffn_conv"].reshape(2, NB, 2, 2 * FT, P).transpose(0, 4, 3, 1, 2).reshape(2, P, 2 * FT, NB * 2),
        "ffn_par": np.concatenate([a["ffn_conv_w"].reshape(2, 3, 2 * FT, P).transpose(0, 3, 2, 1),
                                   a["ffn_conv_b"].reshape(2, 1, 2 * FT, P).transpose(0, 3, 2, 1)], 3),
        "kv_b": a["kv_b_f"].reshape(NH, 1),
        "cache_k": a["cache_k"].reshape(-1, PAGE, KT, P).transpose(0, 3, 2, 1),
        "cache_v": a["cache_v"].reshape(-1, PAGE, D),
        "cache_lf": a["cache_logf"].transpose(0, 2, 1),
        "page_table": a["page_table"].reshape(1, NB * NPG),
        "ident": np.eye(P, dtype=f),
        "mask": np.where(q[None, :] <= q[:, None], 0.0, NEG).astype(f).reshape(P, KT, NH),
        "pick_head": pick,
        "req_rows": ((hs[:, None] // NH) == np.arange(NB)[None, :]).astype(f),
        "pick_q": -((hs[:, None] % TD) == np.arange(TD)[None, :]).astype(f),
        "mask_new": mask_new.reshape(P, NB, TS),
    }


def kernel(**inputs):
    import numpy as np
    import concourse.bacc as bacc
    from concourse.bass_utils import run_bass_kernel_spmd

    nc = bacc.Bacc("TRN2", target_bir_lowering=False, num_devices=1)
    arrays, ins, outs = {}, {}, {}
    for name, v in _layouts(inputs).items():
        arrays[f"in_{name}"] = np.ascontiguousarray(v)
        ins[name] = nc.dram_tensor(f"in_{name}", v.shape, mybir.dt.from_np(v.dtype), kind="ExternalInput").ap()
    for name, shape in _OUTS.items():
        outs[name] = nc.dram_tensor(f"out_{name}", shape, F32, kind="ExternalOutput").ap()
    trunk(nc, ins, outs)
    res = run_bass_kernel_spmd(nc, [arrays], core_ids=[0]).results[0]
    g = {n: res[f"out_{n}"] for n in _OUTS}

    y = g["yT"].reshape(D, T).T
    kv = g["kv"].reshape(2, D, T).transpose(0, 2, 1).reshape(2, T, NH, HD)
    lf = g["lf"].T
    rst = g["rst"].transpose(2, 1, 0).reshape(NV, 3, D_RNN)
    hst = g["hst"].transpose(2, 1, 0).reshape(NV, D_RNN)
    fst = g["fst"].transpose(0, 3, 2, 1).reshape(2, NV, 2, 2 * D_FF)
    return (y[None, :SEQ], y[S0:].reshape(NB, TD, D),
            kv[0][None, :SEQ], kv[1][None, :SEQ], lf[None, :SEQ],
            rst[None, :1], hst[None, :1], fst[:, :1],
            kv[0][S0:].reshape(NB, TD, NH, HD), kv[1][S0:].reshape(NB, TD, NH, HD), lf[S0:].reshape(NB, TD, NH),
            rst[None, 1:], hst[None, 1:], fst[:, 1:])
```

```python
from contextlib import ExitStack, contextmanager

import concourse.bass as bass
from concourse import mybir

ALU = mybir.AluOpType
ACT = mybir.ActivationFunctionType
F32 = mybir.dt.float32
F32R = mybir.dt.float32r
BF16 = mybir.dt.bfloat16
AX_X = mybir.AxisListType.X

P = 128
D = 1024
KT = D // P
SEQ = 1024
NB, TD = 8, 8
TS = NB * TD
PAD = 2
S0 = SEQ + PAD
T = S0 + TS
PC = S0 // 3
NV = 1 + NB
D_RNN = 1280
RT = D_RNN // P
RH = RT // 2
D_FF = 3072
FT = D_FF // P
GC = 4
NG = FT // GC
NH, HD = 16, 64
PAGE, NPG = 128, 4
PAST = PAGE * NPG
EPS = 1e-6
NEG = -1e30
KV_ROUNDS = 2 * KT // 4
UNIT = KT * P
MODS_BEFORE = 4
MB = 4

SH1, SC1, G1, SH2, SC2, G2 = range(6)
MT = 2 * 6 * KT + 2 * KT


def mod_at(layer, chunk):
    return (layer * 6 + chunk) * KT


KV_SH, KV_SC = 2 * 6 * KT, 2 * 6 * KT + KT
NORMS = [(mod_at(0, SH1), mod_at(0, SC1)), (mod_at(0, SH2), mod_at(0, SC2)), (KV_SH, KV_SC),
         (mod_at(1, SH1), mod_at(1, SC1)), (mod_at(1, SH2), mod_at(1, SC2)), None]

RG_W = D_RNN // 16
GATE_IN = []
for _j in range(RT):
    _b0, _b1 = (P * _j) // RG_W, (P * _j + P - 1) // RG_W
    GATE_IN.append(list(range(RG_W * _b0 // P, (RG_W * (_b1 + 1) - 1) // P + 1)))

U_RG, U_OUT, U_FFN, U_LF, U_D = 2 * RT, 2 * KT, 2 * FT + NG * GC, 2, KT
UNITS_1 = U_RG + U_OUT + U_FFN + U_LF + 3 * U_D
UNITS_2 = U_D + U_FFN
PIECES = ((0, PC), (PC, 2 * PC), (2 * PC, T))


class Count:

    def __init__(self, sem, n=0):
        self.sem, self.n, self.loop = sem, n, 0

    def next(self, k=1):
        self.n += k
        return self.n + self.loop

    def now(self):
        return self.n + self.loop


@contextmanager
def rounds(eng, trips, per):
    before = [(c, c.n, c.loop) for c in per]
    with eng.Fori(0, trips) as i:
        for c, k in per.items():
            c.loop = c.loop + i * k
        yield i
    for c, n, loop in before:
        assert c.n - n == per[c], (c.sem, c.n - n, per[c])
        c.n, c.loop = n + per[c] * trips, loop


def trunk(nc, I, O):
    ctx = ExitStack()
    B0 = 16512
    placed = []

    def at(name, off, shape, dt=F32):
        size = 4 if dt != BF16 else 2
        for s in shape[1:]:
            size *= s
        placed.append(off + size)
        assert off + size <= 212832, (name, off + size)
        return nc.alloc_sbuf_tensor_at(name, shape, dt, offset=B0 + off, align_bytes=4)

    class Area:
        def __init__(self, off, end):
            self.off, self.end = off, end

        def __call__(self, name, shape, dt=F32):
            t = at(name, self.off, shape, dt)
            self.off = (placed[-1] + 31) // 32 * 32
            assert placed[-1] <= self.end, (name, placed[-1], self.end)
            return t

    TB = T * 4
    O_X, O_HN, O_R3, O_W, O_C = 0, KT * TB, 3 * KT * TB, 3 * KT * TB + 65408, 3 * KT * TB + 65408 + 6 * UNIT * 4

    X = at("X", O_X, [P, KT, T])
    HH = at("HH", O_HN, [P, KT, T], F32R)
    HL = at("HL", O_HN + KT * TB, [P, KT, T], F32R)
    w = Area(O_W, O_C)
    WRAW = w("WRAW", [P, 2, UNIT])
    WH = w("WH", [P, 2, UNIT], F32R)
    WL = w("WL", [P, 2, UNIT], F32R)
    c = Area(O_C, 212832)
    MOD = c("MOD", [P, MT, NV])
    MODB = c("MODB", [P, MT])
    NGAIN = c("NGAIN", [P, 6, KT])
    RS_OFF = c.off
    RS = c("RS", [P, T])
    ID = c("ID", [P, P])
    ONES = c("ONES", [P, P])
    IDB = c("IDB", [P, P], BF16)
    MSKB = c("MSKB", [P, P], BF16)
    RGP = c("RGP", [P, RT, 8])
    SP4 = c("SP4", [P, RT])
    SPT = c("SPT", [P, 4, RT])
    H0 = c("H0", [P, RT, NB])
    KVB = c("KVB", [NH, 1])
    CT = c("CT", [P, KT, NV])
    SG = c("SG", [P, KT, NV])
    ZERO = c("ZERO", [P, 1])
    TINY = c("TINY", [P, 1])
    NM = c("NM", [P, 4])
    SUM = c("SUM", [P, 4])
    RI = c("RI", [P, 4])
    CQ_OFF = c.off
    CQ = c("CQ", [P, KT, NH])
    HST = at("HST", CQ_OFF, [P, RT, NV])
    EA = c("EA", [P, P])
    BM = c("BM", [P, NB])
    MQ = c("MQ", [P, TD])
    CQS = c("CQS", [P, NB])
    LFN = c("LFN", [P, TD])
    CN = c("CN", [P, TD])
    CNM = c("CNM", [P, NB, TD])
    CQT = c("CQT", [P, NB, TD])
    CUM_OFF = c.off
    CUM = c("CUM", [NH, SEQ])
    CUMM = at("CUMM", CUM_OFF, [P, PAST + TS])
    CUMS = at("CUMS", RS_OFF, [P, PAST + TS])
    MKS = at("MKS", RS_OFF + 4 * (PAST + TS), [P, NB, TS])

    n_ = Area(O_R3, O_W)
    TN = n_("TN", [P, 2, T])
    NT = n_("NT", [P, T])
    YO_OFF = n_.off
    YO = n_("YO", [P, 2, T])
    n_.off = O_R3 + 2 * GC * TB
    SQ = n_("SQ", [P, 2, T])
    ACC = n_("ACC", [P, T])
    MWB = n_("MWB", [P, 2, KT // 2, MB * P])
    n_.off = YO_OFF
    MROW = n_("MROW", [NV, 2, MB * P])
    MWA = n_("MWA", [P, 2, KT // 2, MB * P])
    assert placed[-1] <= O_R3 + 2 * GC * TB
    MW = [MWA[:, 0], MWA[:, 1], MWB[:, 0], MWB[:, 1]]

    r = Area(O_X, O_HN)
    WU = 3 + S0 + NB * (3 + TD)
    RU = r("RU", [P, WU])
    RS1 = r("RS1", [P, T])
    RI1 = r("RI1", [P, T])
    RQ1 = r("RQ1", [P, T])
    RA1 = r("RA1", [P, T])
    B0H0 = r("B0H0", [P, NB])
    GW = r("GW", [P, 2, 2, 3, P])
    RHALO = r("RHALO", [P, RT, NB * 3])
    RST = r("RST", [P, RT, 3 * NV])
    XC = at("XC", O_R3, [P, RH, T])
    YG = at("YG", O_R3 + RH * TB, [P, RT, T])
    YH = at("YH", O_HN, [P, RT, T], F32R)
    YL = at("YL", O_HN + RT * TB, [P, RT, T], F32R)
    YHF = at("YHF", O_HN, [P, RT, T])

    def gate_buffers(half, j):
        if j % 2 == 0:
            return RS1[:], RI1[:], RQ1[:], RA1[:]
        return [(YHF if half else YG)[:, RH + n, :] for n in range(4)]


    f = Area(O_R3, O_W)
    AH = f("AH", [P, GC, T], F32R)
    AL = f("AL", [P, GC, T], F32R)
    WF = 2 + S0 + NB * (2 + TD)
    FU = f("FU", [P, 2, WF])
    FC = f("FC", [P, 2, T])
    FHALO = f("FHALO", [P, 2 * FT, NB * 2])
    FST = f("FST", [P, 2 * FT, 2 * NV])
    FCW = f("FCW", [P, 2 * FT, 4])
    XS = f("XS", [P, 2, TS])

    kv = Area(O_R3, O_W)
    STG = kv("STG", [P, 4, T])
    LZ = kv("LZ", [NH, T])
    LA = kv("LA", [NH, T])
    LE = kv("LE", [NH, T])
    LF = kv("LF", [NH, T])
    LH = kv("LH", [NH, SEQ], F32R)
    LL = kv("LL", [NH, SEQ], F32R)
    Q = at("Q", O_R3, [P, KT, T])
    OT = at("OT", O_HN, [P, KT, T])
    LOGS, MAXR = HD + 4, 98
    K1, Q1, K2, Q2 = [], [], [], []
    a, w2 = Area(O_HN + KT * TB, O_R3), Area(O_W, O_C)
    for n in range(3):
        for name, tiles_ in (("K1", K1), ("Q1", Q1), ("K2", K2), ("Q2", Q2)):
            tiles_.append((a if n < 2 else w2)(f"{name}_{n}", [P, SEQ], F32R))
    KRAW = w2("KRAW", [P, SEQ])
    QRAW = w2("QRAW", [P, SEQ])
    b = Area(O_R3 + KT * TB, O_W)
    VT = b("VT", [P, SEQ])
    V = b("V", [P, 3, KT, 2, HD + 1])
    PT = b("PT", [P, 2, SEQ])
    OSB = b("OSB", [P, SEQ])
    KEYS = PAST + TS
    a = Area(O_HN + KT * TB, O_R3)
    KB = [a("KB0", [P, KT, KEYS])[:], Q[:, :, 0:KEYS]]
    SSB = a("SSB", [P, 2, KEYS])
    SS = [SSB[:, e, :] for e in range(2)]
    VN = a("VN", [TS, D])[:]
    CUMX = [CUMM[:], a("CUMN", [P, KEYS])[:]]
    OS = a("OS", [P, D])
    b = Area(O_R3 + KT * TB, O_W)
    VB = b("VB", [P, NPG, D])
    QX = b("QX", [P, 2, KT * (P + 16)])
    PTS = b("PTS", [P, NPG + 1, P])
    LFP = CUMM[:, 0:PAST]
    OH = at("OH", O_HN + KT * TB, [P, KT, T], F32R)
    OL = at("OL", O_R3, [P, KT, T], F32R)

    PS = ctx.enter_context(nc.psum_tensor("PS", [P, 8 * 512], F32))
    SLOT = (0, 1536)

    names = """w_raw0 w_raw1 pool_hi split_done used_pe used_act used_dve ready0 ready1 free0 free1
        mw0 mw1 mw2 mw3 mw_used consts filled sigmoid silu mods_psum mods_row mods_turned mods_tile mods_done lam_exp sp_done x_in
        act_sq dve_acc dve_var act_root act_hi dve_tn dve_lo act_self dve_self
        rg_halo gate_w0 gate_w1 conv_free xc_ready act_tanh act_sqrt pair_free
        y_hi y_ready x_done x_back rst_out ffn_in ffn_out f_conv f_gelu f_prod f_hi act_ready
        kv_out0 kv_out1 kv_out2 kv_out3 lf_e lf_ready lf_out q_ready
        k_in q_in vt_in const_rows pool_self kq_ready m_hi v_turned v_used s_ready max_done mr_psum m_row
        st_ready exp_done o_psum o_free sums_inv bc_psum bc_used cum_out cq_psum cq_done
        lfp_in lfn_in kb_in0 kb_in1 vb_in new_k0 new_k1 vst_in vn_psum vn_ready qx_ready cumm_ready
        sc_psum sc_nm sc_exp sc_p sc_ptp sc_pt sc_o sc_os sc_diag sc_done sconst o_hi o_ready y_out0 y_out1""".split()
    S = {n: ctx.enter_context(nc.semaphore(n)) for n in names}

    def bc_t(ap):
        return ap.unsqueeze(2).broadcast_to([ap.shape[0], NB, TD])

    def req(ap):
        return ap.rearrange("p (b t) -> p b t", b=NB)

    def three(ap):
        return ap.rearrange("p (b x) -> p b x", b=3)

    def prompt(slot, rows=P):
        return three(PS[0:rows, SLOT[slot]:SLOT[slot] + 1536])[:, :, 0:PC]

    def sample(slot, rows=P):
        o = SLOT[slot] + 1024 + PC
        return PS[0:rows, o:o + TS]

    block = ctx.enter_context(nc.Block())

    @block.sync
    def _(sp):
        def weights(first, units, peel):
            k = 0
            if peel:
                for u in range(2):
                    sp.dma_start(WRAW[:, u, :], I["wstream"][u]).then_inc(S[f"w_raw{u}"], 16)
                k = 1
            with sp.Fori(k, units // 2) as i:
                for u in range(2):
                    sp.wait_ge(S["split_done"], first + i * 2 + u - 1)
                    sp.dma_start(WRAW[:, u, :], I["wstream"][i * 2 + first + u]).then_inc(S[f"w_raw{u}"], 16)

        for dst, src in ((CT, "cT"), (MODB, "mod_b"), (NGAIN, "gains"), (ID, "ident"), (CQ, "mask"),
                         (RGP, "rg_par"), (H0, "rg_h0"), (KVB, "kv_b"), (EA, "pick_head"), (BM, "req_rows"), (MQ, "pick_q")):
            sp.dma_start(dst[:], I[src]).then_inc(S["consts"], 16)
        for v in range(4):
            sp.dma_start(MW[v], I["mod_w"][v]).then_inc(S[f"mw{v}"], 16)
        sp.dma_start(X[:], I["xT"].rearrange("k p t -> p k t")).then_inc(S["x_in"], 16)
        with sp.Fori(1, MT // (2 * MB)) as i:
            for v in range(4):
                sp.wait_ge(S["mods_psum" if v % 2 else "mw_used"], i * 2 + (v // 2 - 1))
                sp.dma_start(MW[v], I["mod_w"][i * 4 + v]).then_inc(S[f"mw{v}"], 16)
        weights(0, UNITS_1, True)

        sp.wait_ge(S["lf_out"], 16)
        sp.wait_ge(S["cum_out"], 32)
        for k in range(NB):
            sp.dma_start(LFN[16 * k:16 * k + 16, :], O["lf"][:, S0 + TD * k:S0 + TD * k + TD])\
              .then_inc(S["lfn_in"], 16)
        for k in range(NB):
            for g in range(NPG):
                page = sp.value_load(I["page_table"][0:1, k * NPG + g:k * NPG + g + 1], min_val=0,
                                     max_val=I["cache_k"].shape[0] - 1)
                sp.dma_start(LFP[16 * k:16 * k + 16, g * PAGE:(g + 1) * PAGE],
                             I["cache_lf"][page]).then_inc(S["lfp_in"], 16)
        for n in range(4):
            sp.wait_ge(S[f"kv_out{n}"], KV_ROUNDS * 16 + 16)
        sp.wait_ge(S["q_ready"], 2)
        sp.wait_ge(S["const_rows"], 1)
        sp.dma_start(MKS[:], I["mask_new"]).then_inc(S["sconst"], 16)

        def pair_in(pair, first=False):
            for e in range(2):
                h = pair * 2 + e
                if not (first and e == 0):
                    sp.wait_ge(S["kq_ready"], h)
                sp.dma_start(KRAW[0:HD, :], O["kv"][pair, HD * e:HD * e + HD, 0:SEQ]).then_inc(S["k_in"], 16)
                for row in (HD, 98):
                    sp.dma_start(KRAW[row:row + 2, :], O["ncum"][h]).then_inc(S["k_in"], 16)
                if e == 0:
                    if not first:
                        sp.wait_ge(S["v_turned"], pair * 2)
                    sp.dma_start(VT[:], O["kv"][pair + KT, :, 0:SEQ]).then_inc(S["vt_in"], 16)

        pair_in(0, first=True)
        with sp.Fori(0, 2) as i:
            for n in range(3):
                pair_in(i * 3 + (n + 1))
        pair_in(KT - 1)

        def pages(k):
            return [sp.value_load(I["page_table"][0:1, bass.ds(k * NPG + g, 1)], min_val=0,
                                  max_val=I["cache_k"].shape[0] - 1) for g in range(NPG)]

        def keys(e, where, scored=None):
            for g, page in enumerate(where):
                if g == 0 and scored is not None:
                    sp.wait_ge(S["sc_psum"], scored)
                sp.dma_start(KB[e][:, :, g * PAGE:(g + 1) * PAGE], I["cache_k"][page]).then_inc(S[f"kb_in{e}"], 16)

        def values(where, weighed=None):
            for g, page in enumerate(where):
                if g == 0 and weighed is not None:
                    sp.wait_ge(S["sc_o"], weighed)
                sp.dma_start(VB[:, g, :], I["cache_v"][page]).then_inc(S["vb_in"], 16)

        first = pages(0)
        sp.wait_ge(S["o_psum"], NH)
        keys(0, first)
        for e in range(2):
            sp.dma_start(KB[e][:, :, PAST:KEYS], O["kv"][0:KT, :, S0:T].rearrange("k p t -> p k t"))\
              .then_inc(S[f"new_k{e}"], 16)
        sp.dma_start(OS[:, 0:KT * TS],
                     O["kv"][KT:2 * KT, :, S0:T].rearrange("k p t -> p k t")).then_inc(S["vst_in"], 16)
        keys(1, pages(1))
        values(pages(0))
        with sp.Fori(0, NB // 2 - 1) as i:
            for e in range(2):
                keys(e, pages(i * 2 + (e + 2)), i * 2 + (e + 1))
                values(pages(i * 2 + (e + 1)), i * 2 + (e + 1))
        values(pages(NB - 1), NB - 1)
        weights(UNITS_1, UNITS_2, False)

    @block.gpsimd
    def _(pool):
        pool.memset(ZERO[:], 0.0).then_inc(S["filled"], 1)
        pool.memset(ONES[:], 1.0).then_inc(S["filled"], 1)
        pool.memset(TINY[:], 1e-30).then_inc(S["filled"], 1)
        pool.wait_ge(S["filled"], 3)
        raw, hi = [Count(S["w_raw0"]), Count(S["w_raw1"])], Count(S["pool_hi"])
        used = {"A": Count(S["used_act"]), "D": Count(S["used_dve"]), "P": Count(S["used_pe"])}

        def split(u, who):
            pool.wait_ge(raw[u].sem, raw[u].next(16))
            if who:
                pool.wait_ge(used[who].sem, used[who].next())
            pool.tensor_tensor(WH[:, u, :], WRAW[:, u, :], ZERO[:].broadcast_to([P, UNIT]),
                               ALU.add).then_inc(hi.sem, 1)
            pool.wait_ge(hi.sem, hi.next())
            pool.tensor_tensor(WL[:, u, :], WRAW[:, u, :], WH[:, u, :].bitcast(F32),
                               ALU.subtract).then_inc(S["split_done"], 1)

        split(0, None)
        split(1, None)
        group = "AA" + "DD" * (KT // 4) + "AA" * (GC - 1)
        order = [("AA", RT), ("PD", KT), ("AA", GC), (group, NG - 1), ("DD", KT // 4), ("DD", 1), ("AA", KT),
                 ("AA", KT // 2 - 1), None, ("AA", 1), ("DD", KT // 2), ("AA", GC), (group, NG - 1),
                 ("DD", KT // 4 - 1)]
        assert 2 + sum(len(o[0]) * o[1] for o in order if o) == UNITS_1 + UNITS_2

        k_in, q_in, own = Count(S["k_in"]), Count(S["q_in"]), Count(S["pool_self"])
        lo_rows, hi_rows = slice(0, HD), slice(HD, P)

        def zeros(rows):
            return ZERO[rows, :].broadcast_to([rows.stop - rows.start, SEQ])

        def head_split(e, s):
            q_rows = hi_rows if e else lo_rows
            q, q1 = QRAW[q_rows, :], Q1[s]
            if e == 0:
                pool.wait_ge(q_in.sem, q_in.next())
            pool.wait_ge(k_in.sem, k_in.next(48))
            logs = slice(0, LOGS)
            for dst, x, y, op in ((K1[s][lo_rows, :], KRAW[lo_rows, :], zeros(lo_rows), ALU.add),
                                  (q1[lo_rows, :], q, zeros(q_rows), ALU.add),
                                  (K2[s][logs, :], KRAW[logs, :], zeros(logs), ALU.add),
                                  (q1[hi_rows, :], q, zeros(q_rows), ALU.add),
                                  (Q2[s][HD:LOGS, :], KRAW[96:100, :], zeros(slice(96, 100)), ALU.add),
                                  (Q2[s][lo_rows, :], q, q1[q_rows, :].bitcast(F32), ALU.subtract)):
                pool.tensor_tensor(dst, x, y, op).then_inc(own.sem, 1)
                pool.wait_ge(own.sem, own.next())
            pool.tensor_tensor(K1[s][hi_rows, :], KRAW[lo_rows, :], K1[s][lo_rows, :].bitcast(F32), ALU.subtract)\
                .then_inc(S["kq_ready"], 1)

        def attention_splits():
            st = Count(S["st_ready"], 1)
            head_split(0, 0)
            head_split(1, 1)
            with rounds(pool, 2, {k_in: 288, q_in: 3, own: 36, st: 6 * KT}):
                for n in range(6):
                    pool.wait_ge(st.sem, st.now())
                    st.next(KT)
                    head_split(n % 2, (2 + n) % 3)
            for n in range(2):
                pool.wait_ge(st.sem, st.now())
                st.next(KT)
                head_split(n, (2 + n) % 3)

        for item in order:
            if item is None:
                attention_splits()
                continue
            whos, n = item
            with rounds(pool, n, {raw[0]: 8 * len(whos), raw[1]: 8 * len(whos), hi: len(whos)}
                        | {used[w_]: whos.count(w_) for w_ in set(whos)}):
                for u, who in enumerate(whos):
                    split(u % 2, who)

    @block.tensor
    def _(pe):
        split = Count(S["split_done"])
        free = [Count(S["free0"]), Count(S["free1"])]
        ready = [S["ready0"], S["ready1"]]
        acc, hn = Count(S["dve_acc"], 2), Count(S["dve_lo"], 1)
        act_chunk = Count(S["act_ready"], 1)

        def tiles(t, u):
            return lambda n: t[:, u, n * P:(n + 1) * P]

        def job(slot, wh, wl, xh, xl, kts, first=True, last=True, fresh=None):
            for n, k in enumerate(kts):
                if fresh:
                    pe.wait_ge(fresh.sem, fresh.next())
                for m, (lhs, rhs) in enumerate(((wh, xh), (wh, xl), (wl, xh))):
                    for c, (lo, hi) in enumerate(PIECES):
                        o = SLOT[slot] + 512 * c
                        mm = pe.matmul(PS[:, o:o + hi - lo], lhs(n), rhs[:, k, lo:hi],
                                       start=first and n == 0 and m == 0,
                                       stop=last and n == len(kts) - 1 and m == 2)
            return mm

        def unit_job(u, xh, xl, fresh=None):
            pe.wait_ge(split.sem, split.next())
            pe.wait_ge(free[u].sem, free[u].next())
            job(u, tiles(WH, u), tiles(WL, u), xh, xl, range(KT), fresh=fresh).then_inc(ready[u], 1)

        def proj(xh, xl, pairs, fresh=None):
            if fresh:
                unit_job(0, xh, xl, fresh)
                unit_job(1, xh, xl)
                pairs -= 1
            with rounds(pe, pairs, {split: 2, free[0]: 1, free[1]: 1}):
                for u in range(2):
                    unit_job(u, xh, xl)

        def norm():
            pe.wait_ge(acc.sem, acc.next(KT))
            pe.wait_ge(free[0].sem, free[0].next())
            for c, (lo, hi) in enumerate(PIECES):
                mm = pe.matmul(PS[:, 512 * c:512 * c + hi - lo], ONES[:], ACC[:, lo:hi], start=True, stop=True)
            mm.then_inc(ready[0], 1)

        mod_rows = Count(S["mods_row"])
        mwi = [Count(S[f"mw{v}"]) for v in range(4)]

        def mod_block(e):
            for h in range(2):
                v = 2 * e + h
                pe.wait_ge(mwi[v].sem, mwi[v].next(16))
                for k in range(KT // 2):
                    mm = pe.matmul(PS[0:NV, 3072 + 512 * e:3584 + 512 * e], CT[:, h * KT // 2 + k, :], MW[v][:, k, :],
                                   start=(h + k == 0), stop=(h == 1 and k == KT // 2 - 1))
                mm.then_inc(S["mods_psum"] if h else S["mw_used"], 1)

        def mod_turn(e):
            pe.wait_ge(mod_rows.sem, mod_rows.next())
            for m in range(MB):
                mm = pe.matmul(PS[:, 2048 + 512 * e + m * NV:2048 + 512 * e + (m + 1) * NV],
                               MROW[:, e, m * P:(m + 1) * P], ID[0:NV, 0:NV], start=True, stop=True)
            mm.then_inc(S["mods_turned"], 1)

        pe.wait_ge(S["silu"], 1)
        mod_block(0)
        for trips in (MODS_BEFORE, MT // (2 * MB) - 1 - MODS_BEFORE):
            with rounds(pe, trips, {mod_rows: 2} | {w_: 16 for w_ in mwi}):
                mod_block(1)
                mod_turn(0)
                mod_block(0)
                mod_turn(1)
            if trips == MODS_BEFORE:
                norm()
        mod_block(1)
        mod_turn(0)
        mod_turn(1)
        gate_w, xc = [Count(S["gate_w0"]), Count(S["gate_w1"])], Count(S["xc_ready"])
        for half in range(2):
            proj(HH, HL, RH, None if half else hn)
            for j in range(RH):
                kk = [k - RH * half for k in GATE_IN[RH * half + j]]
                pe.wait_ge(xc.sem, RH * half + max(kk) + 1)
                gw = gate_w[(RH * half + j) % 2]
                pe.wait_ge(gw.sem, gw.next(16))
                for u in range(2):
                    pe.wait_ge(free[u].sem, free[u].next())
                    for n, k in enumerate(kk):
                        for c, (lo, hi) in enumerate(PIECES):
                            mm = pe.matmul(PS[:, SLOT[u] + 512 * c:SLOT[u] + 512 * c + hi - lo], GW[:, (RH * half + j) % 2, u, n, :],
                                           XC[:, k, lo:hi], start=(n == 0), stop=(n == len(kk) - 1))
                    mm.then_inc(ready[u], 1)
        y = Count(S["y_ready"])

        def out_pair(fresh=None):
            for s in range(2):
                pe.wait_ge(free[s].sem, free[s].next())
                for u in range(2):
                    pe.wait_ge(split.sem, split.next())
                    mm = job(s, tiles(WH, u), tiles(WL, u), YH, YL, range(5 * u, 5 * u + 5), u == 0, u == 1,
                             fresh if s == 0 else None)
                    if u == 1:
                        mm.then_inc(ready[s], 1)
                    else:
                        pe.drain().then_inc(S["used_pe"], 1)

        out_pair(y)
        with rounds(pe, KT // 2 - 1, {split: 4, free[0]: 1, free[1]: 1}):
            out_pair()

        def ffn():
            def up(pairs, fresh=None):
                proj(HH, HL, pairs, fresh)

            def down():
                chunks = act_chunk.next(GC)
                with rounds(pe, 2, {split: 2, free[0]: 2, free[1]: 2}):
                    pe.wait_ge(act_chunk.sem, chunks)
                    for u in range(2):
                        pe.wait_ge(split.sem, split.next())
                        for s in range(2):
                            pe.wait_ge(free[s].sem, free[s].next())
                            job(s, lambda n: WH[:, u, (s * GC + n) * P:(s * GC + n + 1) * P],
                                lambda n: WL[:, u, (s * GC + n) * P:(s * GC + n + 1) * P],
                                AH, AL, range(GC)).then_inc(ready[s], 1)
            up(GC, hn)
            with rounds(pe, NG - 1, {split: 12, free[0]: 8, free[1]: 8, act_chunk: GC}):
                for u in range(2):
                    unit_job(u, HH, HL)
                down()
                up(GC - 1)
            down()

        norm()
        ffn()
        norm()
        pe.wait_ge(split.sem, split.next())
        pe.wait_ge(free[0].sem, free[0].next())
        job(0, tiles(WH, 0), tiles(WL, 0), HH, HL, range(KT), fresh=hn).then_inc(ready[0], 1)
        split.next()
        proj(HH, HL, KT)
        proj(HH, HL, KT // 2, hn)

        mx, bcu, vu, o_free = (Count(S[n]) for n in ("max_done", "bc_used", "v_used", "o_free"))
        mrow, expd, kq, inv, vt = (Count(S[n]) for n in ("m_row", "exp_done", "kq_ready", "sums_inv", "vt_in"))
        bank1 = None

        def take_bank1(reader=None):
            nonlocal bank1
            if bank1:
                pe.wait_ge(bank1.sem, bank1.next())
            bank1 = reader

        def maxima(s, qi):
            L = (qi + 1) * P
            q = slice(qi * P, qi * P + P)
            if qi == KT - 1:
                pe.wait_ge(kq.sem, kq.next())
                take_bank1()
            for lo in range(0, L, 512):
                hi = min(L, lo + 512)
                pe.matmul(PS[:, lo:hi], Q1[s][:, q], K1[s][:, lo:hi], start=True, stop=False)
                pe.matmul(PS[:, lo:hi], Q2[s][0:LOGS, q], K2[s][0:LOGS, lo:hi], start=False, stop=True)
            pe.matmul(PS[:, L - P:L], IDB[:], MSKB[:], start=False, stop=True, skip_group_check=True)\
              .then_inc(S["s_ready"], 1)

        def max_row(e, qi):
            pe.wait_ge(mx.sem, mx.next())
            mm = pe.matmul(PS[96:MAXR, 3072 + qi * P:3072 + (qi + 1) * P],
                           CQ[:, qi, 2 * e:2 * e + 2], ID[:],
                           start=True, stop=True, skip_group_check=True)
            if qi in (0, KT // 2):
                mm.then_inc(S["mr_psum"], 1)

        def exponents(s, kt):
            L, o = SEQ - kt * P, 1024 + 1024 * (kt % 2)
            k = slice(kt * P, kt * P + P)
            if kt == 0:
                pe.wait_ge(mrow.sem, mrow.next(2))
            for lo in range(0, L, 512):
                hi = min(L, lo + 512)
                pe.matmul(PS[:, o + lo:o + hi], K1[s][:, k], Q1[s][:, kt * P + lo:kt * P + hi], start=True, stop=False)
                pe.matmul(PS[:, o + lo:o + hi], K2[s][0:MAXR, k], Q2[s][0:MAXR, kt * P + lo:kt * P + hi],
                          start=False, stop=True)
            pe.matmul(PS[:, o:o + P], MSKB[:], IDB[:], start=False, stop=True, skip_group_check=True)\
              .then_inc(S["st_ready"], 1)

        def weigh(pair3, e, kt, first):
            pe.wait_ge(expd.sem, expd.next())
            if kt == 0 and not first:
                pe.wait_ge(o_free.sem, o_free.next())
            for lo, hi in ((kt * P, 512), (max(kt * P, 512), SEQ)):
                if lo < hi:
                    mm = pe.matmul(PS[0:HD + 1, 3072 + lo:3072 + hi], V[:, pair3, kt, e, :],
                                   PT[:, kt % 2, lo - kt * P:hi - kt * P], start=(kt == 0),
                                   stop=True, skip_group_check=True)
            if kt == KT - 1:
                mm.then_inc(S["o_psum"], 1)

        def turn_values(half):
            if half == 0:
                pe.wait_ge(vt.sem, vt.next(16))
            take_bank1(vu)
            for k in range(4):
                mm = pe.transpose(PS[:, 512 + k * P:512 + (k + 1) * P],
                                  VT[:, (half * 4 + k) * P:(half * 4 + k + 1) * P], ID[:])
            mm.then_inc(S["v_turned"], 1)

        def spread(half):
            pe.wait_ge(inv.sem, inv.next())
            take_bank1(bcu)
            pe.matmul(PS[0:HD, 512:1024], ONES[HD:HD + 1, 0:HD], OSB[HD:HD + 1, 512 * half:512 * half + 512],
                      start=True, stop=True).then_inc(S["bc_psum"], 1)

        def heads(count, base, first=False, last=False):
            for n in range(count):
                h = base + n
                ahead = not (last and n == count - 1)
                behind = not (first and n == 0)
                for j in range(KT):
                    exponents(h % 3, j)
                    if ahead:
                        if j:
                            max_row((h + 1) % 2, KT - j)
                        maxima((h + 1) % 3, KT - 1 - j)
                    if j:
                        weigh(h // 2 % 3, h % 2, j - 1, not behind)
                    if j in (4, 6) and h % 2 and ahead:
                        turn_values((j - 4) // 2)
                    if j in (5, 7) and behind:
                        spread((j - 5) // 2)
                if ahead:
                    max_row((h + 1) % 2, 0)
                weigh(h // 2 % 3, h % 2, KT - 1, False)

        pe.wait_ge(S["q_ready"], 2)
        turn_values(0)
        turn_values(1)
        take_bank1()
        for qi in range(KT - 1, -1, -1):
            maxima(0, qi)
            max_row(0, qi)
        heads(2, 0, first=True)
        with rounds(pe, 2, {mx: 48, bcu: 12, vu: 6, o_free: 6, mrow: 12, expd: 48, kq: 6, inv: 12, vt: 48}):
            heads(6, 2)
        heads(2, 2, last=True)
        pe.wait_ge(S["vst_in"], 16)
        for k in range(KT):
            mm = pe.transpose(PS[0:TS, 2048 + k * P:2048 + (k + 1) * P], OS[:, k * TS:(k + 1) * TS], ID[:])
        mm.then_inc(S["vn_psum"], 1)
        spread(0)
        spread(1)
        take_bank1()

        pe.wait_ge(S["cumm_ready"], 1)
        pe.matmul(PS[:, 0:TS], EA[:], CNM[:].rearrange("p b t -> p (b t)"), start=True, stop=True)\
          .then_inc(S["cq_psum"], 1)
        pe.wait_ge(S["cq_done"], 1)
        pe.wait_ge(S["vn_ready"], 1)
        for e in range(2):
            pe.wait_ge(S[f"new_k{e}"], 16)
        vbi, qx, scp, scpt, outs, turned_back = (Count(S[n]) for n in ("vb_in", "qx_ready", "sc_p", "sc_pt", "sc_done",
                                                                       "sc_os"))
        kbi = [Count(S["kb_in0"]), Count(S["kb_in1"])]
        HALF = KEYS // 2

        def scores(e, ks):
            if ks[0] == 0:
                pe.wait_ge(kbi[e].sem, kbi[e].next(64))
                pe.wait_ge(qx.sem, qx.next())
            for k in ks:
                for h in range(2):
                    o = 1024 * e + 512 * h
                    pe.matmul(PS[:, o:o + HALF], QX[:, e, k * P:(k + 1) * P], KB[e][:, k, h * HALF:(h + 1) * HALF],
                              start=(k == 0), stop=False)
            if ks[-1] == KT - 1:
                for h in range(2):
                    o = 1024 * e + 512 * h
                    mm = pe.matmul(PS[:, o:o + HALF], EA[:], CUMX[e][:, h * HALF:(h + 1) * HALF], start=False, stop=True)
                mm.then_inc(S["sc_psum"], 1)

        def turn(e, drawn=True):
            pe.wait_ge(scp.sem, scp.next())
            if drawn:
                pe.wait_ge(outs.sem, outs.next())
            for k in range(NPG):
                pe.transpose(PS[:, 2048 + k * P:2048 + (k + 1) * P], SS[e][:, k * P:(k + 1) * P], ID[:])
            pe.transpose(PS[0:TS, 2560:2560 + P], SS[e][:, PAST:KEYS], ID[:]).then_inc(S["sc_ptp"], 1)

        def weigh_all():
            pe.wait_ge(vbi.sem, vbi.next(64))
            for g in range(NPG):
                for h in range(2):
                    pe.matmul(PS[:, 3072 + 512 * h:3584 + 512 * h], PTS[:, g, :], VB[:, g, 512 * h:512 * h + 512],
                              start=(g == 0), stop=False)
            for h in range(2):
                mm = pe.matmul(PS[:, 3072 + 512 * h:3584 + 512 * h], PTS[0:TS, NPG, :], VN[:, 512 * h:512 * h + 512],
                               start=False, stop=True)
            mm.then_inc(S["sc_o"], 1)

        def own_heads():
            pe.wait_ge(turned_back.sem, turned_back.next())
            for k in range(KT):
                mm = pe.matmul(PS[:, 2560 + 16 * k:2576 + 16 * k], OS[:, k * P:(k + 1) * P], ID[:, 16 * k:16 * k + 16],
                               start=True, stop=True)
            mm.then_inc(S["sc_diag"], 1)

        def request(e, first=False, last=False, second=False):
            if not last:
                scores(1 - e, range(0, KT // 2))
            turn(e, drawn=not (first or second))
            if not last:
                scores(1 - e, range(KT // 2, KT))
            pe.wait_ge(scpt.sem, scpt.next())
            if not first:
                own_heads()
            weigh_all()

        scores(0, range(KT))
        request(0, first=True)
        request(1, second=True)
        with rounds(pe, NB // 2 - 2, {kbi[0]: 64, kbi[1]: 64, vbi: 128, qx: 2, scp: 2, scpt: 2, outs: 2, turned_back: 2}):
            for e in range(2):
                request(e)
        request(0)
        request(1, last=True)
        pe.wait_ge(outs.sem, outs.next())
        own_heads()
        pe.wait_ge(S["sc_done"], NB)
        pe.wait_ge(S["o_ready"], KT)
        proj(OH, OL, KT // 2)
        norm()
        ffn()
        norm()

    @block.scalar
    def _(act):
        ready, free = [Count(S["ready0"]), Count(S["ready1"])], [S["free0"], S["free1"]]
        sq_free, x_done, var, tn = Count(S["dve_acc"]), Count(S["x_done"]), Count(S["dve_var"]), Count(S["dve_tn"])
        me = Count(S["act_self"])
        for n in range(4):
            act.sem_inc(S[f"kv_out{n}"], 16)

        def chain(ins):
            ins.then_inc(me.sem, 1)
            act.wait_ge(me.sem, me.next())

        def got(s):
            act.wait_ge(ready[s].sem, ready[s].next())
            act.sem_inc(S["used_act"], 1)

        def squares(made=None):
            with rounds(act, KT // 2, {sq_free: 2} | ({made: 2} if made else {})) as i:
                for u in range(2):
                    if made:
                        act.wait_ge(made.sem, made.next())
                    act.wait_ge(sq_free.sem, sq_free.next())
                    act.activation(SQ[:, u, :], X[:, i * 2 + u, :], ACT.Square).then_inc(S["act_sq"], 1)

        def norm(n, sums=True):
            if sums:
                ready[0].next()
                act.wait_ge(var.sem, var.next())
                chain(act.activation(RS[:], ACC[:], ACT.Ln))
                act.activation(RS[:], RS[:], ACT.Exp, scale=-0.5).then_inc(S["act_root"], 1)
            if NORMS[n]:
                sh, sc = NORMS[n]
                with rounds(act, KT // 2, {tn: 2}) as i:
                    for u in range(2):
                        act.wait_ge(tn.sem, tn.next())
                        par = dict(scale=MOD[:, sc + u + i * 2, 0:1], bias=MOD[:, sh + u + i * 2, 0:1])
                        act.activation(HH[:, i * 2 + u, 0:S0], TN[:, u, 0:S0], ACT.Identity, **par)
                        act.activation(HH[:, i * 2 + u, S0:T], TN[:, u, S0:T], ACT.Copy)
                        act.activation(TN[:, u, 0:S0], TN[:, u, 0:S0], ACT.Identity, **par)\
                           .then_inc(S["act_hi"], 1)

        act.wait_ge(S["consts"], 16 * N_CONSTS)
        act.wait_ge(S["filled"], 3)
        act.activation(SG[:], CT[:], ACT.Sigmoid).then_inc(S["sigmoid"], 1)
        chain(act.activation(SPT[:, 0, :], RGP[:, :, 7], ACT.Abs))
        act.activation(SPT[:, 1, :], SPT[:, 0, :], ACT.Exp, scale=-1.0).then_inc(S["lam_exp"], 1)
        act.wait_ge(S["x_in"], 16)
        squares()
        norm(0)
        act.dma_start(RHALO[:], I["rg_halo"]).then_inc(S["rg_halo"], 16)
        act.wait_ge(S["rg_halo"], 16)
        conv_free, pair_free, tanh_ = Count(S["conv_free"]), Count(S["pair_free"]), Count(S["act_tanh"])
        for jt in range(2):
            act.dma_start(GW[:, jt], I["rg_gate_w"][jt]).then_inc(S[f"gate_w{jt}"], 16)
        for half in range(2):
            if half:
                act.wait_ge(S["pair_free"], 2 + RH - 1)
            with rounds(act, RH, {ready[0]: 1, ready[1]: 1, conv_free: 1}) as j:
                got(0)
                act.wait_ge(conv_free.sem, conv_free.next())
                act.activation(three(RU[:, 3:3 + S0]), prompt(0), ACT.Copy)
                ru = RU[:, 3 + S0:WU].rearrange("p (b t) -> p b t", b=NB)
                act.activation(ru[:, :, 0:3], RHALO[:, j + RH * half, :].rearrange("p (b t) -> p b t", b=NB), ACT.Copy)
                act.activation(ru[:, :, 3:3 + TD], req(sample(0)), ACT.Copy).then_inc(free[0], 1)
                got(1)
                act.activation(three(YG[:, j + RH * half, 0:S0]), prompt(1), ACT.Gelu_apprx_tanh)
                act.activation(YG[:, j + RH * half, S0:T], sample(1), ACT.Gelu_apprx_tanh).then_inc(free[1], 1)
            for j in range(RH):
                jt = RH * half + j
                act.wait_ge(pair_free.sem, pair_free.next())
                act.wait_ge(ready[0].sem, ready[0].next())
                rs, ri, rq, ra = gate_buffers(half, j)
                act.activation(three(rs[:, 0:S0]), prompt(0), ACT.Sigmoid, bias=RGP[:, jt, 5:6])
                act.activation(rs[:, S0:T], sample(0), ACT.Sigmoid, bias=RGP[:, jt, 5:6]).then_inc(free[0], 1)
                act.wait_ge(ready[1].sem, ready[1].next())
                act.activation(three(ri[:, 0:S0]), prompt(1), ACT.Sigmoid, bias=RGP[:, jt, 6:7])
                act.activation(ri[:, S0:T], sample(1), ACT.Sigmoid, bias=RGP[:, jt, 6:7]).then_inc(free[1], 1)
                if jt + 2 < RT:
                    act.dma_start(GW[:, jt % 2], I["rg_gate_w"][jt + 2]).then_inc(S[f"gate_w{jt % 2}"], 16)
                act.wait_ge(free[0], ready[0].now() + 1)
                act.wait_ge(free[1], ready[1].now() + 1)
                act.wait_ge(S["sp_done"], 1)
                chain(act.activation(ra, rs, ACT.Exp, scale=SPT[:, 1, jt:jt + 1]))
                act.activation(rs, rs, ACT.Tanh, scale=SP4[:, jt:jt + 1]).then_inc(tanh_.sem, 1)
                act.wait_ge(tanh_.sem, tanh_.next())
                act.activation(rq, rs, ACT.Sqrt, bias=TINY[:]).then_inc(S["act_sqrt"], 1)
                if half:
                    act.activation(YH[:, j, :], YG[:, j, :], ACT.Copy).then_inc(S["y_hi"], 1)
        act.wait_ge(pair_free.sem, pair_free.next(2))
        act.dma_start(O["rst"], RST[:]).then_inc(S["rst_out"], 16)
        act.dma_start(O["hst"], HST[:]).then_inc(S["rst_out"], 16)
        with act.Fori(RH, RT) as k:
            act.activation(YH[:, k, :], YG[:, k, :], ACT.Copy).then_inc(S["y_hi"], 1)
        act.wait_ge(S["rst_out"], 32)
        act.dma_start(X[:], I["xT"].rearrange("k p t -> p k t")).then_inc(S["x_back"], 16)
        for s in range(2):
            ready[s].next(KT // 2)

        act_rdy = Count(S["act_ready"])
        conv, prod = Count(S["f_conv"]), Count(S["f_prod"])
        loads, stores = Count(S["ffn_in"]), Count(S["ffn_out"])

        def ffn(layer):
            def chunk(n, c):
                act.wait_ge(act_rdy.sem, act_rdy.next())
                for s in range(2):
                    got(s)
                    fu = FU[:, s, 2 + S0:WF].rearrange("p (b t) -> p b t", b=NB)
                    act.activation(three(FU[:, s, 2:2 + S0]), prompt(s), ACT.Copy)
                    act.activation(fu[:, :, 2:2 + TD], req(sample(s)), ACT.Copy)
                    act.activation(fu[:, :, 0:2], FHALO[:, n + FT * s, :].rearrange("p (b t) -> p b t", b=NB), ACT.Copy)
                    par = dict(scale=FCW[:, n + FT * s, 2:3], bias=FCW[:, n + FT * s, 3:4])
                    act.activation(three(FC[:, s, 0:S0]), prompt(s), ACT.Identity, **par)
                    act.activation(FC[:, s, S0:T], sample(s), ACT.Identity, **par).then_inc(free[s], 1)
                act.wait_ge(conv.sem, conv.next())
                act.activation(FC[:, 0, :], FC[:, 0, :], ACT.Gelu_apprx_tanh).then_inc(S["f_gelu"], 1)
                act.wait_ge(prod.sem, prod.next())
                act.activation(AH[:, c, :], FC[:, 0, :], ACT.Copy).then_inc(S["f_hi"], 1)

            def down():
                for s in range(2):
                    ready[s].next(KT // 2)
            act.dma_start(FHALO[:], I["ffn_halo"][layer]).then_inc(S["ffn_in"], 16)
            act.dma_start(FCW[:], I["ffn_par"][layer]).then_inc(S["ffn_in"], 16)
            norm(1 if layer == 0 else 4)
            act.wait_ge(loads.sem, loads.next(32))
            ones = {ready[0]: 1, ready[1]: 1, act_rdy: 1, conv: 1, prod: 1}
            with rounds(act, GC, ones) as c:
                chunk(c, c)
            with rounds(act, NG - 1, {ready[0]: 8, ready[1]: 8, act_rdy: GC, conv: GC, prod: GC}) as g:
                chunk(g * GC + GC, 0)
                down()
                with rounds(act, GC - 1, ones) as c:
                    chunk(g * GC + c + (GC + 1), c + 1)
            down()
            x_done.next((NG - 1) * KT)
            squares(x_done)
            act.dma_start(O["fst"][layer], FST[:]).then_inc(S["ffn_out"], 16)
            act.wait_ge(stores.sem, stores.next(16))

        squares(x_done)
        ffn(0)
        norm(2)
        ready[0].next()
        act.wait_ge(free[0], ready[0].now() + 1)
        chain(act.activation(LA[:], LZ[:], ACT.Abs))
        chain(act.activation(LE[:], LA[:], ACT.Exp, scale=-1.0))
        act.activation(LE[:], LE[:], ACT.Ln, bias=ONES[0:NH, 0:1]).then_inc(S["lf_e"], 1)
        act.wait_ge(S["lf_ready"], 1)
        act.dma_start(O["lf"], LF[:]).then_inc(S["lf_out"], 16)
        act.wait_ge(S["lf_ready"], 4)
        act.dma_start(O["ncum"][:, 0, :], LH[:].bitcast(F32)).then_inc(S["cum_out"], 16)
        act.dma_start(O["ncum"][:, 1, :], LL[:].bitcast(F32)).then_inc(S["cum_out"], 16)
        out = [Count(S[f"kv_out{n}"]) for n in range(4)]
        per = {ready[0]: 2, ready[1]: 2, me: 4} | {o: 16 for o in out}
        with rounds(act, KV_ROUNDS, per) as i:
            for n in range(4):
                s = n % 2
                got(s)
                act.wait_ge(out[n].sem, out[n].next(16))
                act.activation(three(STG[:, n, 0:S0]), prompt(s), ACT.Copy)
                act.activation(STG[:, n, S0:T], sample(s), ACT.Copy).then_inc(me.sem, 1)
                act.wait_ge(me.sem, me.next())
                act.sem_inc(free[s], 1)
                act.dma_start(O["kv"][i * 4 + n], STG[:, n, :]).then_inc(out[n].sem, 16)
        for n in range(4):
            act.wait_ge(out[n].sem, out[n].next(16))
        act.wait_ge(S["lf_out"], 16)
        norm(3, sums=False)
        act.wait_ge(S["dve_lo"], 4 * KT + 1)
        with rounds(act, KT // 2, {ready[0]: 1, ready[1]: 1}) as i:
            for s in range(2):
                got(s)
                act.activation(three(Q[:, i * 2 + s, 0:S0]), prompt(s), ACT.Copy, scale=float(HD) ** -0.5)
                act.activation(Q[:, i * 2 + s, S0:T], sample(s), ACT.Copy, scale=float(HD) ** -0.5).then_inc(free[s], 1)
        act.drain().then_inc(S["q_ready"], 2)

        st, mr, vturn = Count(S["st_ready"]), Count(S["mr_psum"]), Count(S["v_turned"])

        def turned_values(par, half):
            act.wait_ge(vturn.sem, vturn.next())
            act.activation(V[:, par, 4 * half:4 * half + 4, :, 0:HD],
                           PS[:, 512:1024].rearrange("p (k e c) -> p k e c", k=4, e=2), ACT.Copy)\
               .then_inc(S["v_used"], 1)

        def max_hi(half):
            act.wait_ge(mr.sem, mr.next())
            cols = slice(512 * half, 512 * half + 512)
            act.activation(OSB[96:MAXR, cols].bitcast(F32R), PS[96:MAXR, 3072 + 512 * half:3584 + 512 * half],
                           ACT.Copy).then_inc(S["m_hi"], 1)

        kq = Count(S["kq_ready"])

        def pair_queries(pair):
            act.activation(QRAW[:], Q[:, pair, 0:SEQ], ACT.Copy).then_inc(S["q_in"], 1)

        def heads(count, base, pair, last=False):
            for n in range(count):
                h = base + n
                ahead = not (last and n == count - 1)
                for j in range(KT):
                    L, o = SEQ - j * P, 1024 + 1024 * (j % 2)
                    act.wait_ge(st.sem, st.next())
                    act.activation(PT[:, j % 2, 0:L], PS[:, o:o + L], ACT.Exp).then_inc(S["exp_done"], 1)
                    if j == 0 and h % 2 == 0 and not last:
                        act.wait_ge(kq.sem, kq.next(2))
                        pair_queries(pair + (n // 2 + 1))
                    if j == 4 and ahead:
                        max_hi(1)
                    if j in (5, 7) and h % 2 and ahead:
                        turned_values((h // 2 + 1) % 3, (j - 5) // 2)
                if ahead:
                    max_hi(0)

        act.wait_ge(S["const_rows"], 1)
        pair_queries(0)
        turned_values(0, 0)
        turned_values(0, 1)
        max_hi(1)
        max_hi(0)
        heads(2, 0, 0)
        with rounds(act, 2, {st: 48, mr: 12, vturn: 6, kq: 6}) as i:
            heads(6, 2, i * 3 + 1)
        heads(2, 2, KT - 1, last=True)

        act.wait_ge(S["vn_psum"], 1)
        act.activation(VN, PS[0:TS, 2048:2048 + D], ACT.Copy).then_inc(S["vn_ready"], 1)
        nm, scp, sco = Count(S["sc_nm"]), Count(S["sc_ptp"]), Count(S["sc_o"])

        def exps(e):
            act.wait_ge(nm.sem, nm.next())
            act.activation(SS[e], SS[e], ACT.Exp, bias=NM[:, e:e + 1], accum_out=SUM[:, e:e + 1])\
               .then_inc(S["sc_exp"], 1)

        def turned():
            act.wait_ge(scp.sem, scp.next())
            act.activation(PTS[:, 0:NPG, :].rearrange("p g q -> p (g q)"), PS[:, 2048:2048 + PAST], ACT.Copy)
            act.activation(PTS[0:TS, NPG, :], PS[0:TS, 2560:2560 + P], ACT.Copy).then_inc(S["sc_pt"], 1)

        def weighed():
            act.wait_ge(sco.sem, sco.next())
            act.activation(OS[:], PS[:, 3072:4096], ACT.Copy).then_inc(S["sc_os"], 1)

        exps(0)
        with rounds(act, NB // 2 - 1, {nm: 2, scp: 2, sco: 2}):
            for e in range(2):
                turned()
                exps(1 - e)
                weighed()
        turned()
        exps(1)
        weighed()
        turned()
        weighed()
        act.wait_ge(S["sc_done"], NB)
        with act.Fori(0, KT) as k:
            act.activation(OH[:, k, :], OT[:, k, :], ACT.Copy).then_inc(S["o_hi"], 1)
        for s in range(2):
            ready[s].next(KT // 2)
        act.wait_ge(S["o_ready"], KT)
        squares(x_done)
        ffn(1)
        norm(5)
        hi, yo = Count(S["act_hi"], 5 * KT), [Count(S["y_out0"]), Count(S["y_out1"])]
        for u in range(2):
            act.sem_inc(yo[u].sem, 16)
        with rounds(act, KT // 2, {tn: 2, hi: 2, yo[0]: 16, yo[1]: 16}) as i:
            for u in range(2):
                act.wait_ge(tn.sem, tn.next())
                act.wait_ge(yo[u].sem, yo[u].next(16))
                act.activation(YO[:, u, :], TN[:, u, :], ACT.Copy, scale=NGAIN[:, 5, bass.ds(i * 2 + u, 1)])\
                   .then_inc(hi.sem, 1)
                act.wait_ge(hi.sem, hi.next())
                act.dma_start(O["yT"][i * 2 + u], YO[:, u, :]).then_inc(yo[u].sem, 16)
        for u in range(2):
            act.wait_ge(yo[u].sem, yo[u].next(16))

    @block.vector
    def _(dve):
        ready, free = [Count(S["ready0"]), Count(S["ready1"])], [S["free0"], S["free1"]]
        sq, root, hi = Count(S["act_sq"]), Count(S["act_root"]), Count(S["act_hi"])
        accs, los = Count(S["dve_acc"], 2), Count(S["dve_lo"], 1)
        me = Count(S["dve_self"])
        TT, TSC, STT = dve.tensor_tensor, dve.tensor_scalar, dve.scalar_tensor_tensor

        def chain(ins):
            ins.then_inc(me.sem, 1)
            dve.wait_ge(me.sem, me.next())

        def got(s):
            dve.wait_ge(ready[s].sem, ready[s].next())

        def add_square(u):
            dve.wait_ge(sq.sem, sq.next())
            TT(ACC[:], ACC[:], SQ[:, u, :], ALU.add).then_inc(accs.sem, 1)
            dve.wait_ge(accs.sem, accs.next())

        def rms():
            got(0)
            TSC(three(ACC[:, 0:S0]), prompt(0), 1.0 / D, EPS, ALU.mult, ALU.add)
            TSC(ACC[:, S0:T], sample(0), 1.0 / D, EPS, ALU.mult, ALU.add).then_inc(S["dve_var"], 1)
            dve.wait_ge(var.sem, var.next())
            dve.sem_inc(free[0], 1)
            dve.wait_ge(root.sem, root.next())
            chain(STT(NT[:], RS[:], -0.5, RS[:], ALU.mult, ALU.mult))
            chain(TT(NT[:], NT[:], ACC[:], ALU.mult))
            chain(STT(RS[:], NT[:], 1.5, RS[:], ALU.add, ALU.mult))

        def normed(n, k, u):
            if not NORMS[n]:
                TT(TN[:, u, :], X[:, k, :], RS[:], ALU.mult).then_inc(S["dve_tn"], 1)
                return
            dve.wait_ge(los.sem, los.now())
            sh, sc = NORMS[n]
            chain(TT(TN[:, u, :], X[:, k, :], RS[:], ALU.mult))
            s = req(TN[:, u, S0:T])
            chain(TT(s, s, bc_t(MOD[:, sc + k, 1:NV]), ALU.mult))
            TT(s, s, bc_t(MOD[:, sh + k, 1:NV]), ALU.add).then_inc(S["dve_tn"], 1)

        def low(n, k, u):
            dve.wait_ge(hi.sem, hi.next())
            if NORMS[n]:
                TT(HL[:, k, :], TN[:, u, :], HH[:, k, :].bitcast(F32), ALU.subtract).then_inc(los.sem, 1)
                los.next()

        def norm(n, sums=True):
            if sums:
                rms()
            m = 2 if NORMS[n] else 0
            normed(n, 0, 0)
            with rounds(dve, KT // 2 - 1, {me: 2 * m, hi: 2, los: m}) as i:
                normed(n, i * 2 + 1, 1)
                low(n, i * 2, 0)
                normed(n, i * 2 + 2, 0)
                low(n, i * 2 + 1, 1)
            normed(n, KT - 1, 1)
            low(n, KT - 2, 0)
            low(n, KT - 1, 1)

        def residual(s, k, gate, per_unit=1):
            got(s)
            if s == 1 or per_unit == 1:
                dve.sem_inc(S["used_dve"], 1)
            TT(req(XS[:, s, :]), req(sample(s)), bc_t(MOD[:, gate + k, 1:NV]), ALU.mult)\
              .then_inc(me.sem, 1)
            STT(three(X[:, k, 0:S0]), prompt(s), MOD[:, gate + k, 0:1], three(X[:, k, 0:S0]),
                ALU.mult, ALU.add).then_inc(free[s], 1)
            dve.wait_ge(me.sem, me.next())
            TT(X[:, k, S0:T], X[:, k, S0:T], XS[:, s, :], ALU.add).then_inc(S["x_done"], 1)

        var = Count(S["dve_var"])
        dve.sem_inc(S["dve_acc"], 2)
        dve.sem_inc(S["dve_lo"], 1)
        dve.sem_inc(S["conv_free"], 1)
        dve.sem_inc(S["pair_free"], 2)
        dve.sem_inc(S["act_ready"], 1)
        dve.wait_ge(S["consts"], 16 * N_CONSTS)
        chain(dve.tensor_copy(IDB[:], ID[:]))
        chain(dve.tensor_copy(MSKB[:], CQ[:].rearrange("p q h -> p (q h)")))
        dve.wait_ge(S["sigmoid"], 1)
        TT(CT[:], CT[:], SG[:], ALU.mult).then_inc(S["silu"], 1)
        lam = RGP[:, :, 7]
        dve.wait_ge(S["lam_exp"], 1)
        e, z, z2, acc_ = SPT[:, 1, :], SPT[:, 2, :], SPT[:, 3, :], SPT[:, 0, :]
        chain(TSC(z, e, 2.0, None, ALU.add))
        chain(dve.reciprocal(z, z))
        chain(TT(z, z, e, ALU.mult))
        chain(TT(z2, z, z, ALU.mult))
        chain(dve.memset(acc_, 1.0 / 17))
        for n in (15, 13, 11, 9, 7, 5, 3, 1):
            chain(TT(acc_, acc_, z2, ALU.mult))
            chain(TSC(acc_, acc_, 1.0 / n, None, ALU.add))
        chain(TT(acc_, acc_, z, ALU.mult))
        chain(TSC(z, lam, -1.0, 0.0, ALU.mult, ALU.max))
        chain(TSC(acc_, acc_, 8.0, None, ALU.mult))
        chain(STT(SP4[:], z, 4.0, acc_, ALU.mult, ALU.add))
        TSC(SPT[:, 1, :], SP4[:], -2.0, None, ALU.mult).then_inc(S["sp_done"], 1)
        dve.sem_inc(free[0], 1)

        def gained(n):
            blk = MOD[:, NORMS[n][1]:NORMS[n][1] + KT, :]
            return STT(blk, blk, 1.0, NGAIN[:, n, :].unsqueeze(2).broadcast_to([P, KT, NV]), ALU.add, ALU.mult)

        chain(dve.memset(ACC[:], 0.0))
        rows_in, turned = Count(S["mods_psum"]), Count(S["mods_turned"])

        def rows(e):
            dve.wait_ge(rows_in.sem, rows_in.next())
            dve.tensor_copy(MROW[:, e, :], PS[0:NV, 3072 + 512 * e:3584 + 512 * e]).then_inc(S["mods_row"], 1)

        def turned_tiles(b, e):
            dve.wait_ge(turned.sem, turned.next())
            TT(MOD[:, bass.ds(b * MB, MB), :],
               PS[:, 2048 + 512 * e:2048 + 512 * e + MB * NV].rearrange("p (m v) -> p m v", v=NV),
               MODB[:, bass.ds(b * MB, MB)].unsqueeze(2).broadcast_to([P, MB, NV]), ALU.add)\
              .then_inc(S["mods_tile"], 1)

        def two_blocks(b):
            rows(1)
            turned_tiles(b, 0)
            rows(0)
            turned_tiles(b + 1, 1)

        first = 2 * KT // MB
        rows(0)
        with rounds(dve, first // 2, {rows_in: 2, turned: 2}) as i:
            two_blocks(i * 2)
        dve.wait_ge(S["mods_tile"], first)
        chain(gained(0))
        dve.wait_ge(S["x_in"], 16)
        with rounds(dve, 2, {rows_in: 2, turned: 2, sq: 4, accs: 4}) as i:
            two_blocks(i * 2 + first)
            for u in (0, 1, 0, 1):
                add_square(u)
        rms()
        with rounds(dve, KT // 2, {rows_in: 4, turned: 4, me: 4, hi: 2, los: 2}) as i:
            for u in range(2):
                two_blocks(i * 4 + (2 * u + 2 * MODS_BEFORE))
                normed(0, i * 2 + u, u)
                low(0, i * 2 + u, u)
        done = 2 * MODS_BEFORE + 2 * KT
        with rounds(dve, (MT // MB - 2 - done) // 2, {rows_in: 2, turned: 2}) as i:
            two_blocks(i * 2 + done)
        rows(1)
        turned_tiles(MT // MB - 2, 0)
        turned_tiles(MT // MB - 1, 1)
        dve.wait_ge(S["mods_tile"], MT // MB)
        dve.sem_inc(free[1], 1)
        for n in range(1, 5):
            gained(n)
        for layer in range(2):
            for chunk in (G1, G2):
                m = mod_at(layer, chunk)
                ins = TSC(MOD[:, m:m + KT, :], MOD[:, m:m + KT, :], 1.0, None, ALU.add)
        ins.then_inc(S["mods_done"], 1)
        dve.wait_ge(S["mods_done"], 1)

        dve.wait_ge(S["dve_lo"], KT + 1)
        chain(dve.memset(RU[:, 0:3], 0.0))
        dve.wait_ge(S["rg_halo"], 16)
        sqr, yhi = Count(S["act_sqrt"]), Count(S["y_hi"])
        for half in range(2):
            if half:
                dve.wait_ge(ready[1].sem, ready[1].now())
            with rounds(dve, RH, {ready[0]: 1, ready[1]: 1, me: 7}) as j:
                jt = j + RH * half
                ready[0].next(), ready[1].next()
                dve.wait_ge(free[0], ready[0].now() + 1)
                ru = RU[:, 3 + S0:WU].rearrange("p (b t) -> p b t", b=NB)
                xp, xs = XC[:, j, 0:S0], req(XC[:, j, S0:T])
                TSC(xp, RU[:, 0:S0], RGP[:, jt, 0:1], RGP[:, jt, 4:5], ALU.mult, ALU.add).then_inc(me.sem, 1)
                TSC(xs, ru[:, :, 0:TD], RGP[:, jt, 0:1], RGP[:, jt, 4:5], ALU.mult, ALU.add).then_inc(me.sem, 1)
                me.next(2)
                for k in (1, 2, 3):
                    dve.wait_ge(me.sem, me.now())
                    STT(xp, RU[:, k:k + S0], RGP[:, jt, k:k + 1], xp, ALU.mult, ALU.add).then_inc(me.sem, 1)
                    STT(xs, ru[:, :, k:k + TD], RGP[:, jt, k:k + 1], xs, ALU.mult, ALU.add)\
                        .then_inc(me.sem if k < 3 else S["xc_ready"], 1)
                    me.next(2 if k < 3 else 1)
                dve.tensor_copy(RST[:, jt, 0:3], RU[:, SEQ:SEQ + 3])
                dve.tensor_copy(RST[:, jt, 3:3 * NV].rearrange("p (b t) -> p b t", b=NB), ru[:, :, TD:TD + 3])\
                   .then_inc(S["conv_free"], 1)
            for j in range(RH):
                jt = RH * half + j
                ready[0].next(), ready[1].next()
                dve.wait_ge(sqr.sem, sqr.next())
                rs, ri, rq, ra = gate_buffers(half, j)
                STT(rs, ra, 1.0, rs, ALU.add, ALU.mult).then_inc(me.sem, 1)
                TT(ri, ri, XC[:, j, :], ALU.mult).then_inc(me.sem, 1)
                dve.wait_ge(me.sem, me.next(2))
                chain(TSC(ra, rs, -1.0, 1.0, ALU.mult, ALU.add))
                chain(STT(rq, ra, 1.0, rq, ALU.add, ALU.mult))
                chain(TT(ri, ri, rq, ALU.mult))
                a0, b0 = req(ra[:, S0:T])[:, :, 0], req(ri[:, S0:T])[:, :, 0]
                chain(TT(B0H0[:], a0, H0[:, jt, :], ALU.mult))
                TT(b0, b0, B0H0[:], ALU.add).then_inc(me.sem, 1)
                dve.memset(a0, 0.0).then_inc(me.sem, 1)
                dve.wait_ge(me.sem, me.next(2))
                chain(dve.tensor_tensor_scan(rq, ra, ri, 0.0, ALU.mult, ALU.add))
                dve.tensor_copy(HST[:, jt, 0:1], rq[:, SEQ - 1:SEQ])
                dve.tensor_copy(HST[:, jt, 1:NV], req(rq[:, S0:T])[:, :, TD - 1])
                TT(YG[:, jt, :], YG[:, jt, :], rq, ALU.mult).then_inc(S["pair_free"], 1)
                if half:
                    dve.wait_ge(yhi.sem, yhi.next())
                    TT(YL[:, j, :], YG[:, j, :], YH[:, j, :].bitcast(F32), ALU.subtract).then_inc(S["y_ready"], 1)
        with rounds(dve, RH, {yhi: 1}) as k:
            dve.wait_ge(yhi.sem, yhi.next())
            TT(YL[:, k + RH, :], YG[:, k + RH, :], YH[:, k + RH, :].bitcast(F32), ALU.subtract)\
                .then_inc(S["y_ready"], 1)
        dve.wait_ge(S["x_back"], 16)

        def residuals(gate, per_unit=1):
            with rounds(dve, KT // 2, {ready[0]: 1, ready[1]: 1, me: 2}) as i:
                for s in range(2):
                    residual(s, i * 2 + s, gate, per_unit)

        def last_residuals(gate, per_unit=1):
            chain(dve.memset(ACC[:], 0.0))
            residual(0, 0, gate, per_unit)
            residual(1, 1, gate, per_unit)
            add_square(0)
            with rounds(dve, KT // 2 - 1, {ready[0]: 1, ready[1]: 1, me: 2, sq: 2, accs: 2}) as i:
                residual(0, i * 2 + 2, gate, per_unit)
                add_square(1)
                residual(1, i * 2 + 3, gate, per_unit)
                add_square(0)
            add_square(1)

        dve.wait_ge(S["y_ready"], RT)
        last_residuals(mod_at(0, G1))
        xdone = Count(S["x_done"])
        dve.wait_ge(xdone.sem, xdone.next(KT))

        gel, fhi, loads = Count(S["f_gelu"]), Count(S["f_hi"]), Count(S["ffn_in"])

        def ffn(layer):
            gate = mod_at(layer, G2)
            norm(1 if layer == 0 else 4)
            dve.wait_ge(S["dve_lo"], KT * (2 if layer == 0 else 5) + 1)
            chain(dve.memset(FU[:, :, 0:2], 0.0))
            dve.wait_ge(loads.sem, loads.next(32))

            def taps(n):
                for s in range(2):
                    got(s)
                    dve.wait_ge(free[s], ready[s].now() + 1)
                    idx = n + FT * s
                    fu = FU[:, s, 2 + S0:WF].rearrange("p (b t) -> p b t", b=NB)
                    STT(FC[:, s, 0:S0], FU[:, s, 1:1 + S0], FCW[:, idx, 1:2], FC[:, s, 0:S0], ALU.mult, ALU.add)\
                        .then_inc(me.sem, 1)
                    STT(req(FC[:, s, S0:T]), fu[:, :, 1:1 + TD], FCW[:, idx, 1:2], req(FC[:, s, S0:T]),
                        ALU.mult, ALU.add).then_inc(me.sem, 1)
                    me.next(2)
                    dve.tensor_copy(FST[:, idx, 0:2], FU[:, s, SEQ:SEQ + 2])
                    dve.tensor_copy(FST[:, idx, 2:2 * NV].rearrange("p (b t) -> p b t", b=NB), fu[:, :, TD:TD + 2])
                    dve.wait_ge(me.sem, me.now())
                    STT(FC[:, s, 0:S0], FU[:, s, 0:S0], FCW[:, idx, 0:1], FC[:, s, 0:S0], ALU.mult, ALU.add)
                    STT(req(FC[:, s, S0:T]), fu[:, :, 0:TD], FCW[:, idx, 0:1], req(FC[:, s, S0:T]),
                        ALU.mult, ALU.add).then_inc(S["f_conv"] if s == 0 else me.sem, 1)
                me.next()

            def finish(c):
                dve.wait_ge(gel.sem, gel.next())
                dve.wait_ge(me.sem, me.now())
                TT(FC[:, 0, :], FC[:, 0, :], FC[:, 1, :], ALU.mult).then_inc(S["f_prod"], 1)
                dve.wait_ge(fhi.sem, fhi.next())
                TT(AL[:, c, :], FC[:, 0, :], AH[:, c, :].bitcast(F32), ALU.subtract).then_inc(S["act_ready"], 1)

            def down():
                residuals(gate, 2)

            ones = {ready[0]: 1, ready[1]: 1, me: 5, gel: 1, fhi: 1}
            with rounds(dve, GC, ones) as c:
                taps(c)
                finish(c)
            with rounds(dve, NG - 1, {ready[0]: 8, ready[1]: 8, me: GC * 5 + KT,
                                      gel: GC, fhi: GC}) as g:
                taps(g * GC + GC)
                down()
                finish(0)
                with rounds(dve, GC - 1, ones) as c:
                    taps(g * GC + c + (GC + 1))
                    finish(c + 1)
            dve.wait_ge(S["act_ready"], FT * (layer + 1) + 1)
            last_residuals(gate, 2)
            dve.wait_ge(xdone.sem, xdone.next(NG * KT))

        ffn(0)
        norm(2)
        got(0)
        dve.sem_inc(S["used_dve"], 2)
        dve.wait_ge(S["dve_lo"], 3 * KT + 1)
        TSC(three(LZ[:, 0:S0]), prompt(0, NH), KVB[:], None, ALU.add)
        TSC(LZ[:, S0:T], sample(0, NH), KVB[:], None, ALU.add).then_inc(free[0], 1)
        dve.wait_ge(free[0], ready[0].now() + 1)
        dve.wait_ge(S["lf_e"], 1)
        STT(LF[:], LZ[:], 0.0, LE[:], ALU.min, ALU.subtract).then_inc(S["lf_ready"], 1)
        dve.wait_ge(S["lf_ready"], 1)
        dve.tensor_tensor_scan(CUM[:], ONES[0:NH, 0:1].broadcast_to([NH, SEQ]), LF[:, 0:SEQ], 0.0,
                               ALU.mult, ALU.subtract).then_inc(S["lf_ready"], 1)
        dve.wait_ge(S["lf_ready"], 2)
        dve.tensor_copy(LH[:], CUM[:]).then_inc(S["lf_ready"], 1)
        dve.wait_ge(S["lf_ready"], 3)
        TT(LL[:], CUM[:], LH[:].bitcast(F32), ALU.subtract).then_inc(S["lf_ready"], 1)
        for s in range(2):
            ready[s].next(KT)
        for n in range(4):
            dve.wait_ge(S[f"kv_out{n}"], KV_ROUNDS * 16 + 16)
        dve.wait_ge(S["lf_out"], 16)
        dve.wait_ge(S["cum_out"], 32)
        norm(3, sums=False)
        for s in range(2):
            ready[s].next(KT // 2)

        dve.wait_ge(S["q_ready"], 2)
        chain(dve.memset(OT[:, :, SEQ:S0], 0.0))
        for s in range(3):
            for rows, x, c in ((slice(HD, P), K2[s], 0.0), (slice(HD, P), Q2[s], 0.0),
                               (slice(96, MAXR), K2[s], -1.0)):
                n = rows.stop - rows.start
                chain(TSC(x[rows, :], ONES[rows, 0:1].broadcast_to([n, SEQ]), c, None, ALU.mult))
        chain(dve.memset(KRAW[HD:LOGS, :], -1.0))
        chain(dve.memset(KRAW[96:100, :], 1.0))
        dve.memset(V[:, :, :, :, HD:HD + 1], 1.0).then_inc(S["const_rows"], 1)
        sr, ops, bc = Count(S["s_ready"]), Count(S["o_psum"]), Count(S["bc_psum"])
        o_free, bcu = Count(S["o_free"]), Count(S["bc_used"])

        mhi = Count(S["m_hi"])

        def maxima(e, qi):
            dve.wait_ge(sr.sem, sr.next())
            chain(dve.tensor_reduce(CQ[:, qi, 2 * e:2 * e + 1], PS[:, 0:(qi + 1) * P], AX_X, ALU.max, negate=True))
            dve.tensor_copy(CQ[:, qi, 2 * e + 1:2 * e + 2], CQ[:, qi, 2 * e:2 * e + 1]).then_inc(S["max_done"], 1)

        def max_rows(s, half):
            cols = slice(512 * half, 512 * half + 512)
            dve.wait_ge(mhi.sem, mhi.next())
            STT(Q2[s][96:MAXR, cols], OSB[96:MAXR, cols], ID[96:MAXR, 97:98],
                PS[96:MAXR, 3072 + 512 * half:3584 + 512 * half], ALU.mult, ALU.subtract).then_inc(S["m_row"], 1)

        def take_output(others=True):
            dve.wait_ge(ops.sem, ops.next())
            if others:
                dve.wait_ge(bcu.sem, bcu.now())
            dve.tensor_copy(OSB[0:HD + 1, :], PS[0:HD + 1, 3072:4096]).then_inc(o_free.sem, 1)
            dve.wait_ge(o_free.sem, o_free.next())

        def invert(q):
            row = OSB[HD:HD + 1, 256 * q:256 * q + 256]
            ins = dve.reciprocal(row, row)
            ins.then_inc(S["sums_inv"] if q % 2 else me.sem, 1)
            if q % 2 == 0:
                me.next()

        def finish(pair, e, half):
            dve.wait_ge(bc.sem, bc.next())
            cols = slice(512 * half, 512 * half + 512)
            TT(OT[HD * e:HD * e + HD, pair, cols], OSB[0:HD, cols], PS[0:HD, 512:1024], ALU.mult).then_inc(bcu.sem, 1)
            bcu.next()

        def heads(count, base, pair, first=False, last=False):
            for n in range(count):
                h = base + n
                ahead, behind = not (last and n == count - 1), not (first and n == 0)
                if behind:
                    take_output(others=not (first and n == 1))
                for j in range(KT):
                    if ahead:
                        maxima((h + 1) % 2, KT - 1 - j)
                    if j < 4 and behind:
                        invert(j)
                    if j in (5, 7) and behind:
                        finish(pair + (n - 1) // 2, (n + 1) % 2, (j - 5) // 2)
                    if j == 4 and ahead:
                        max_rows((h + 1) % 3, 1)
                if ahead:
                    max_rows((h + 1) % 3, 0)

        for qi in range(KT - 1, -1, -1):
            maxima(0, qi)
        max_rows(0, 1)
        max_rows(0, 0)
        heads(2, 0, 0, first=True)
        dve.wait_ge(S["lfp_in"], NB * NPG * 16)
        dve.wait_ge(S["lfn_in"], NB * 16)
        chain(dve.tensor_tensor_scan(CUMS[:, 0:PAST], ONES[:, 0:1].broadcast_to([P, PAST]), LFP, 0.0, ALU.mult, ALU.add))
        chain(dve.tensor_tensor_scan(CN[:], ONES[:, 0:TD], LFN[:], CUMS[:, PAST - 1:PAST], ALU.mult, ALU.add))
        chain(dve.tensor_copy(req(CUMS[:, PAST:KEYS]), CN[:].unsqueeze(1).broadcast_to([P, NB, TD])))
        TT(CNM[:], CN[:].unsqueeze(1).broadcast_to([P, NB, TD]), bc_t(BM[:]), ALU.mult).then_inc(S["cumm_ready"], 1)
        with rounds(dve, 2, {sr: 48, ops: 6, bc: 12, o_free: 6, bcu: 12, me: 12 + 48, mhi: 12}) as i:
            heads(6, 2, i * 3 + 1)
        heads(2, 2, KT - 1, last=True)
        take_output()
        for q in range(4):
            invert(q)
        for half in range(2):
            finish(KT - 1, 1, half)

        chain(dve.memset(QX[:], 0.0))
        dve.wait_ge(S["cq_psum"], 1)
        chain(TT(CQT[:], req(PS[:, 0:TS]), MQ[:].unsqueeze(1).broadcast_to([P, NB, TD]), ALU.mult))
        dve.tensor_reduce(CQS[:], CQT[:], AX_X, ALU.add).then_inc(S["cq_done"], 1)
        dve.wait_ge(S["cq_done"], 1)
        dve.wait_ge(S["sconst"], 16)
        scps, scex, scd = Count(S["sc_psum"]), Count(S["sc_exp"]), Count(S["sc_diag"])

        def queries(k, e):
            for hv in range(2):
                rows = slice(HD * hv, HD * hv + HD)
                dve.tensor_copy(QX[rows, e, :].rearrange("p (k x) -> p k x", x=P + 16)[:, :, 8 * hv:8 * hv + 8],
                                Q[rows, :, bass.ds(k * TD + S0, TD)])
            TSC(CUMX[e], CUMS[:], BM[:, bass.ds(k, 1)], None, ALU.mult).then_inc(S["qx_ready"], 1)

        def output(k):
            dve.wait_ge(scd.sem, scd.next())
            for hv in range(2):
                rows = slice(HD * hv, HD * hv + HD)
                ins = dve.tensor_copy(OT[rows, :, bass.ds(k * TD + S0, TD)],
                                      PS[rows, 2560:2560 + P]
                                      .rearrange("p (k x) -> p k x", x=16)[:, :, 8 * hv:8 * hv + 8])
            ins.then_inc(S["sc_done"], 1)

        def softmax(k, e, ahead=True, before=True):
            nm, ri = NM[:, e:e + 1], RI[:, e:e + 1]
            dve.wait_ge(scps.sem, scps.next())
            chain(TSC(SS[e].rearrange("p (h c) -> p h c", h=2),
                      PS[:, 1024 * e:1024 * e + 1024].rearrange("p (h c) -> p h c", h=2)[:, :, 0:KEYS // 2],
                      CQS[:, bass.ds(k, 1)], None, ALU.add))
            chain(TT(SS[e][:, PAST:PAST + TS], SS[e][:, PAST:PAST + TS], MKS[:, k, :], ALU.add))
            dve.tensor_reduce(nm, SS[e], AX_X, ALU.max, negate=True).then_inc(S["sc_nm"], 1)
            if ahead:
                queries(k + 2, e)
            dve.wait_ge(scex.sem, scex.next())
            chain(dve.reciprocal(ri, SUM[:, e:e + 1]))
            TSC(SS[e], SS[e], ri, None, ALU.mult).then_inc(S["sc_p"], 1)
            if before:
                output(k - 2)

        queries(0, 0)
        queries(1, 1)
        softmax(0, 0, before=False)
        softmax(1, 1, before=False)
        with rounds(dve, NB // 2 - 2, {scps: 2, scex: 2, scd: 2, me: 6}) as i:
            for e in range(2):
                softmax(i * 2 + (e + 2), e)
        softmax(NB - 2, 0, ahead=False)
        softmax(NB - 1, 1, ahead=False)
        output(NB - 2)
        output(NB - 1)
        ohi = Count(S["o_hi"])
        with rounds(dve, KT, {ohi: 1}) as k:
            dve.wait_ge(ohi.sem, ohi.next())
            TT(OL[:, k, :], OT[:, k, :], OH[:, k, :].bitcast(F32), ALU.subtract).then_inc(S["o_ready"], 1)
        last_residuals(mod_at(1, G1))
        dve.wait_ge(xdone.sem, xdone.next(KT))
        ffn(1)
        norm(5)


N_CONSTS = 11
_OUTS = {"yT": (KT, P, T), "kv": (2 * KT, P, T), "lf": (NH, T), "ncum": (NH, 2, SEQ), "rst": (P, RT, 3 * NV), "hst": (P, RT, NV),
         "fst": (2, P, 2 * FT, 2 * NV)}


def _layouts(d):
    import numpy as np
    f = np.float32
    a = {k: np.asarray(v) for k, v in d.items()}

    def cols(w, c0, c1, r0=0, r1=None):
        w = w[r0:r1, c0:c1]
        return w.reshape(-1, P, c1 - c0).transpose(1, 0, 2)

    def unit(*parts):
        u = np.concatenate([p.reshape(P, -1) for p in parts], 1)
        out = np.zeros((P, UNIT), f)
        out[:, :u.shape[1]] = u
        return out

    units = []
    w_in, w_out = a["rg_w_in"][0], a["rg_w_out"][0]
    for j in range(RT):
        units += [unit(cols(w_in, D_RNN + P * j, D_RNN + P * j + P)), unit(cols(w_in, P * j, P * j + P))]
    for o in range(KT):
        units += [unit(cols(w_out, P * o, P * o + P, 5 * P * h, 5 * P * h + 5 * P)) for h in range(2)]

    def ffn(l):
        up, dn = a["ffn_w_up"][l], a["ffn_w_down"][l]

        def pair(n):
            return [unit(cols(up, P * n, P * n + P)), unit(cols(up, D_FF + P * n, D_FF + P * n + P))]

        def down(g):
            r0 = g * GC * P
            return [unit(*(cols(dn, P * o, P * o + P, r0, r0 + GC * P) for o in (2 * v, 2 * v + 1))) for v in range(4)]
        out = []
        for g in range(NG):
            out += pair(GC * g)
            if g:
                out += down(g - 1)
            for c in range(1, GC):
                out += pair(GC * g + c)
        return out + down(NG - 1)

    units += ffn(0)
    kvw = a["kv_w"]
    units += [unit(np.pad(cols(kvw, 2 * D, 2 * D + NH), ((0, 0), (0, 0), (0, P - NH)))), np.zeros((P, UNIT), f)]
    units += [unit(cols(kvw, P * j, P * j + P)) for j in range(2 * KT)]
    units += [unit(cols(a["fa_wq"][0], P * j, P * j + P)) for j in range(KT)]
    units += [unit(cols(a["fa_wo"][0], P * j, P * j + P)) for j in range(KT)]
    units += ffn(1)
    assert len(units) == UNITS_1 + UNITS_2

    mw = np.concatenate([a["mod_w"][0], a["mod_w"][1], a["kv_mod_w"]], 1)
    mb = np.concatenate([a["mod_b"][0], a["mod_b"][1], a["kv_mod_b"]])
    chan = lambda v: v.reshape(-1, P).T
    x = np.concatenate([a["x_prompt"][0], np.zeros((PAD, D), f), a["x_sample"].reshape(TS, D)])
    c = np.concatenate([a["c_prompt"], a["c_sample"]])
    gates = np.zeros((RT, P, 2, 3, P), f)
    for u, w in enumerate((a["rg_wa"][0], a["rg_wx"][0])):
        full = np.zeros((D_RNN, D_RNN), f)
        for h in range(16):
            full[RG_W * h:RG_W * h + RG_W, RG_W * h:RG_W * h + RG_W] = w[h]
        for j in range(RT):
            for n, k in enumerate(GATE_IN[j]):
                gates[j, :, u, n] = full[P * k:P * k + P, P * j:P * j + P]
    par = np.stack([chan(v) for v in (*a["rg_conv_w"][0], a["rg_conv_b"][0], a["rg_ba"][0], a["rg_bx"][0],
                                      a["rg_lambda"][0])], 2)
    hs = np.arange(P)
    q = np.arange(P)
    pick = -((hs[:, None] % NH) == (hs[None, :] // TD)).astype(f)
    mask_new = np.full((P, NB, NB, TD), NEG, f)
    for b in range(NB):
        mask_new[:, b, b, :] = np.where(np.arange(TD)[None, :] <= (hs % TD)[:, None], 0.0, NEG)
    return {
        "wstream": np.stack(units),
        "mod_w": mw.reshape(2, KT // 2, P, MT // MB, MB * P).transpose(3, 0, 2, 1, 4)
                   .reshape(2 * MT // MB, P, KT // 2, MB * P),
        "mod_b": chan(mb),
        "cT": c.reshape(NV, KT, P).transpose(2, 1, 0),
        "gains": np.stack([chan(v) for v in (a["norm_mix_g"][0], a["norm_ffn_g"][0], a["kv_norm_g"],
                                             a["norm_mix_g"][1], a["norm_ffn_g"][1], a["final_norm_g"])], 1),
        "xT": x.T.reshape(KT, P, T),
        "rg_par": par,
        "rg_h0": a["state_rglru_h"][0].reshape(NB, RT, P).transpose(2, 1, 0),
        "rg_halo": a["state_rglru_conv"][0].reshape(NB, 3, RT, P).transpose(3, 2, 0, 1).reshape(P, RT, NB * 3),
        "rg_gate_w": gates,
        "ffn_halo": a["state_ffn_conv"].reshape(2, NB, 2, 2 * FT, P).transpose(0, 4, 3, 1, 2).reshape(2, P, 2 * FT, NB * 2),
        "ffn_par": np.concatenate([a["ffn_conv_w"].reshape(2, 3, 2 * FT, P).transpose(0, 3, 2, 1),
                                   a["ffn_conv_b"].reshape(2, 1, 2 * FT, P).transpose(0, 3, 2, 1)], 3),
        "kv_b": a["kv_b_f"].reshape(NH, 1),
        "cache_k": a["cache_k"].reshape(-1, PAGE, KT, P).transpose(0, 3, 2, 1),
        "cache_v": a["cache_v"].reshape(-1, PAGE, D),
        "cache_lf": a["cache_logf"].transpose(0, 2, 1),
        "page_table": a["page_table"].reshape(1, NB * NPG),
        "ident": np.eye(P, dtype=f),
        "mask": np.where(q[None, :] <= q[:, None], 0.0, NEG).astype(f).reshape(P, KT, NH),
        "pick_head": pick,
        "req_rows": ((hs[:, None] // NH) == np.arange(NB)[None, :]).astype(f),
        "pick_q": -((hs[:, None] % TD) == np.arange(TD)[None, :]).astype(f),
        "mask_new": mask_new.reshape(P, NB, TS),
    }


def kernel(**inputs):
    import numpy as np
    import concourse.bacc as bacc
    from concourse.bass_utils import run_bass_kernel_spmd

    nc = bacc.Bacc("TRN2", target_bir_lowering=False, num_devices=1)
    arrays, ins, outs = {}, {}, {}
    for name, v in _layouts(inputs).items():
        arrays[f"in_{name}"] = np.ascontiguousarray(v)
        ins[name] = nc.dram_tensor(f"in_{name}", v.shape, mybir.dt.from_np(v.dtype), kind="ExternalInput").ap()
    for name, shape in _OUTS.items():
        outs[name] = nc.dram_tensor(f"out_{name}", shape, F32, kind="ExternalOutput").ap()
    trunk(nc, ins, outs)
    res = run_bass_kernel_spmd(nc, [arrays], core_ids=[0]).results[0]
    g = {n: res[f"out_{n}"] for n in _OUTS}

    y = g["yT"].reshape(D, T).T
    kv = g["kv"].reshape(2, D, T).transpose(0, 2, 1).reshape(2, T, NH, HD)
    lf = g["lf"].T
    rst = g["rst"].transpose(2, 1, 0).reshape(NV, 3, D_RNN)
    hst = g["hst"].transpose(2, 1, 0).reshape(NV, D_RNN)
    fst = g["fst"].transpose(0, 3, 2, 1).reshape(2, NV, 2, 2 * D_FF)
    return (y[None, :SEQ], y[S0:].reshape(NB, TD, D),
            kv[0][None, :SEQ], kv[1][None, :SEQ], lf[None, :SEQ],
            rst[None, :1], hst[None, :1], fst[:, :1],
            kv[0][S0:].reshape(NB, TD, NH, HD), kv[1][S0:].reshape(NB, TD, NH, HD), lf[S0:].reshape(NB, TD, NH),
            rst[None, 1:], hst[None, 1:], fst[:, 1:])
```
